# Optimizing a Trainium2 kernel written in Bass

```python
import jax, jax.numpy as jnp
from jax import lax
import numpy as np
import math

D_MODEL = 1024
BATCH = 1
SEQ = 256
DEPTH = 2

D_FF = 2816
EPS = 1e-6
NSA_HEADS = 8
NSA_KV_GROUPS = 2
HEAD_DIM = 64
NSA_WIDTH = NSA_HEADS * HEAD_DIM
KV_WIDTH = NSA_KV_GROUPS * HEAD_DIM
CMP_BLOCK = 32
CMP_STRIDE = 16
CMP_HIDDEN = 128
SLC_BLOCK = 64
RATIO = SLC_BLOCK // CMP_STRIDE
SLC_TOP_N = 16
WINDOW = 512
Q_BLOCK = 128
FORCE_BONUS = 1e4
CONV_WIDTH = 512
CONV_K = 3
IN_SIZES = (NSA_WIDTH, 3 * NSA_HEADS, KV_WIDTH, KV_WIDTH, KV_WIDTH, KV_WIDTH,
            KV_WIDTH, KV_WIDTH, CONV_WIDTH, CONV_WIDTH, CONV_WIDTH)
IN_COLS = sum(IN_SIZES)
IN_SPLITS = tuple(int(s) for s in np.cumsum(IN_SIZES)[:-1])
MIX_OUT = NSA_WIDTH + CONV_WIDTH
RWKV_HEAD = 64
RWKV_HEADS = D_MODEL // RWKV_HEAD
DECAY_LORA = 64
AAA_LORA = 64
GATE_LORA = 128
LNX_EPS = 64e-5


def rmsnorm(x, g):
    xf = x.astype(jnp.float32)
    y = xf * lax.rsqrt(jnp.mean(xf * xf, -1, keepdims=True) + EPS)
    return (y * g.astype(jnp.float32)).astype(x.dtype)

def macaron_half_ffn(x, pre_g, post_g, w_gate, w_up, w_down):
    h = rmsnorm(x, pre_g)
    h = (jax.nn.silu(h @ w_gate) * (h @ w_up)) @ w_down
    return x + 0.5 * rmsnorm(h, post_g)

def alibi_slopes(n):
    return 2.0 ** (-8.0 * jnp.arange(1, n + 1, dtype=jnp.float32) / n)

def masked_softmax(s, mask):
    s = jnp.where(mask, s.astype(jnp.float32), -jnp.inf)
    m = jnp.max(s, -1, keepdims=True)
    m = jnp.where(jnp.isfinite(m), m, 0.0)
    p = jnp.exp(s - m)
    return p / jnp.maximum(jnp.sum(p, -1, keepdims=True), 1e-30)

def compress_blocks(kv, pe, w1, w2):
    B, S, G, Dh = kv.shape
    halves = kv.reshape(B, S // CMP_STRIDE, CMP_STRIDE, G, Dh)
    blocks = jnp.concatenate([halves[:, :-1], halves[:, 1:]], axis=2)
    blocks = blocks + pe[None, None, :, None, :]
    nc = blocks.shape[1]
    flat = blocks.transpose(0, 1, 3, 2, 4).reshape(B, nc, G, CMP_BLOCK * Dh)
    return jax.nn.gelu(flat @ w1) @ w2

def nsa_attention(q, gates, kc, vc, k_slc, v_slc, k_win, v_win):
    B, S, H, Dh = q.shape
    G = kc.shape[2]
    R = H // G
    n_cmp = kc.shape[1]
    n_slc = S // SLC_BLOCK
    top_n = min(SLC_TOP_N, n_slc)
    slopes = alibi_slopes(H).reshape(G, R)
    cmp_end = jnp.arange(n_cmp) * CMP_STRIDE + (CMP_BLOCK - 1)
    qg = q.reshape(B, S, G, R, Dh) * (Dh ** -0.5)
    gg = gates.reshape(B, S, G, R, 3)
    kb = k_slc.reshape(B, n_slc, SLC_BLOCK, G, Dh).transpose(0, 3, 1, 2, 4)
    vb = v_slc.reshape(B, n_slc, SLC_BLOCK, G, Dh).transpose(0, 3, 1, 2, 4)
    gather = jax.vmap(jax.vmap(lambda blocks, ix: blocks[ix]))
    kw = jnp.pad(k_win, ((0, 0), (WINDOW, 0), (0, 0), (0, 0)))
    vw = jnp.pad(v_win, ((0, 0), (WINDOW, 0), (0, 0), (0, 0)))
    j = jnp.arange(n_slc)
    offs = jnp.arange(SLC_BLOCK)
    woffs = jnp.arange(Q_BLOCK + WINDOW) - WINDOW

    def query_block(qi):
        q0 = qi * Q_BLOCK
        t = q0 + jnp.arange(Q_BLOCK)
        qb = lax.dynamic_slice_in_dim(qg, q0, Q_BLOCK, axis=1)
        gb = lax.dynamic_slice_in_dim(gg, q0, Q_BLOCK, axis=1)
        d_cmp = t[:, None] - cmp_end[None, :]
        s = jnp.einsum("btgrd,bngd->bgrtn", qb, kc) - slopes[:, :, None, None] * d_cmp
        p_cmp = masked_softmax(s, d_cmp >= 0)
        o_cmp = jnp.einsum("bgrtn,bngd->btgrd", p_cmp.astype(vc.dtype), vc)
        imp = jnp.pad(p_cmp.sum(2), ((0, 0), (0, 0), (0, 0), (0, 1)))
        imp = imp.reshape(B, G, Q_BLOCK, n_slc, RATIO)
        last = imp[..., RATIO - 1]
        prev = jnp.pad(last, ((0, 0), (0, 0), (0, 0), (1, 0)))[..., :-1]
        imp = imp.sum(-1) - 0.5 * last + 0.5 * prev
        blk_t = (t // SLC_BLOCK)[:, None]
        forced = (j == 0) | (j == blk_t) | (j == blk_t - 1)
        imp = jnp.where(forced, imp + FORCE_BONUS, imp)
        imp = jnp.where(j <= blk_t, imp, -jnp.inf)
        _, idx = lax.top_k(imp, top_n)
        ks = gather(kb, idx)
        vs = gather(vb, idx)
        d_slc = t[:, None, None] - (idx[..., None] * SLC_BLOCK + offs)
        s = jnp.einsum("btgrd,bgtnld->bgrtnl", qb, ks) - slopes[:, :, None, None, None] * d_slc[:, :, None]
        mask = jnp.broadcast_to((d_slc >= 0)[:, :, None], s.shape)
        p = masked_softmax(s.reshape(B, G, R, Q_BLOCK, -1), mask.reshape(B, G, R, Q_BLOCK, -1))
        o_slc = jnp.einsum("bgrtm,bgtmd->btgrd", p.astype(vs.dtype),
                           vs.reshape(B, G, Q_BLOCK, top_n * SLC_BLOCK, Dh))
        kwb = lax.dynamic_slice_in_dim(kw, q0, Q_BLOCK + WINDOW, axis=1)
        vwb = lax.dynamic_slice_in_dim(vw, q0, Q_BLOCK + WINDOW, axis=1)
        kpos = q0 + woffs
        d_win = t[:, None] - kpos[None, :]
        mask = (d_win >= 0) & (d_win < WINDOW) & (kpos[None, :] >= 0)
        s = jnp.einsum("btgrd,bsgd->bgrts", qb, kwb) - slopes[:, :, None, None] * d_win
        p = masked_softmax(s, mask)
        o_win = jnp.einsum("bgrts,bsgd->btgrd", p.astype(vwb.dtype), vwb)
        return gb[..., 0:1] * o_cmp + gb[..., 1:2] * o_slc + gb[..., 2:3] * o_win

    out = lax.map(query_block, jnp.arange(S // Q_BLOCK))
    return out.transpose(1, 0, 2, 3, 4, 5).reshape(B, S, H * Dh)

def short_conv(b_gate, c_gate, u, conv_w, conv_b):
    z = c_gate * u
    y = lax.conv_general_dilated(z, conv_w[:, None, :].astype(z.dtype), window_strides=(1,),
                                 padding=[(CONV_K - 1, 0)],
                                 dimension_numbers=("NWC", "WIO", "NWC"),
                                 feature_group_count=z.shape[-1])
    return b_gate * (y + conv_b)

def nsa_shortconv_mixer(h, w_in, cmp_pe_k, cmp_w1_k, cmp_w2_k, cmp_pe_v, cmp_w1_v, cmp_w2_v,
                        conv_w, conv_b, w_out):
    B, S, _ = h.shape
    q, g, kc, vc, ks, vs, kw, vw, cb, cc, cu = jnp.split(h @ w_in, IN_SPLITS, axis=-1)
    kv = lambda t: t.reshape(B, S, NSA_KV_GROUPS, HEAD_DIM)
    kc = compress_blocks(kv(kc), cmp_pe_k, cmp_w1_k, cmp_w2_k)
    vc = compress_blocks(kv(vc), cmp_pe_v, cmp_w1_v, cmp_w2_v)
    o_nsa = nsa_attention(q.reshape(B, S, NSA_HEADS, HEAD_DIM),
                          jax.nn.sigmoid(g).reshape(B, S, NSA_HEADS, 3),
                          kc, vc, kv(ks), kv(vs), kv(kw), kv(vw))
    o_conv = short_conv(cb, cc, cu, conv_w, conv_b)
    return jnp.concatenate([o_nsa.astype(h.dtype), o_conv], axis=-1) @ w_out

def rwkv7_mixer(h, mu, w_r, w_k, w_v, w_o, w0, w_dec1, w_dec2, a0, w_a1, w_a2,
                w_g1, w_g2, k_k, k_a, r_k, lnx_g, lnx_b):
    B, S, D = h.shape
    H, N = RWKV_HEADS, RWKV_HEAD
    xx = jnp.pad(h, ((0, 0), (1, 0), (0, 0)))[:, :-1] - h
    xr, xw, xk, xv, xa, xg = [h + xx * mu[i] for i in range(6)]
    r = xr @ w_r
    k = xk @ w_k
    v = xv @ w_v
    w_log = -jax.nn.softplus(-(w0 + jnp.tanh(xw @ w_dec1) @ w_dec2)) - 0.5
    a = jax.nn.sigmoid(a0 + (xa @ w_a1) @ w_a2)
    g = jax.nn.sigmoid(xg @ w_g1) @ w_g2
    kk = (k * k_k).reshape(B, S, H, N).astype(jnp.float32)
    kk = kk * lax.rsqrt(jnp.maximum(jnp.sum(kk * kk, -1, keepdims=True), 1e-12))
    k = k * (1.0 + (a - 1.0) * k_a)
    decay = jnp.exp(-jnp.exp(w_log.astype(jnp.float32)))
    heads = lambda t: t.reshape(B, S, H, N).astype(jnp.float32).transpose(1, 0, 2, 3)
    xs = (heads(r), heads(decay), heads(k), heads(v), kk.transpose(1, 0, 2, 3), heads(a))

    def step(state, inp):
        r_t, w_t, k_t, v_t, kk_t, a_t = inp
        sa = jnp.einsum("bhij,bhj->bhi", state, -kk_t)
        state = (state * w_t[:, :, None, :] + sa[..., None] * (kk_t * a_t)[:, :, None, :]
                 + v_t[..., None] * k_t[:, :, None, :])
        return state, jnp.einsum("bhij,bhj->bhi", state, r_t)

    state0 = jnp.zeros((B, H, N, N), jnp.float32)
    _, y = lax.scan(step, state0, xs)
    y = y.transpose(1, 0, 2, 3)
    mean = jnp.mean(y, -1, keepdims=True)
    var = jnp.mean(jnp.square(y - mean), -1, keepdims=True)
    y = ((y - mean) * lax.rsqrt(var + LNX_EPS)).reshape(B, S, D) * lnx_g + lnx_b
    rh, kh, vh = (t.reshape(B, S, H, N).astype(jnp.float32) for t in (r, k, v))
    bonus = (jnp.sum(rh * kh * r_k, -1, keepdims=True) * vh).reshape(B, S, D)
    return ((y + bonus).astype(h.dtype) * g) @ w_o

def first_inputs(seed: int = 0) -> dict:
    key = jax.random.key(seed)
    keys = iter(jax.random.split(key, 80))

    def nrm(shape, scale):
        return jax.random.normal(next(keys), shape, jnp.float32) * scale

    def unif(shape, lo, hi):
        return jax.random.uniform(next(keys), shape, jnp.float32, lo, hi)

    def gain(n=D_MODEL):
        return 1.0 + nrm((n,), 0.05)

    inp = {"x": nrm((BATCH, SEQ, D_MODEL), 1.0)}

    def add_ffn(p):
        inp[p + "_pre_g"] = gain()
        inp[p + "_post_g"] = gain()
        inp[p + "_w_gate"] = nrm((D_MODEL, D_FF), D_MODEL ** -0.5)
        inp[p + "_w_up"] = nrm((D_MODEL, D_FF), D_MODEL ** -0.5)
        inp[p + "_w_down"] = nrm((D_FF, D_MODEL), D_FF ** -0.5)

    add_ffn("l0_ffn1")
    inp["l0_mix_pre_g"] = gain()
    inp["l0_mix_post_g"] = gain()
    inp["l0_w_in"] = nrm((D_MODEL, IN_COLS), D_MODEL ** -0.5)
    for kvn in ("k", "v"):
        inp["l0_cmp_pe_" + kvn] = nrm((CMP_BLOCK, HEAD_DIM), 0.1)
        inp["l0_cmp_w1_" + kvn] = nrm((CMP_BLOCK * HEAD_DIM, CMP_HIDDEN), (CMP_BLOCK * HEAD_DIM) ** -0.5)
        inp["l0_cmp_w2_" + kvn] = nrm((CMP_HIDDEN, HEAD_DIM), CMP_HIDDEN ** -0.5)
    inp["l0_conv_w"] = nrm((CONV_K, CONV_WIDTH), 0.5)
    inp["l0_conv_b"] = nrm((CONV_WIDTH,), 0.02)
    inp["l0_w_out"] = nrm((MIX_OUT, D_MODEL), MIX_OUT ** -0.5)
    add_ffn("l0_ffn2")
    add_ffn("l1_ffn1")
    inp["l1_mix_pre_g"] = gain()
    inp["l1_mix_post_g"] = gain()
    inp["l1_mu"] = unif((6, D_MODEL), 0.0, 1.0)
    inp["l1_w_r"] = nrm((D_MODEL, D_MODEL), D_MODEL ** -0.5)
    inp["l1_w_k"] = nrm((D_MODEL, D_MODEL), D_MODEL ** -0.5)
    inp["l1_w_v"] = nrm((D_MODEL, D_MODEL), D_MODEL ** -0.5)
    inp["l1_w_o"] = nrm((D_MODEL, D_MODEL), D_MODEL ** -0.5)
    inp["l1_w0"] = unif((D_MODEL,), -6.0, 1.0)
    inp["l1_w_dec1"] = nrm((D_MODEL, DECAY_LORA), D_MODEL ** -0.5)
    inp["l1_w_dec2"] = nrm((DECAY_LORA, D_MODEL), 0.1 * DECAY_LORA ** -0.5)
    inp["l1_a0"] = nrm((D_MODEL,), 0.5)
    inp["l1_w_a1"] = nrm((D_MODEL, AAA_LORA), D_MODEL ** -0.5)
    inp["l1_w_a2"] = nrm((AAA_LORA, D_MODEL), 0.5 * AAA_LORA ** -0.5)
    inp["l1_w_g1"] = nrm((D_MODEL, GATE_LORA), D_MODEL ** -0.5)
    inp["l1_w_g2"] = nrm((GATE_LORA, D_MODEL), GATE_LORA ** -0.5)
    inp["l1_k_k"] = 0.85 + nrm((D_MODEL,), 0.05)
    inp["l1_k_a"] = 1.0 + nrm((D_MODEL,), 0.05)
    inp["l1_r_k"] = nrm((RWKV_HEADS, RWKV_HEAD), 0.1)
    inp["l1_lnx_g"] = gain()
    inp["l1_lnx_b"] = nrm((D_MODEL,), 0.02)
    add_ffn("l1_ffn2")
    return inp

def first_block(x,
              l0_ffn1_pre_g, l0_ffn1_post_g, l0_ffn1_w_gate, l0_ffn1_w_up, l0_ffn1_w_down,
              l0_mix_pre_g, l0_mix_post_g, l0_w_in,
              l0_cmp_pe_k, l0_cmp_w1_k, l0_cmp_w2_k, l0_cmp_pe_v, l0_cmp_w1_v, l0_cmp_w2_v,
              l0_conv_w, l0_conv_b, l0_w_out,
              l0_ffn2_pre_g, l0_ffn2_post_g, l0_ffn2_w_gate, l0_ffn2_w_up, l0_ffn2_w_down,
              l1_ffn1_pre_g, l1_ffn1_post_g, l1_ffn1_w_gate, l1_ffn1_w_up, l1_ffn1_w_down,
              l1_mix_pre_g, l1_mix_post_g, l1_mu, l1_w_r, l1_w_k, l1_w_v, l1_w_o,
              l1_w0, l1_w_dec1, l1_w_dec2, l1_a0, l1_w_a1, l1_w_a2, l1_w_g1, l1_w_g2,
              l1_k_k, l1_k_a, l1_r_k, l1_lnx_g, l1_lnx_b,
              l1_ffn2_pre_g, l1_ffn2_post_g, l1_ffn2_w_gate, l1_ffn2_w_up, l1_ffn2_w_down):
    layers = [
        dict(ffn1=(l0_ffn1_pre_g, l0_ffn1_post_g, l0_ffn1_w_gate, l0_ffn1_w_up, l0_ffn1_w_down),
             norms=(l0_mix_pre_g, l0_mix_post_g),
             mixer=nsa_shortconv_mixer,
             mix=(l0_w_in, l0_cmp_pe_k, l0_cmp_w1_k, l0_cmp_w2_k, l0_cmp_pe_v, l0_cmp_w1_v,
                  l0_cmp_w2_v, l0_conv_w, l0_conv_b, l0_w_out),
             ffn2=(l0_ffn2_pre_g, l0_ffn2_post_g, l0_ffn2_w_gate, l0_ffn2_w_up, l0_ffn2_w_down)),
        dict(ffn1=(l1_ffn1_pre_g, l1_ffn1_post_g, l1_ffn1_w_gate, l1_ffn1_w_up, l1_ffn1_w_down),
             norms=(l1_mix_pre_g, l1_mix_post_g),
             mixer=rwkv7_mixer,
             mix=(l1_mu, l1_w_r, l1_w_k, l1_w_v, l1_w_o, l1_w0, l1_w_dec1, l1_w_dec2, l1_a0,
                  l1_w_a1, l1_w_a2, l1_w_g1, l1_w_g2, l1_k_k, l1_k_a, l1_r_k, l1_lnx_g, l1_lnx_b),
             ffn2=(l1_ffn2_pre_g, l1_ffn2_post_g, l1_ffn2_w_gate, l1_ffn2_w_up, l1_ffn2_w_down)),
    ]
    for i in range(DEPTH):
        p = layers[i]
        x = macaron_half_ffn(x, *p["ffn1"])
        pre_g, post_g = p["norms"]
        x = x + rmsnorm(p["mixer"](rmsnorm(x, pre_g), *p["mix"]), post_g)
        x = macaron_half_ffn(x, *p["ffn2"])
    return x


CHUNK = 64
N_MIXERS = 2
FOX_HEADS = 16
FOX_HEAD_DIM = D_MODEL // FOX_HEADS
HGRN_EXPAND = 128
HGRN_HEADS = D_MODEL // HGRN_EXPAND
HGRN_HEAD_DIM = HGRN_EXPAND
D_FF_2 = -(-8 * D_MODEL // (3 * 256)) * 256
N_FOX = (DEPTH + 1) // 2
N_HGRN = DEPTH // 2


def rmsnorm_2(x, g):
    x32 = x.astype(jnp.float32)
    y = x32 * lax.rsqrt(jnp.mean(x32 * x32, axis=-1, keepdims=True) + EPS)
    return (y * g.astype(jnp.float32)).astype(x.dtype)

def fox_attention(h, w_in, b_f, w_out):
    bsz, seq, _ = h.shape
    proj = jnp.einsum('bsd,de->bse', h, w_in)
    q, k, v, f_logit = jnp.split(proj, [D_MODEL, 2 * D_MODEL, 3 * D_MODEL], axis=-1)

    def heads(t):
        return t.reshape(bsz, seq, FOX_HEADS, FOX_HEAD_DIM).transpose(0, 2, 1, 3)

    q = heads(q) * (FOX_HEAD_DIM ** -0.5)
    k = heads(k)
    v = heads(v)
    log_f = jax.nn.log_sigmoid(f_logit.astype(jnp.float32) + b_f.astype(jnp.float32))
    c = jnp.cumsum(log_f, axis=1).transpose(0, 2, 1)
    key_pos = jnp.arange(seq)

    def q_block(blk):
        start = blk * Q_BLOCK
        qb = lax.dynamic_slice_in_dim(q, start, Q_BLOCK, axis=2)
        cb = lax.dynamic_slice_in_dim(c, start, Q_BLOCK, axis=2)
        q_pos = start + jnp.arange(Q_BLOCK)
        logits = jnp.einsum('bhqd,bhkd->bhqk', qb, k).astype(jnp.float32)
        logits = logits + cb[:, :, :, None] - c[:, :, None, :]
        logits = jnp.where(q_pos[:, None] >= key_pos[None, :], logits, -jnp.inf)
        p = jax.nn.softmax(logits, axis=-1).astype(v.dtype)
        return jnp.einsum('bhqk,bhkd->bhqd', p, v)

    out = lax.map(q_block, jnp.arange(seq // Q_BLOCK))
    out = out.transpose(1, 0, 3, 2, 4).reshape(bsz, seq, D_MODEL)
    return jnp.einsum('bsd,de->bse', out, w_out)

def hgrn2_recurrence(h, w_in, lb, g_norm_w, w_out):
    bsz, seq, _ = h.shape
    n_chunks = seq // CHUNK
    proj = jnp.einsum('bsd,de->bse', h, w_in)
    q, f_logit, i_val, g = jnp.split(proj, [D_MODEL, 2 * D_MODEL, 3 * D_MODEL], axis=-1)
    f = lb + (1.0 - lb) * jax.nn.sigmoid(f_logit.astype(jnp.float32))
    log_f = jnp.log(f)
    k = 1.0 - f

    def to_chunks(t):
        t = t.astype(jnp.float32).reshape(bsz, n_chunks, CHUNK, HGRN_HEADS, HGRN_HEAD_DIM)
        return t.transpose(1, 0, 3, 2, 4)

    qc = to_chunks(q)
    kc = to_chunks(k)
    vc = to_chunks(i_val)
    bc = jnp.cumsum(to_chunks(log_f), axis=3)
    causal = jnp.arange(CHUNK)[:, None] >= jnp.arange(CHUNK)[None, :]

    def step(state, xs):
        q_t, k_t, v_t, b_t = xs
        o_inter = jnp.einsum('bhtk,bhkv->bhtv', q_t * jnp.exp(b_t), state)
        diff = b_t[:, :, :, None, :] - b_t[:, :, None, :, :]
        decay = jnp.exp(jnp.where(causal[:, :, None], diff, -jnp.inf))
        scores = jnp.einsum('bhtk,bhsk,bhtsk->bhts', q_t, k_t, decay)
        o = o_inter + jnp.einsum('bhts,bhsv->bhtv', scores, v_t)
        b_last = b_t[:, :, -1, :]
        k_dec = k_t * jnp.exp(b_last[:, :, None, :] - b_t)
        new_state = jnp.exp(b_last)[..., None] * state + jnp.einsum('bhsk,bhsv->bhkv', k_dec, v_t)
        return new_state, o

    state0 = jnp.zeros((bsz, HGRN_HEADS, HGRN_HEAD_DIM, HGRN_HEAD_DIM), jnp.float32)
    _, o = lax.scan(step, state0, (qc, kc, vc, bc))
    o = o.transpose(1, 0, 3, 2, 4).reshape(bsz, seq, HGRN_HEADS, HGRN_HEAD_DIM)
    g = g.astype(jnp.float32).reshape(bsz, seq, HGRN_HEADS, HGRN_HEAD_DIM)
    o = rmsnorm_2(o, g_norm_w) * jax.nn.silu(g)
    return jnp.einsum('bsd,de->bse', o.reshape(bsz, seq, D_MODEL).astype(h.dtype), w_out)

def swiglu_ffn(h, w_in, w_out):
    gate, up = jnp.split(jnp.einsum('bsd,df->bsf', h, w_in), 2, axis=-1)
    return jnp.einsum('bsf,fd->bsd', jax.nn.silu(gate) * up, w_out)

def second_inputs(seed: int = 0) -> dict:
    key = jax.random.key(seed)
    ks = jax.random.split(key, 11)
    f32 = jnp.float32

    def normal(k, shape, fan_in):
        return jax.random.normal(k, shape, f32) * (fan_in ** -0.5)

    x = jax.random.normal(ks[0], (BATCH, SEQ, D_MODEL), f32)
    fox_w_in = normal(ks[1], (N_FOX, D_MODEL, 3 * D_MODEL + FOX_HEADS), D_MODEL)
    fox_b_f = jax.random.uniform(ks[2], (N_FOX, FOX_HEADS), f32, 1.0, 4.0)
    fox_w_out = normal(ks[3], (N_FOX, D_MODEL, D_MODEL), D_MODEL)
    hgrn_w_in = normal(ks[4], (N_HGRN, D_MODEL, 4 * D_MODEL), D_MODEL)
    hgrn_lb_table = 0.5 * jax.random.normal(ks[5], (DEPTH + 1, D_MODEL), f32)
    hgrn_gnorm = 1.0 + 0.02 * jax.random.normal(ks[6], (N_HGRN, HGRN_HEAD_DIM), f32)
    hgrn_w_out = normal(ks[7], (N_HGRN, D_MODEL, D_MODEL), D_MODEL)
    ffn_w_in = normal(ks[8], (DEPTH, D_MODEL, 2 * D_FF_2), D_MODEL)
    ffn_w_out = normal(ks[9], (DEPTH, D_FF_2, D_MODEL), D_FF_2)
    norm_gains = 1.0 + 0.02 * jax.random.normal(ks[10], (DEPTH, 4, D_MODEL), f32)
    return {'x': x, 'fox_w_in': fox_w_in, 'fox_b_f': fox_b_f, 'fox_w_out': fox_w_out,
            'hgrn_w_in': hgrn_w_in, 'hgrn_lb_table': hgrn_lb_table, 'hgrn_gnorm': hgrn_gnorm,
            'hgrn_w_out': hgrn_w_out, 'ffn_w_in': ffn_w_in, 'ffn_w_out': ffn_w_out,
            'norm_gains': norm_gains}

def second_block(x, fox_w_in, fox_b_f, fox_w_out, hgrn_w_in, hgrn_lb_table, hgrn_gnorm,
              hgrn_w_out, ffn_w_in, ffn_w_out, norm_gains):
    lower_bounds = jnp.cumsum(jax.nn.softmax(hgrn_lb_table.astype(jnp.float32), axis=0), axis=0)
    h = x
    for layer in range(DEPTH):
        j = layer // N_MIXERS
        hn = rmsnorm_2(h, norm_gains[layer, 0])
        if layer % N_MIXERS == 0:
            mixed = fox_attention(hn, fox_w_in[j], fox_b_f[j], fox_w_out[j])
        else:
            mixed = hgrn2_recurrence(hn, hgrn_w_in[j], lower_bounds[layer], hgrn_gnorm[j],
                                     hgrn_w_out[j])
        h = h + rmsnorm_2(mixed, norm_gains[layer, 1])
        hn = rmsnorm_2(h, norm_gains[layer, 2])
        h = h + rmsnorm_2(swiglu_ffn(hn, ffn_w_in[layer], ffn_w_out[layer]), norm_gains[layer, 3])
    return h


def setup_inputs(seed=0):
    out = dict(first_inputs(seed))
    for name, value in second_inputs(seed + 1).items():
        if name != "x":
            out[name + "_2"] = value
    return out


def reference(
    x, l0_ffn1_pre_g, l0_ffn1_post_g, l0_ffn1_w_gate, l0_ffn1_w_up, l0_ffn1_w_down,
    l0_mix_pre_g, l0_mix_post_g, l0_w_in, l0_cmp_pe_k, l0_cmp_w1_k, l0_cmp_w2_k, l0_cmp_pe_v,
    l0_cmp_w1_v, l0_cmp_w2_v, l0_conv_w, l0_conv_b, l0_w_out, l0_ffn2_pre_g, l0_ffn2_post_g,
    l0_ffn2_w_gate, l0_ffn2_w_up, l0_ffn2_w_down, l1_ffn1_pre_g, l1_ffn1_post_g, l1_ffn1_w_gate,
    l1_ffn1_w_up, l1_ffn1_w_down, l1_mix_pre_g, l1_mix_post_g, l1_mu, l1_w_r, l1_w_k, l1_w_v,
    l1_w_o, l1_w0, l1_w_dec1, l1_w_dec2, l1_a0, l1_w_a1, l1_w_a2, l1_w_g1, l1_w_g2, l1_k_k,
    l1_k_a, l1_r_k, l1_lnx_g, l1_lnx_b, l1_ffn2_pre_g, l1_ffn2_post_g, l1_ffn2_w_gate,
    l1_ffn2_w_up, l1_ffn2_w_down, fox_w_in_2, fox_b_f_2, fox_w_out_2, hgrn_w_in_2,
    hgrn_lb_table_2, hgrn_gnorm_2, hgrn_w_out_2, ffn_w_in_2, ffn_w_out_2, norm_gains_2,
):
    x = first_block(
        x, l0_ffn1_pre_g, l0_ffn1_post_g, l0_ffn1_w_gate, l0_ffn1_w_up, l0_ffn1_w_down,
        l0_mix_pre_g, l0_mix_post_g, l0_w_in, l0_cmp_pe_k, l0_cmp_w1_k, l0_cmp_w2_k,
        l0_cmp_pe_v, l0_cmp_w1_v, l0_cmp_w2_v, l0_conv_w, l0_conv_b, l0_w_out, l0_ffn2_pre_g,
        l0_ffn2_post_g, l0_ffn2_w_gate, l0_ffn2_w_up, l0_ffn2_w_down, l1_ffn1_pre_g,
        l1_ffn1_post_g, l1_ffn1_w_gate, l1_ffn1_w_up, l1_ffn1_w_down, l1_mix_pre_g,
        l1_mix_post_g, l1_mu, l1_w_r, l1_w_k, l1_w_v, l1_w_o, l1_w0, l1_w_dec1, l1_w_dec2,
        l1_a0, l1_w_a1, l1_w_a2, l1_w_g1, l1_w_g2, l1_k_k, l1_k_a, l1_r_k, l1_lnx_g, l1_lnx_b,
        l1_ffn2_pre_g, l1_ffn2_post_g, l1_ffn2_w_gate, l1_ffn2_w_up, l1_ffn2_w_down,
    )
    return second_block(
        x, fox_w_in_2, fox_b_f_2, fox_w_out_2, hgrn_w_in_2, hgrn_lb_table_2, hgrn_gnorm_2,
        hgrn_w_out_2, ffn_w_in_2, ffn_w_out_2, norm_gains_2,
    )


_drawn_inputs = setup_inputs


def setup_inputs(seed=0):
    import zlib

    import numpy as np

    out = dict(_drawn_inputs(seed))
    spreads = {}
    factors = {'l0_cmp_pe_k': 8.0,
     'l1_w_dec1': 8.0,
     'l1_w_dec2': 8.0,
     'l1_ffn2_post_g': 2.978,
     'hgrn_gnorm_2': 51.713,
     'l1_lnx_b': 2.917}
    for name, (base, spread) in spreads.items():
        noise = np.random.default_rng([zlib.crc32(name.encode()), seed]).standard_normal(out[name].shape)
        drawn = base * np.exp(spread * noise) if base else spread * noise
        out[name] = __import__('jax').numpy.asarray(drawn.astype(out[name].dtype))
    for name, factor in factors.items():
        out[name] = (out[name] * factor).astype(out[name].dtype)
    return out
```

```python
from contextlib import ExitStack

import concourse.bass as bass
from concourse import mybir

F32 = mybir.dt.float32
F32R = mybir.dt.float32r
BF16 = mybir.dt.bfloat16
U32 = mybir.dt.uint32
ALU = mybir.AluOpType
ACT = mybir.ActivationFunctionType
AX_X = mybir.AxisListType.X

P = 128
SEQ = 256
D = 1024
KT = D // P
TT = SEQ // P
D_FF = 2816
SLAB = 2048
COLS = SLAB // KT
RING = 3
AHEAD = RING - 1
STEPS = D_FF // COLS
EPS = 1e-6
LNX_EPS = 64e-5
BIG = 1e32
STOP = 10
N_CONSTS = 5
MASKS_MADE = 43
SUBLAYERS = [("ffn", 3 * STEPS, 1), ("nsa", 17, 3), ("ffn", 3 * STEPS, 1), ("ffn", 3 * STEPS, 1), ("rwkv", 16, 3),
             ("ffn", 3 * STEPS, 1), ("fox", 16, 1), ("ffn", 3 * STEPS, 1), ("hgrn", 20, 1), ("ffn", 3 * STEPS, 1)]


def vector_names():
    names = []
    for ffn in ("l0_ffn1", "l0_ffn2", "l1_ffn1", "l1_ffn2"):
        names += [ffn + "_pre_g", ffn + "_post_g"]
    for layer in ("l0", "l1"):
        names += [layer + "_mix_pre_g", layer + "_mix_post_g"]
    names += ["mu%d" % i for i in range(6)]
    names += ["l1_w0", "l1_a0", "l1_k_k", "l1_k_a", "l1_r_k", "l1_lnx_g", "l1_lnx_b"]
    names += ["gain%d%d" % (layer, i) for layer in range(2) for i in range(4)]
    names += ["lb%d" % i for i in range(3)]
    return names


COL = {name: KT * i for i, name in enumerate(vector_names())}
N_VEC = KT * len(COL)
CONV_COL = N_VEC
PE_COL = CONV_COL + 16
GNORM_COL = PE_COL + 64
VEC_COLS = GNORM_COL + 1

SMALL, SMALL_COLS = {}, 0
for _name, _cols in (("g", KT * 24), ("f", KT * 16), ("w2_k", 64), ("w2_v", 64), ("b_f", 1), ("dec1", KT * 64),
                     ("a1", KT * 64), ("g1", KT * 128), ("dec2", D), ("a2", D), ("g2", D)):
    SMALL[_name] = (SMALL_COLS, _cols)
    SMALL_COLS += _cols


def build(nc, xT_dram, slabs_dram, vec_dram, small_dram, yT_dram, n_slabs):
    ctx = ExitStack()
    with ctx:
        def sb(name, shape, dt=F32):
            return ctx.enter_context(nc.sbuf_tensor(name, shape, dt))

        def sem(name):
            return ctx.enter_context(nc.semaphore(name))

        X = sb("residual", [P, KT, SEQ])
        RAW = sb("slab_raw", [P, RING, SLAB])
        HI = sb("slab_hi", [P, RING, SLAB], F32R)
        LO = sb("slab_lo", [P, RING, SLAB], F32R)
        XH = sb("operand_hi", [P, KT, SEQ], F32R)
        XL = sb("operand_lo", [P, KT, SEQ], F32R)
        MH = sb("mixed_hi", [P, KT, SEQ], F32R)
        ML = sb("mixed_lo", [P, KT, SEQ], F32R)
        SQ = sb("squares", [P, KT, SEQ])
        RSTD = sb("rstd_pre", [P, SEQ])
        RSTD_POST = sb("rstd_post", [P, SEQ])
        STD = sb("std", [P, 1, SEQ])
        EPSILON = sb("epsilons", [P, 2])
        TABLE = sb("table_preloads", [P, 40])
        VEC = sb("vectors", [P, VEC_COLS])
        SMALLW = sb("small_weights", [P, SMALL_COLS])
        MEAN = sb("mean_matrix", [P, P])
        ZERO = sb("zeros", [P, 512], BF16)
        IDENT = sb("identity", [P, P])
        LMASK = sb("level_masks", [P, 7, 2, P], BF16)
        CARRY = sb("carry", [P, SEQ])
        SCR = sb("stage_scratch", [P, 13100])
        PS = ctx.enter_context(nc.psum_tensor("psum", [P, 8, 512], F32))
        ACC = PS[:, 0:4, :].rearrange("p b (h t) -> p (b h) t", h=2)
        NORMED = SCR[:, 0:1024].rearrange("p (k t) -> p k t", k=4)
        GATE, UP = PS[:, 4, :], PS[:, 5, :]
        MS_PRE, MS_POST = PS[:, 6, 0:SEQ], PS[:, 7, 0:SEQ]

        raw_loaded = [sem("raw_loaded%d" % i) for i in range(RING)]
        hi_ready = sem("hi_ready")
        lo_ready = sem("lo_ready")
        products_done = sem("products_done")
        consts_loaded = sem("consts_loaded")
        consts_made = sem("consts_made")
        vec_ready = sem("vec_ready")
        x_ready = sem("x_ready")
        outputs_done = sem("outputs_done")
        small_loaded = sem("small_loaded")
        sq_ready = sem("squares_pre_ready")
        ms_ready = sem("mean_pre_ready")
        rstd_ready = sem("rstd_pre_ready")
        xh_ready = sem("operand_hi_ready")
        xl_ready = sem("operand_lo_ready")
        ysq_ready = sem("squares_post_ready")
        yms_ready = sem("mean_post_ready")
        std_ready, ystd_ready = sem("std_pre_ready"), sem("std_post_ready")
        dve_order = sem("vector_order")
        act_order = sem("scalar_order")
        gate_taken, up_taken = sem("gate_taken"), sem("up_taken")
        silu_ready = sem("silu_ready")
        hidden_ready = sem("hidden_ready")
        hh_ready, hl_ready = sem("hidden_hi_ready"), sem("hidden_lo_ready")
        stored = sem("stored")
        pool_order = sem("gpsimd_order")
        masks_made = sem("masks_made")

        def m_off(l, side):
            return (1 << l) if side == 0 else 0

        def slab(ring, n):
            return ring[:, n % RING, :].rearrange("p (k n) -> p k n", k=KT)

        def rows(ring, n):
            return ring[:, n % RING, :].rearrange("p (k n) -> p k n", k=2)

        class Order:
            def __init__(self, engine, semaphore):
                self.engine, self.semaphore, self.n = engine, semaphore, 0

            def after(self, instruction):
                self.n += 1
                instruction.then_inc(self.semaphore, 1)
                self.engine.wait_ge(self.semaphore, self.n)

        def split_hi(act, n, i=0):
            act.wait_ge(raw_loaded[n % RING], (i + n // RING) * 16 + 16)
            if n >= RING:
                act.wait_ge(products_done, i * RING + n - RING + 1)
            act.activation(HI[:, n % RING, :], RAW[:, n % RING, :], ACT.Copy).then_inc(hi_ready, 1)

        def split_lo(dve, n, i=0):
            dve.wait_ge(hi_ready, i * RING + n + 1)
            dve.tensor_tensor(LO[:, n % RING, :], RAW[:, n % RING, :], HI[:, n % RING, :].bitcast(F32),
                              ALU.subtract).then_inc(lo_ready, 1)

        def turn_hi(act, n, i=0):
            if n + AHEAD < n_slabs:
                split_hi(act, n + AHEAD, i)

        def turn_lo(dve, n, i=0):
            if n + AHEAD < n_slabs:
                split_lo(dve, n + AHEAD, i)

        def product(pe, out, w, x, start, stop):
            pe.matmul(out, w[0], x[0], start=start, stop=False, skip_group_check=True)
            pe.matmul(out, w[0], x[1], start=False, stop=False, skip_group_check=True)
            return pe.matmul(out, w[1], x[0], start=False, stop=stop, skip_group_check=True)

        def pre_squares(act, s):
            for b in range(4):
                act.wait_ge(x_ready, KT * s + 2 * b + 2)
                act.activation(SQ[:, 2 * b:2 * b + 2, :], X[:, 2 * b:2 * b + 2, :], ACT.Square).then_inc(sq_ready, 1)

        def pre_mean(pe, s):
            for k in range(KT):
                if k % 2 == 0:
                    pe.wait_ge(sq_ready, 4 * s + k // 2 + 1)
                last = pe.matmul(MS_PRE, MEAN[:], SQ[:, k, :], start=k == 0, stop=k == KT - 1)
            last.then_inc(ms_ready, 1)

        def pre_std(act, s):
            act.wait_ge(ms_ready, s + 1)
            act.activation(STD[:, 0, :], MS_PRE, ACT.Sqrt, bias=EPSILON[:, 0:1]).then_inc(std_ready, 1)

        def pre_rstd(dve, s):
            dve.wait_ge(std_ready, s + 1)
            dve.reciprocal(RSTD[:], STD[:, 0, :]).then_inc(rstd_ready, 1)

        def preload(act, function):
            preloads[0] += 1
            act.activation(TABLE[:, preloads[0] - 1:preloads[0]], EPSILON[:, 0:1], function)

        preloads = [0]

        def post_squares(act, s, n_end):
            preload(act, ACT.Sqrt)
            for b in range(4):
                if b < 3:
                    act.wait_ge(outputs_done, 3 * s + b + 1)
                else:
                    act.wait_ge(products_done, n_end)
                act.activation(SQ[:, 2 * b:2 * b + 2, :], ACC[:, 2 * b:2 * b + 2, :], ACT.Square).then_inc(ysq_ready, 1)

        def post_mean(pe, s, b):
            pe.wait_ge(ysq_ready, 4 * s + b + 1)
            for k in (2 * b, 2 * b + 1):
                last = pe.matmul(MS_POST, MEAN[:], SQ[:, k, :], start=k == 0, stop=k == KT - 1)
            if b == 3:
                last.then_inc(yms_ready, 1)

        def post_std(act, s):
            act.wait_ge(yms_ready, s + 1)
            act.activation(STD[:, 0, :], MS_POST, ACT.Sqrt, bias=EPSILON[:, 0:1]).then_inc(ystd_ready, 1)

        def post_add(dve, order, s, col):
            dve.wait_ge(ystd_ready, s + 1)
            order.after(dve.reciprocal(RSTD_POST[:], STD[:, 0, :]))
            first = order.n
            for k in range(KT + 3):
                if k < KT:
                    if k >= 4:
                        dve.wait_ge(x_ready, KT * (s + 1) + k - 3)
                    dve.scalar_tensor_tensor(NORMED[:, k % 4, :], ACC[:, k, :], VEC[:, col + k:col + k + 1],
                                             RSTD_POST[:], ALU.mult, ALU.mult).then_inc(dve_order, 1)
                    order.n += 1
                if 1 <= k <= KT:
                    dve.wait_ge(dve_order, first + k)
                    dve.tensor_tensor(X[:, k - 1, :], X[:, k - 1, :], NORMED[:, (k - 1) % 4, :], ALU.add).then_inc(x_ready, 1)
                if k >= 3 and s + 1 in ffn_operand:
                    ffn_lo(dve, *ffn_operand[s + 1], k - 3)

        def ffn_lo(dve, op, col, k):
            dve.wait_ge(xh_ready, KT * op + k + 1)
            dve.wait_ge(x_ready, KT * sublayer_of[op] + k + 1)
            dve.scalar_tensor_tensor(XL[:, k, :], X[:, k, :], VEC[:, col + k:col + k + 1], XH[:, k, :].bitcast(F32),
                                     ALU.mult, ALU.subtract).then_inc(xl_ready, 1)

        HH, HL = MH[:, 0:2, :], ML[:, 0:2, :]
        GS, US, SILU, HID = (SCR[:, 512 * i:512 * (i + 1)] for i in range(4))
        RSTD2 = RSTD[:, None, :].to_broadcast([P, 2, SEQ])

        def two(ap):
            return ap.rearrange("p (h t) -> p h t", h=2)

        def ffn_act(act, s, f, n0, op, col):
            for k in range(KT):
                act.wait_ge(x_ready, KT * s + k + 1)
                act.activation(XH[:, k, :], X[:, k, :], ACT.Copy, scale=VEC[:, col + k:col + k + 1]).then_inc(xh_ready, 1)
            pre_squares(act, s)
            pre_std(act, s)
            preload(act, ACT.Silu)

            def gate_turn(n, j, i=0):
                turn_hi(act, n, i)
                act.wait_ge(gate_taken, j + STEPS * f + 1)
                act.activation(SILU, GS, ACT.Silu).then_inc(silu_ready, 1)

            def hidden_hi(j):
                act.wait_ge(hidden_ready, j + STEPS * f + 1)
                act.activation(HH, two(HID), ACT.Copy).then_inc(hh_ready, 1)

            gate_turn(n0, 0)
            turn_hi(act, n0 + 1)
            hidden_hi(0)

            def step(n, j, i=0):
                gate_turn(n, j, i)
                turn_hi(act, n + 1, i)
                turn_hi(act, n + 2, i)
                act.wait_ge(products_done, i * RING + n + 3)
                hidden_hi(j)

            with act.Fori(0, STEPS - 2) as i:
                step(n0 + 2, i + 1, i)
            step(n0 + 3 * STEPS - 4, STEPS - 1)
            turn_hi(act, n0 + 3 * STEPS - 1)
            post_squares(act, s, n0 + 3 * STEPS)
            post_std(act, s)

        def ffn_dve(dve, order, s, f, n0, op, col, post_col):
            if s == 0:
                for k in range(KT):
                    ffn_lo(dve, op, col, k)
            pre_rstd(dve, s)

            def gate_turn(n, j, i=0):
                turn_lo(dve, n, i)
                dve.wait_ge(products_done, i * RING + n + 1)
                dve.wait_ge(rstd_ready, s + 1)
                dve.tensor_tensor(two(GS), two(GATE), RSTD2, ALU.mult).then_inc(gate_taken, 1)

            def up_turn(n, j, i=0):
                turn_lo(dve, n, i)
                dve.wait_ge(products_done, i * RING + n + 1)
                dve.tensor_tensor(two(US), two(UP), RSTD2, ALU.mult).then_inc(up_taken, 1)
                dve.wait_ge(up_taken, j + STEPS * f + 1)
                dve.wait_ge(silu_ready, j + STEPS * f + 1)
                dve.tensor_tensor(HID, US, SILU, ALU.mult).then_inc(hidden_ready, 1)

            def hidden_lo(j):
                dve.wait_ge(hh_ready, j + STEPS * f + 1)
                dve.tensor_tensor(HL, two(HID), HH.bitcast(F32), ALU.subtract).then_inc(hl_ready, 1)

            gate_turn(n0, 0)
            up_turn(n0 + 1, 0)
            hidden_lo(0)

            def step(n, j, i=0):
                gate_turn(n, j, i)
                up_turn(n + 1, j, i)
                turn_lo(dve, n + 2, i)
                hidden_lo(j)

            with dve.Fori(0, STEPS - 2) as i:
                step(n0 + 2, i + 1, i)
            step(n0 + 3 * STEPS - 4, STEPS - 1)
            turn_lo(dve, n0 + 3 * STEPS - 1)
            post_add(dve, order, s, post_col)

        def open_outputs(pe, s):
            for b in range(4):
                if b == 0 and s:
                    pe.wait_ge(x_ready, KT * (s + 1))
                pe.matmul(PS[:, b, :], ZERO[:, 0:P], ZERO[:], start=True, stop=False, skip_group_check=True)

        def row_products(pe, n, xh, xl, i=0, end=None):
            pe.wait_ge(lo_ready, i * RING + n + 1)
            for m in range(KT):
                for k in range(2):
                    w = [rows(r, n)[:, k, m * P:(m + 1) * P] for r in (HI, LO)]
                    last = product(pe, ACC[:, m, :], w, (xh[:, k, :], xl[:, k, :]), False, end is not None and k == 1)
                if m == KT - 1:
                    last.then_inc(products_done, 1)
                elif end is not None and m % 2:
                    last.then_inc(outputs_done, 1)
                if end is not None and m in (3, 5, 7):
                    post_mean(pe, end, (m - 3) // 2)
            if end is not None:
                post_mean(pe, end, 3)

        def opening_products(pe, n, op):
            pe.wait_ge(lo_ready, n + 2)
            for k in range(KT):
                pe.wait_ge(xl_ready, KT * op + k + 1)
                for u, bank in enumerate((GATE, UP)):
                    for m in range(2):
                        w = [slab(r, n + u)[:, k, m * P:(m + 1) * P] for r in (HI, LO)]
                        last = product(pe, bank[:, m * SEQ:(m + 1) * SEQ], w, (XH[:, k, :], XL[:, k, :]),
                                       k == 0 and m == 0, k == KT - 1)
                    if k == KT - 1:
                        last.then_inc(products_done, 1)

        def column_products(pe, n, bank, i=0, op=None, x=(XH, XL), tiles=2):
            pe.wait_ge(lo_ready, i * RING + n + 1)
            for m in range(2):
                for k in range(KT):
                    if op is not None and m == 0:
                        pe.wait_ge(xl_ready, KT * op + k + 1)
                    w = [slab(r, n)[:, k, m * P:(m + 1) * P] for r in (HI, LO)]
                    last = product(pe, bank[:, m * SEQ:(m + 1) * SEQ], w, (x[0][:, k, :], x[1][:, k, :]), k == 0, k == KT - 1)
            last.then_inc(products_done, 1)

        def ffn_pe(pe, s, f, n0, op):
            opening_products(pe, n0, op)
            pre_mean(pe, s)
            open_outputs(pe, s)
            with pe.Fori(0, STEPS - 1) as i:
                pe.wait_ge(gate_taken, i + STEPS * f + 1)
                column_products(pe, n0 + 2, GATE, i)
                pe.wait_ge(up_taken, i + STEPS * f + 1)
                column_products(pe, n0 + 3, UP, i)
                pe.wait_ge(hl_ready, i + STEPS * f + 1)
                row_products(pe, n0 + 4, HH, HL, i)
            pe.wait_ge(hl_ready, STEPS * (f + 1))
            row_products(pe, n0 + 3 * STEPS - 1, HH, HL, end=s)

        N_H, N_G, HD, N_CMP = 8, 2, 64, 16
        UNITS = [(j, qt, hh) for j in range(4) for qt in range(TT) for hh in range(2)]
        HN = SCR[:, 0:2048].rearrange("p (k t) -> p k t", k=KT)
        QT = SCR[:, 2048:3072].rearrange("p (j t) -> p j t", j=4)
        KTB = SCR[:, 3072:4096].rearrange("p (b g t) -> p b g t", b=2, g=2)
        VB = SCR[:, 4096:4608].rearrange("p (b t c) -> p b t c", b=2, t=2)
        KV2 = SCR[:, 4608:5696].rearrange("p (v g t) -> p v g t", v=2, g=2)
        KV2H = MH[:].rearrange("p k t -> p (k t)")[:, 0:1088]
        KV2L = ML[:].rearrange("p k t -> p (k t)")[:, 0:1088]
        PEH = MH[:].rearrange("p k t -> p (k t)")[:, 1088:1152]
        PEL = ML[:].rearrange("p k t -> p (k t)")[:, 1088:1152]
        GELU = SCR[:, 5696:5760].rearrange("p (v n) -> p v n", v=2)
        HB = SCR[:, 5760:5764]
        KC2 = SCR[:, 5764:5796]
        VC = SCR[:, 5796:5924]
        GATES = SCR[:, 5924:5972]
        DIST = SCR[:, 5972:6516].rearrange("p (q s) -> p q s", q=2)
        SB = SCR[:, 6516:7572].rearrange("p (b s) -> p b s", b=2)
        PB = SCR[:, 7572:8628].rearrange("p (b s) -> p b s", b=2)
        MX = SCR[:, 8628:8636].rearrange("p (b s) -> p b s", b=2)
        NM = SCR[:, 8636:8644].rearrange("p (b s) -> p b s", b=2)
        SM = SCR[:, 8644:8652].rearrange("p (b s) -> p b s", b=2)
        RC = SCR[:, 8652:8660].rearrange("p (b s) -> p b s", b=2)
        PTS = SCR[:, 8660:9940].rearrange("p (b s) -> p b s", b=2)
        CC, CU, CB = (SCR[:, 9940 + 512 * i:9940 + 512 * (i + 1)] for i in range(3))
        Z = SCR[:, 11476:11992].rearrange("p (m t) -> p m t", m=2)
        YC = SCR[:, 11992:12504].rearrange("p (m t) -> p m t", m=2)
        DISTI = SCR[:, 12504:13048].bitcast(mybir.dt.int32)
        BANK = [PS[:, 4, :], PS[:, 5, :]]
        nsa_taken = sem("nsa_bank_taken")
        hn_ready = sem("normed_ready")
        gates_ready, gates_taken = sem("nsa_gates_ready"), sem("nsa_gates_taken")
        gelu_ready = sem("nsa_gelu_ready")
        cmp_ready, cmp_taken = sem("nsa_compressed_ready"), sem("nsa_compressed_taken")
        scores_ready, biased = sem("nsa_scores_ready"), sem("nsa_scores_biased")
        nm_ready, exp_ready, prob_ready = sem("nsa_max_ready"), sem("nsa_exp_ready"), sem("nsa_probs_ready")
        pt_ready, pt_taken_a, pt_taken_d = sem("nsa_pt_ready"), sem("nsa_pt_taken_a"), sem("nsa_pt_taken_d")
        o_ready, oh_ready, ol_ready = sem("nsa_out_ready"), sem("nsa_out_hi_ready"), sem("nsa_out_lo_ready")
        conv_in, conv_out, convh_ready, convl_ready = (sem("conv_" + x) for x in ("in", "out", "hi", "lo"))

        def mixer_operand_act(act, mixer, op):
            for k in range(KT):
                act.wait_ge(hn_ready, KT * mixer + k + 1)
                act.activation(XH[:, k, :], HN[:, k, :], ACT.Copy).then_inc(xh_ready, 1)

        def mixer_norm_dve(dve, s, mixer, col, op=None):
            dve.wait_ge(rstd_ready, s + 1)
            for k in range(KT + 2):
                if k < KT:
                    dve.scalar_tensor_tensor(HN[:, k, :], X[:, k, :], VEC[:, col + k:col + k + 1], RSTD[:],
                                             ALU.mult, ALU.mult).then_inc(hn_ready, 1)
                if k >= 2 and op is not None:
                    dve.wait_ge(xh_ready, KT * op + k - 1)
                    dve.tensor_tensor(XL[:, k - 2, :], HN[:, k - 2, :], XH[:, k - 2, :].bitcast(F32),
                                      ALU.subtract).then_inc(xl_ready, 1)

        def token_products(pe, n, out, cols, x=(XH, XL)):
            for t in range(TT):
                for k in range(KT):
                    w = [slab(r, n)[:, k, cols[0]:cols[1]] for r in (HI, LO)]
                    xt = [y[:, k, t * P:(t + 1) * P] for y in x]
                    last = product(pe, out[t], xt, w, k == 0, k == KT - 1)
            return last

        def nsa_pool(pool):
            for qt in range(TT):
                for part, (a, b, base, step) in enumerate([(0, 16, qt * P - 31, -16), (16, 272, qt * P, -1)]):
                    pool.iota(DISTI[:, qt * 272 + a:qt * 272 + b], pattern=[[step, b - a]], base=base,
                              channel_multiplier=1).then_inc(pool_order, 1)
            pool.wait_ge(pool_order, 5)
            pool.tensor_copy(DIST.rearrange("p q s -> p (q s)"), DISTI).then_inc(pool_order, 1)
            pool.wait_ge(pool_order, 6)
            for qt in range(TT):
                for part, (a, b, base, step) in enumerate([(0, 16, qt * P - 31, -16), (16, 272, qt * P, -1)]):
                    d = DIST[:, qt, a:b]
                    pool.affine_select(out=d, in_=d, compare_op=ALU.is_ge, fill=BIG, base=base,
                                       pattern=[[step, b - a]], channel_multiplier=1).then_inc(pool_order, 1)
            pool.wait_ge(pool_order, 10)
            for qt in range(TT):
                pool.memset(DIST[:, qt, 15:16], BIG)
            pool.memset(KV2[:, :, :, 255:272], 0.0)
            pool.memset(Z[:, :, 0:2], 0.0).then_inc(consts_made, 1)

        def nsa_act(act, order, s, n0, op, col):
            pre_squares(act, s)
            pre_std(act, s)
            mixer_operand_act(act, 0, op)
            act.activation(PEH, VEC[:, PE_COL:PE_COL + 64], ACT.Copy).then_inc(xh_ready, KT)
            act.wait_ge(gates_ready, 1)
            act.activation(GATES, PS[:, 7, 0:48], ACT.Sigmoid).then_inc(gates_taken, 1)
            for i in range(2):
                turn_hi(act, n0 + i)
                act.wait_ge(products_done, n0 + i + 1)
                act.activation(QT[:, 2 * i:2 * i + 2, :], two(BANK[i % 2]), ACT.Copy, scale=HD ** -0.5).then_inc(nsa_taken, 1)
            turn_hi(act, n0 + 2)
            act.wait_ge(consts_made, N_CONSTS)
            act.wait_ge(products_done, n0 + 3)
            for v in range(2):
                for g in range(N_G):
                    src = BANK[0][HD * g:HD * g + HD, v * SEQ:(v + 1) * SEQ]
                    act.activation(KV2[0:HD, v, g, 0:SEQ], src, ACT.Copy)
                    last = act.activation(KV2[HD:P, v, g, 0:SEQ - 1], src[:, 1:SEQ], ACT.Copy)
            last.then_inc(nsa_taken, 1)
            act.wait_ge(nsa_taken, 3)
            act.activation(KV2H, SCR[:, 4608:5696], ACT.Copy).then_inc(xh_ready, KT)
            for b in range(2):
                turn_hi(act, n0 + 3 + b)
                act.wait_ge(products_done, n0 + 4 + b)
                bank = BANK[(3 + b) % 2]
                for g in range(N_G):
                    for half in range(2):
                        act.activation(KTB[HD * half:HD * half + HD, b, g, :], bank[HD * g:HD * g + HD, 0:SEQ], ACT.Copy)
                act.activation(VB[:, b, :, :], bank[:, SEQ:2 * SEQ].rearrange("p (t c) -> p t c", t=2), ACT.Copy).then_inc(nsa_taken, 1)
            for v in range(2):
                turn_hi(act, n0 + 5 + v)
                act.wait_ge(products_done, n0 + 6 + v)
                bank = BANK[(5 + v) % 2]
                order.after(act.activation(HB[:, 2 * v:2 * v + 2], bank[:, 32:34], ACT.Copy))
                act.activation(GELU[:, v, :], bank[:, 0:32], ACT.Gelu_apprx_tanh, bias=HB[:, 2 * v:2 * v + 1]).then_inc(nsa_taken, 1)
            act.wait_ge(cmp_ready, 1)
            act.activation(KC2, PS[:, 7, 0:32], ACT.Copy)
            act.activation(VC[0:N_CMP, :], PS[0:N_CMP, 7, 64:192], ACT.Copy).then_inc(cmp_taken, 1)
            for c in range(2):
                for i, dst in enumerate((CC, CU, CB)):
                    turn_hi(act, n0 + 7 + 3 * c + i)
                    act.wait_ge(products_done, n0 + 8 + 3 * c + i)
                    if c and i == 0:
                        act.wait_ge(conv_out, 1)
                    last = act.activation(dst, BANK[(7 + 3 * c + i) % 2], ACT.Copy)
                    last.then_inc(nsa_taken, 1)
                act.wait_ge(conv_out, c + 1)
                act.activation(MH[:, 4 + 2 * c:6 + 2 * c, :], two(CB), ACT.Copy).then_inc(convh_ready, 1)

            def exps(u):
                j, qt, hh = UNITS[u]
                nk = P * (qt + 1)
                act.wait_ge(nm_ready, u + 1)
                if u >= 2:
                    act.wait_ge(pt_ready, u - 1)
                for i, (a, b) in enumerate([(0, 16), (16, 16 + nk), (16 + nk, 16 + 2 * nk)]):
                    last = act.activation(PB[:, u % 2, a:b], SB[:, u % 2, a:b], ACT.Exp, bias=NM[:, u % 2, i:i + 1],
                                          accum_out=SM[:, u % 2, i:i + 1])
                last.then_inc(exp_ready, 1)

            def take_pt(u):
                j, qt, hh = UNITS[u]
                nk = P * (qt + 1)
                act.wait_ge(pt_ready, u + 1)
                if u >= 2:
                    act.wait_ge(o_ready, u - 1)
                act.activation(PTS[:, u % 2, 0:nk], PS[:, 4, 0:nk], ACT.Copy)
                act.activation(PTS[0:N_CMP, u % 2, 512:640], PS[0:N_CMP, 4, 256:384], ACT.Copy).then_inc(pt_taken_a, 1)

            def out_hi(j):
                act.wait_ge(o_ready, 4 * j + 4)
                act.activation(MH[:, j, :], PS[:, 6 + j % 2, 0:SEQ], ACT.Copy).then_inc(oh_ready, 1)

            for u in range(16):
                exps(u)
                if u:
                    take_pt(u - 1)
                if u % 4 == 1 and u > 4:
                    out_hi(u // 4 - 1)
            take_pt(15)
            out_hi(3)
            for i in range(4):
                turn_hi(act, n0 + 13 + i)
            post_squares(act, s, n0 + 17)
            post_std(act, s)

        def nsa_dve(dve, order, s, n0, op, col, post_col):
            pre_rstd(dve, s)
            mixer_norm_dve(dve, s, 0, col, op)
            for i in range(3):
                turn_lo(dve, n0 + i)
            dve.wait_ge(xh_ready, KT * (op + 2))
            dve.tensor_tensor(PEL, VEC[:, PE_COL:PE_COL + 64], PEH.bitcast(F32), ALU.subtract).then_inc(xl_ready, KT)
            dve.wait_ge(xh_ready, KT * (op + 3))
            dve.tensor_tensor(KV2L, SCR[:, 4608:5696], KV2H.bitcast(F32), ALU.subtract).then_inc(xl_ready, KT)
            for i in range(3, 7):
                turn_lo(dve, n0 + i)
            for c in range(2):
                turn_lo(dve, n0 + 7 + 3 * c)
                turn_lo(dve, n0 + 8 + 3 * c)
                dve.wait_ge(nsa_taken, 9 + 3 * c)
                if c:
                    dve.wait_ge(convh_ready, 1)
                order.after(dve.tensor_tensor(Z[:, :, 2:258], two(CC), two(CU), ALU.mult))
                for m in range(2):
                    w = [VEC[:, CONV_COL + 4 * tap + 2 * c + m:CONV_COL + 4 * tap + 2 * c + m + 1] for tap in range(4)]
                    order.after(dve.tensor_scalar(YC[:, m, :], Z[:, m, 0:256], w[0], w[3], ALU.mult, ALU.add))
                    order.after(dve.scalar_tensor_tensor(YC[:, m, :], Z[:, m, 1:257], w[1], YC[:, m, :], ALU.mult, ALU.add))
                    order.after(dve.scalar_tensor_tensor(YC[:, m, :], Z[:, m, 2:258], w[2], YC[:, m, :], ALU.mult, ALU.add))
                turn_lo(dve, n0 + 9 + 3 * c)
                dve.wait_ge(nsa_taken, 10 + 3 * c)
                dve.tensor_tensor(two(CB), two(CB), YC, ALU.mult).then_inc(conv_out, 1)
                dve.wait_ge(convh_ready, c + 1)
                dve.tensor_tensor(ML[:, 4 + 2 * c:6 + 2 * c, :], two(CB), MH[:, 4 + 2 * c:6 + 2 * c, :].bitcast(F32),
                                  ALU.subtract).then_inc(convl_ready, 1)

            def bias(u):
                j, qt, hh = UNITS[u]
                nk = P * (qt + 1)
                slope = -2.0 ** -(2 * j + hh + 1)
                dve.wait_ge(scores_ready, u + 1)
                if u >= 2:
                    dve.wait_ge(exp_ready, u - 1)
                bank = 2 * (u % 2)
                dve.scalar_tensor_tensor(SB[:, u % 2, 0:16 + nk], DIST[:, qt, 0:16 + nk], slope, PS[:, bank, 0:16 + nk],
                                         ALU.mult, ALU.add)
                dve.scalar_tensor_tensor(SB[:, u % 2, 16 + nk:16 + 2 * nk], DIST[:, qt, 16:16 + nk], slope,
                                         PS[:, bank + 1, 0:nk], ALU.mult, ALU.add).then_inc(biased, 1)
                dve.wait_ge(biased, u + 1)
                dve.reduce_max(MX[:, u % 2, 0:1], SB[:, u % 2, 0:16], AX_X)
                order.after(dve.reduce_max(MX[:, u % 2, 1:3], SB[:, u % 2, 16:16 + 2 * nk].rearrange("p (b s) -> p b s", b=2), AX_X))
                dve.tensor_scalar(NM[:, u % 2, 0:3], MX[:, u % 2, 0:3], -1e20, -1.0, ALU.max, ALU.mult).then_inc(nm_ready, 1)

            def normalize(u):
                j, qt, hh = UNITS[u]
                nk, h = P * (qt + 1), 2 * j + hh
                dve.wait_ge(exp_ready, u + 1)
                r = RC[:, u % 2, 0:3]
                order.after(dve.tensor_scalar(r, SM[:, u % 2, 0:3], 1e-30, None, ALU.max))
                order.after(dve.reciprocal(r, r))
                order.after(dve.tensor_tensor(r, r, GATES[:, qt * 24 + 3 * h:qt * 24 + 3 * h + 3], ALU.mult))
                for i, (a, b) in enumerate([(0, 16), (16, 16 + nk), (16 + nk, 16 + 2 * nk)]):
                    last = dve.tensor_scalar(PB[:, u % 2, a:b], PB[:, u % 2, a:b], RC[:, u % 2, i:i + 1], None, ALU.mult)
                last.then_inc(prob_ready, 1)

            def take_pt(u):
                j, qt, hh = UNITS[u]
                nk = P * (qt + 1)
                dve.wait_ge(pt_ready, u + 1)
                if u >= 2:
                    dve.wait_ge(o_ready, u - 1)
                dve.tensor_copy(PTS[:, u % 2, 256:256 + nk], PS[:, 5, 0:nk]).then_inc(pt_taken_d, 1)

            def out_lo(j):
                dve.wait_ge(oh_ready, j + 1)
                dve.tensor_tensor(ML[:, j, :], PS[:, 6 + j % 2, 0:SEQ], MH[:, j, :].bitcast(F32), ALU.subtract).then_inc(ol_ready, 1)

            dve.wait_ge(gates_taken, 1)
            bias(0)
            bias(1)
            for u in range(16):
                normalize(u)
                if u + 2 < 16:
                    bias(u + 2)
                if u:
                    take_pt(u - 1)
                if u % 4 == 1 and u > 4:
                    out_lo(u // 4 - 1)
            take_pt(15)
            out_lo(3)
            for i in range(4):
                turn_lo(dve, n0 + 13 + i)
            post_add(dve, order, s, post_col)

        def nsa_pe(pe, s, n0, op):
            pre_mean(pe, s)
            pe.wait_ge(small_loaded, 16)
            pe.wait_ge(consts_made, N_CONSTS)
            g_cols = SMALLW[:, SMALL["g"][0]:SMALL["g"][0] + KT * 24].rearrange("p (k n) -> p k n", k=KT)
            if s:
                pe.wait_ge(x_ready, KT * (s + 1))
            for t in range(TT):
                for k in range(KT):
                    pe.wait_ge(hn_ready, k + 1)
                    last = pe.matmul(PS[:, 7, 24 * t:24 * t + 24], HN[:, k, t * P:(t + 1) * P], g_cols[:, k, :],
                                     start=k == 0, stop=k == KT - 1)
            last.then_inc(gates_ready, 1)
            opening_products(pe, n0, op)
            pe.wait_ge(nsa_taken, 1)
            column_products(pe, n0 + 2, BANK[0])
            for b in range(2):
                n, bank = n0 + 3 + b, BANK[(3 + b) % 2]
                pe.wait_ge(nsa_taken, 2 + b)
                pe.wait_ge(lo_ready, n + 1)
                for k in range(KT):
                    product(pe, bank[:, 0:SEQ], [slab(r, n)[:, k, 0:P] for r in (HI, LO)], (XH[:, k, :], XL[:, k, :]),
                            k == 0, k == KT - 1)
                last = token_products(pe, n, [bank[:, SEQ + P * t:SEQ + P * (t + 1)] for t in range(TT)], (P, 2 * P))
                last.then_inc(products_done, 1)
            kh = KV2H.rearrange("p (v g t) -> p v g t", v=2, g=2)
            kl = KV2L.rearrange("p (v g t) -> p v g t", v=2, g=2)
            pe.wait_ge(xl_ready, KT * (op + 3))
            pe.wait_ge(gates_taken, 1)
            for v, name in enumerate(("w2_k", "w2_v")):
                n, bank = n0 + 5 + v, BANK[(5 + v) % 2]
                pe.wait_ge(nsa_taken, 4 + v)
                pe.wait_ge(lo_ready, n + 1)
                w1 = [r[:, n % RING, :].rearrange("p (l n) -> p l n", l=16) for r in (HI, LO)]
                for l in range(16):
                    x = [y[:, v, :, 2 * l:2 * l + 241:16] for y in (kh, kl)]
                    product(pe, bank[:, 0:32].rearrange("p (g n) -> p g n", g=2), [w[:, l, :] for w in w1], x, l == 0, l == 15)
                for l in range(16):
                    x = [y[:, 32 * v + 2 * l:32 * v + 2 * l + 2] for y in (PEH, PEL)]
                    last = product(pe, bank[:, 32:34], [w[:, l, :] for w in w1], x, l == 0, l == 15)
                last.then_inc(products_done, 1)
            for v, name in enumerate(("w2_k", "w2_v")):
                w2 = SMALLW[:, SMALL[name][0]:SMALL[name][0] + 64]
                pe.wait_ge(nsa_taken, 6 + v)
                for g in range(N_G):
                    if v == 0:
                        for half in range(2):
                            pe.matmul(PS[HD * half:HD * half + HD, 7, 16 * g:16 * g + 16], w2, GELU[:, 0, 16 * g:16 * g + 16],
                                      start=True, stop=True)
                    else:
                        last = pe.matmul(PS[0:N_CMP, 7, 64 + 64 * g:128 + 64 * g], GELU[:, 1, 16 * g:16 * g + 16], w2,
                                         start=True, stop=True)
            last.then_inc(cmp_ready, 1)
            for i in range(6):
                pe.wait_ge(nsa_taken, 6 + i)
                column_products(pe, n0 + 7 + i, BANK[(7 + i) % 2])
            pe.wait_ge(nsa_taken, 13)
            pe.wait_ge(cmp_taken, 1)

            def scores(u):
                j, qt, hh = UNITS[u]
                nk, g, a = P * (qt + 1), j // 2, HD * hh
                if u >= 2:
                    pe.wait_ge(biased, u - 1)
                bank = 2 * (u % 2)
                q = QT[a:a + HD, j, qt * P:(qt + 1) * P]
                pe.matmul(PS[:, bank, 0:16], q, KC2[a:a + HD, 16 * g:16 * g + 16], start=True, stop=True)
                pe.matmul(PS[:, bank, 16:16 + nk], q, KTB[a:a + HD, 0, g, 0:nk], start=True, stop=True)
                pe.matmul(PS[:, bank + 1, 0:nk], q, KTB[a:a + HD, 1, g, 0:nk], start=True, stop=True).then_inc(scores_ready, 1)

            def transposes(u):
                j, qt, hh = UNITS[u]
                nk = P * (qt + 1)
                pe.wait_ge(prob_ready, u + 1)
                if u:
                    pe.wait_ge(pt_taken_a, u)
                    pe.wait_ge(pt_taken_d, u)
                for b in range(qt + 1):
                    pe.transpose(PS[:, 4, b * P:(b + 1) * P], PB[:, u % 2, 16 + b * P:16 + (b + 1) * P], IDENT[:])
                    pe.transpose(PS[:, 5, b * P:(b + 1) * P], PB[:, u % 2, 16 + nk + b * P:16 + nk + (b + 1) * P], IDENT[:])
                pe.transpose(PS[0:N_CMP, 4, 256:384], PB[:, u % 2, 0:16], IDENT[:]).then_inc(pt_ready, 1)

            def values(u):
                j, qt, hh = UNITS[u]
                g = j // 2
                pe.wait_ge(pt_taken_a, u + 1)
                pe.wait_ge(pt_taken_d, u + 1)
                if u % 4 == 0 and j >= 2:
                    pe.wait_ge(ol_ready, j - 1)
                out = PS[HD * hh:HD * hh + HD, 6 + j % 2, qt * P:(qt + 1) * P]
                pe.matmul(out, VC[0:N_CMP, HD * g:HD * g + HD], PTS[0:N_CMP, u % 2, 512:640], start=True, stop=False)
                for b in range(2):
                    for kb in range(qt + 1):
                        last = pe.matmul(out, VB[:, b, kb, HD * g:HD * g + HD], PTS[:, u % 2, 256 * b + P * kb:256 * b + P * (kb + 1)],
                                         start=False, stop=b == 1 and kb == qt)
                last.then_inc(o_ready, 1)

            scores(0)
            scores(1)
            for u in range(16):
                if u + 2 < 16:
                    scores(u + 2)
                transposes(u)
                if u:
                    values(u - 1)
            values(15)
            pe.wait_ge(biased, 16)
            open_outputs(pe, s)
            pe.wait_ge(convl_ready, 2)
            for i in range(4):
                if i < 2:
                    pe.wait_ge(ol_ready, 2 * i + 2)
                row_products(pe, n0 + 13 + i, MH[:, 2 * i:2 * i + 2, :], ML[:, 2 * i:2 * i + 2, :], end=s if i == 3 else None)

        DECAY = 2.718281828459045 ** -0.5
        NJ, TOPS = KT, 7
        V0 = SCR[:, 0:2048].rearrange("p (c n) -> p c n", c=2)
        XX = SCR[:, 2048:4096].rearrange("p (k t) -> p k t", k=KT)
        XI = [SCR[:, 4096 + 2048 * i:6144 + 2048 * i].rearrange("p (k t) -> p k t", k=KT) for i in range(2)]
        XI.append(SQ)
        RT = SCR[:, 8192:10240].rearrange("p (k t) -> p k t", k=KT)
        KF = SCR[:, 10240:12288].rearrange("p (k t) -> p k t", k=KT)
        WM, AM, GM = SCR[0:64, 12288:12544], SCR[0:64, 12544:12800], SCR[:, 12800:13056]
        RN = SCR[:, 13056:13088]
        OMK = SCR[:, 13088:13096]
        G4 = SCR[:, 2048:4096].rearrange("p (q n) -> p q n", q=4)
        TI = SCR[:, 4096:5120].rearrange("p (q n) -> p q n", q=4)
        NTS = SCR[:, 5120:5632].rearrange("p (c n) -> p c n", c=2)
        KR = [SCR[:, 5632 + 512 * i:6144 + 512 * i].rearrange("p (c w t) -> p c w t", c=2, w=2) for i in range(2)]
        BETA = [SCR[:, 6656 + 256 * i:6912 + 256 * i] for i in range(2)]
        KH = [SCR[:, 7168 + 256 * i:7424 + 256 * i] for i in range(2)]
        RK = [SCR[:, 7680 + 256 * i:7936 + 256 * i] for i in range(2)]
        S_T, A_T, C_T, D_T, EP, EN, EX, KKN = (SQ[:, i, :] for i in range(8))
        RFREE = SMALLW[:, SMALL["dec1"][0]:SMALL["dec1"][0] + 2048]
        TOK, RS, U_S, Y_C, YQ, BV, FO = (RFREE[:, 256 * i:256 * (i + 1)] for i in range(7))
        ST = RFREE[:, 1792:1920]
        RMN, RVR, RBS, SF = (RFREE[:, 1920 + 8 * i:1928 + 8 * i] for i in range(4))
        HSEL = sb("head_columns", [P, 2])
        MASK2 = sb("strict_inclusive", [P, 2 * P], BF16)
        rk_taken, rk_x, rk_mid, rk_mid_taken = (sem("rwkv_" + x) for x in ("bank_taken", "operand", "lora_mid", "lora_mid_taken"))
        rk_ksq, rk_n2, rk_n2max, rk_n2root, rk_n2done = (sem("rwkv_kk_" + x) for x in ("squares", "sums", "bounded", "root", "norm"))

        class Steps:
            def __init__(self, name, steps):
                self.semaphore, self.steps = sem(name), steps

            def at(self, j, step):
                return len(self.steps) * j + self.steps.index(step) + 1

        levels = [(l, c) for l in range(1, TOPS) for c in range(2)]
        pe_inv = [x + "%d%d" % lc for l in range(1, TOPS) for x, lc in
                  (("nt", (l, 0)), ("nt", (l, 1)), ("tnt", (l, 0)), ("tnt", (l, 1)))]
        ew_pe, ew_act, ew_dve = (Steps("rwkv_factors_" + e, x) for e, x in (
            ("tensor", ["lora", "norm"]), ("scalar", ["sigmoid", "exp"]), ("vector", ["exponents", "kk", "factors"])))
        in_pe = Steps("rwkv_inverse_tensor", ["matrices"] + pe_inv)
        in_act = Steps("rwkv_inverse_scalar", ["identity", "tokens"] + ["nt%d%d" % lc for lc in levels])
        in_dve = Steps("rwkv_inverse_vector", ["masked", "first"] + ["t%d%d" % lc for lc in levels])
        po_pe = Steps("rwkv_output_tensor", ["r0", "u0", "y0", "state", "r1", "u1", "y1", "turned"])
        po_act = Steps("rwkv_output_scalar", ["r0", "u0", "r1", "u1", "std", "hi"])
        po_dve = Steps("rwkv_output_vector", ["state", "variance", "normed", "output", "lo"])

        def rwkv_pool(pool):
            pool.memset(MASK2[:], 1.0).then_inc(pool_order, 1)
            pool.wait_ge(pool_order, 12)
            for w in range(2):
                v = MASK2[:, P * w:P * (w + 1)]
                pool.affine_select(out=v, in_=v, compare_op=ALU.is_ge, fill=0.0, base=w - 1, pattern=[[1, P]],
                                   channel_multiplier=-1).then_inc(consts_made, 1)

        def rwkv_act(act, order, s, n0, op, col):
            pre_squares(act, s)
            pre_std(act, s)

            def operand(i, hi):
                for k in range(KT):
                    act.wait_ge(rk_x, KT * i + k + 1)
                    act.activation(hi[:, k, :], XI[(0, 1, None, None, 2)[i]][:, k, :], ACT.Copy).then_inc(xh_ready, 1)

            def take(i):
                turn_hi(act, n0 + i)
                act.wait_ge(products_done, n0 + i + 1)
                bank = two(BANK[i % 2])
                if i < 8:
                    last = act.activation((RT, KF)[i // 4][:, 2 * (i % 4):2 * (i % 4) + 2, :], bank, ACT.Copy)
                else:
                    last = act.activation(V0[:, :, 256 * (i - 8):256 * (i - 7)], bank, ACT.Copy)
                last.then_inc(rk_taken, 1)

            operand(0, XH)
            operand(1, MH)
            for i in range(4):
                take(i)
            take(4)
            operand(4, XH)
            for i in range(5, 8):
                take(i)
            act.wait_ge(rk_mid, 1)
            act.activation(WM, PS[0:64, 6, 0:SEQ], ACT.Tanh).then_inc(rk_mid_taken, 1)
            act.wait_ge(rk_mid, 2)
            act.activation(AM, PS[0:64, 7, 0:SEQ], ACT.Copy).then_inc(rk_mid_taken, 1)
            act.wait_ge(rk_taken, 8)
            for k in range(KT):
                c = COL["l1_k_k"] + k
                last = act.activation(XI[1][:, k, :], KF[:, k, :], ACT.Square, scale=VEC[:, c:c + 1])
            last.then_inc(rk_ksq, 1)
            act.wait_ge(rk_x, KT * 6)
            for i in range(8, 12):
                take(i)
            act.wait_ge(rk_mid, 3)
            act.activation(GM, PS[:, 6, 0:SEQ], ACT.Sigmoid).then_inc(rk_mid_taken, 1)
            act.wait_ge(rk_n2max, 1)
            act.activation(RN, RN, ACT.Sqrt).then_inc(rk_n2root, 1)

            def factors(j, part):
                if part == 0:
                    act.wait_ge(ew_pe.semaphore, ew_pe.at(j, "lora"))
                    a0, w0 = COL["l1_a0"] + j, COL["l1_w0"] + j
                    act.activation(A_T, PS[:, 6, 0:SEQ], ACT.Sigmoid, bias=VEC[:, a0:a0 + 1])
                    act.activation(S_T, PS[:, 6, SEQ:2 * SEQ], ACT.Sigmoid, bias=VEC[:, w0:w0 + 1]).then_inc(ew_act.semaphore, 1)
                if part == 1:
                    act.wait_ge(ew_dve.semaphore, ew_dve.at(j, "exponents"))
                    act.activation(EP, D_T, ACT.Exp, scale=-DECAY)
                    act.activation(EN, D_T, ACT.Exp, scale=DECAY)
                    act.activation(SF[:, j % 2:j % 2 + 1], SF[:, 2 + j % 2:3 + j % 2], ACT.Exp, scale=-DECAY)
                    act.activation(EX, EX, ACT.Exp, scale=-DECAY).then_inc(ew_act.semaphore, 1)

            def inverse(j):
                if j:
                    act.wait_ge(po_pe.semaphore, po_pe.at(j - 1, "turned"))
                act.activation(TI.rearrange("p q (w n) -> p (q w) n", w=2), IDENT[:, None, :].to_broadcast([P, 8, P]),
                               ACT.Copy).then_inc(in_act.semaphore, 1)
                act.wait_ge(in_pe.semaphore, in_pe.at(j, "matrices"))
                act.activation(TOK, PS[:, 4, SEQ:2 * SEQ], ACT.Copy)
                act.activation(RBS[:, 0:4], PS[:, 5, SEQ:SEQ + 4], ACT.Copy).then_inc(in_act.semaphore, 1)
                for l, c in levels:
                    if c == 0 and l in (2, 4) and j + 1 < NJ:
                        factors(j + 1, l // 2 - 1)
                    act.wait_ge(in_pe.semaphore, in_pe.at(j, "nt%d%d" % (l, c)))
                    act.activation(NTS[:, c, :], PS[:, 4 + c, 0:SEQ], ACT.Copy).then_inc(in_act.semaphore, 1)

            def outputs(j):
                for c in range(2):
                    act.wait_ge(po_pe.semaphore, po_pe.at(j, "r%d" % c))
                    act.activation(RS[:, 0:P], PS[:, 2, 0:P], ACT.Copy).then_inc(po_act.semaphore, 1)
                    act.wait_ge(po_pe.semaphore, po_pe.at(j, "u%d" % c))
                    act.activation(U_S[:, 0:P], PS[:, 3, 0:P], ACT.Copy).then_inc(po_act.semaphore, 1)
                act.wait_ge(po_dve.semaphore, po_dve.at(j, "variance"))
                act.activation(RVR[:, 4:8], RVR[:, 0:4], ACT.Sqrt, scale=1.0 / HD, bias=EPSILON[:, 1:2]).then_inc(po_act.semaphore, 1)
                act.wait_ge(po_dve.semaphore, po_dve.at(j, "output"))
                act.activation(MH[:, j, :], FO, ACT.Copy).then_inc(po_act.semaphore, 1)

            factors(0, 0)
            factors(0, 1)
            for j in range(NJ):
                inverse(j)
                outputs(j)
            for i in range(4):
                turn_hi(act, n0 + 12 + i)
            post_squares(act, s, n0 + 16)
            post_std(act, s)

        def rwkv_dve(dve, order, s, n0, op, col, post_col):
            pre_rstd(dve, s)
            mixer_norm_dve(dve, s, 1, col)
            dve.wait_ge(hn_ready, KT * 2)
            order.after(dve.tensor_tensor(XX[:, :, 1:SEQ], HN[:, :, 0:SEQ - 1], HN[:, :, 1:SEQ], ALU.subtract))
            order.after(dve.tensor_scalar(XX[:, :, 0:1], HN[:, :, 0:1], -1.0, None, ALU.mult))

            def mix(i, mu, out):
                for k in range(KT):
                    c = COL["mu%d" % mu] + k
                    dve.scalar_tensor_tensor(out[:, k, :], XX[:, k, :], VEC[:, c:c + 1], HN[:, k, :], ALU.mult,
                                             ALU.add).then_inc(rk_x, 1)

            def lo(i, x, hi, out):
                for k in range(KT):
                    dve.wait_ge(xh_ready, KT * (op + i) + k + 1)
                    dve.tensor_tensor(out[:, k, :], x[:, k, :], hi[:, k, :].bitcast(F32), ALU.subtract).then_inc(xl_ready, 1)

            mix(0, 0, XI[0])
            lo(0, XI[0], XH, XL)
            mix(1, 2, XI[1])
            lo(1, XI[1], MH, ML)
            turn_lo(dve, n0)
            dve.wait_ge(xl_ready, KT * (op + 1))
            mix(2, 1, XI[0])
            turn_lo(dve, n0 + 1)
            dve.wait_ge(xl_ready, KT * (op + 2))
            mix(3, 4, XI[1])
            turn_lo(dve, n0 + 2)
            mix(4, 3, SQ)
            for i in range(3, 5):
                turn_lo(dve, n0 + i)
            lo(2, SQ, XH, XL)
            for i in range(5, 8):
                turn_lo(dve, n0 + i)
            dve.wait_ge(rk_mid, 1)
            mix(5, 5, XI[0])
            for i in range(8, 12):
                turn_lo(dve, n0 + i)
            c = COL["l1_k_a"]
            order.after(dve.tensor_scalar(OMK, VEC[:, c:c + KT], -1.0, 1.0, ALU.mult, ALU.add))
            dve.wait_ge(rk_mid_taken, 3)
            order.after(dve.memset(ST, 0.0))
            dve.wait_ge(rk_n2, 1)
            dve.tensor_scalar(RN, PS[:, 7, 0:32], 1e-12, None, ALU.max).then_inc(rk_n2max, 1)
            dve.wait_ge(rk_n2root, 1)
            dve.reciprocal(RN, RN).then_inc(rk_n2done, 1)
            dve.wait_ge(masks_made, MASKS_MADE)

            def factors(j, part):
                if part == 0:
                    dve.wait_ge(ew_act.semaphore, ew_act.at(j, "sigmoid"))
                    order.after(dve.tensor_tensor_scan(C_T, CARRY[:], S_T, 0.0, ALU.mult, ALU.add))
                    c3 = C_T.rearrange("p (c t) -> p c t", c=2)
                    d3 = D_T.rearrange("p (c t) -> p c t", c=2)
                    order.after(dve.tensor_tensor(d3, c3, c3[:, :, 63:64].to_broadcast([P, 2, P]), ALU.subtract))
                    dve.tensor_tensor(SF[:, 2 + j % 2:3 + j % 2], D_T[:, P - 1:P], C_T[:, P + 63:P + 64], ALU.add)
                    dve.tensor_tensor(EX, D_T, S_T, ALU.subtract).then_inc(ew_dve.semaphore, 1)
                if part == 1:
                    dve.wait_ge(ew_pe.semaphore, ew_pe.at(j, "norm"))
                    c = COL["l1_k_k"] + j
                    dve.scalar_tensor_tensor(KKN, KF[:, j, :], VEC[:, c:c + 1], PS[:, 7, 0:SEQ], ALU.mult, ALU.mult).then_inc(ew_dve.semaphore, 1)
                if part == 2:
                    c = COL["l1_k_a"] + j
                    dve.wait_ge(ew_dve.semaphore, ew_dve.at(j, "kk"))
                    order.after(dve.tensor_tensor(BETA[j % 2], KKN, A_T, ALU.mult))
                    order.after(dve.tensor_scalar(A_T, A_T, VEC[:, c:c + 1], OMK[:, j:j + 1], ALU.mult, ALU.add))
                    order.after(dve.tensor_tensor(KF[:, j, :], KF[:, j, :], A_T, ALU.mult))
                if part == 3:
                    kr, t3 = KR[j % 2], lambda x: x.rearrange("p (c t) -> p c t", c=2)
                    c = COL["l1_r_k"] + j
                    dve.wait_ge(ew_act.semaphore, ew_act.at(j, "exp"))
                    dve.scalar_tensor_tensor(kr[:, :, 0, :], t3(KKN), -1.0, t3(EX), ALU.mult, ALU.mult)
                    dve.tensor_tensor(kr[:, :, 1, :], t3(RT[:, j, :]), t3(EP), ALU.mult)
                    dve.tensor_tensor(BETA[j % 2], BETA[j % 2], EN, ALU.mult)
                    dve.tensor_tensor(KH[j % 2], KF[:, j, :], EN, ALU.mult)
                    dve.scalar_tensor_tensor(RK[j % 2], RT[:, j, :], VEC[:, c:c + 1], KF[:, j, :], ALU.mult, ALU.mult).then_inc(ew_dve.semaphore, 1)

            def inverse(j):
                dve.wait_ge(in_pe.semaphore, in_pe.at(j, "matrices"))
                for q in range(4):
                    last = dve.tensor_tensor(G4[:, q, :].rearrange("p (w n) -> p w n", w=2), PS[:, q, :].rearrange("p (w n) -> p w n", w=2),
                                             MASK2[:, None, :].to_broadcast([P, 2, 2 * P]), ALU.mult)
                last.then_inc(in_dve.semaphore, 1)
                dve.wait_ge(in_act.semaphore, in_act.at(j, "tokens"))
                for hh in range(2):
                    mask = LMASK[:, 0, 0:1, :].bitcast(mybir.dt.uint16).to_broadcast([P, 2, P])
                    dve.copy_predicated(TI.rearrange("p (c h) n -> p h c n", h=2)[:, hh, :, 0:P], mask,
                                        PS[:, 4 + hh, 0:SEQ].rearrange("p (c n) -> p c n", c=2))
                mask = LMASK[:, 0, 1:2, :].bitcast(mybir.dt.uint16).to_broadcast([P, 4, P])
                dve.copy_predicated(TI[:, :, P:2 * P], mask, PS[:, 0:4, 0:P]).then_inc(in_dve.semaphore, 1)
                for l, c in levels:
                    if c == 0 and l in (2, 3, 4, 5) and j + 1 < NJ:
                        factors(j + 1, l - 2)
                    dve.wait_ge(in_pe.semaphore, in_pe.at(j, "tnt%d%d" % (l, c)))
                    mask = LMASK[:, l:l + 1, :, :].rearrange("p l w n -> p l (w n)").bitcast(mybir.dt.uint16).to_broadcast([P, 2, 2 * P])
                    dve.copy_predicated(TI[:, 2 * c:2 * c + 2, :], mask, PS[:, c, :].rearrange("p (h n) -> p h n", h=2)).then_inc(in_dve.semaphore, 1)

            def outputs(j):
                dve.wait_ge(po_pe.semaphore, po_pe.at(j, "state"))
                for hh in range(2):
                    a = slice(HD * hh, HD * hh + HD)
                    last = dve.tensor_scalar(ST[a, a], PS[a, 1, 0:HD], SF[a, j % 2:j % 2 + 1], None, ALU.mult)
                last.then_inc(po_dve.semaphore, 1)
                h4 = lambda x: x.rearrange("p (h n) -> p h n", h=4)
                wide = lambda x: x.unsqueeze(2).to_broadcast([P, 4, HD])
                dve.wait_ge(po_pe.semaphore, po_pe.at(j, "y1"))
                order.after(dve.reduce_sum(RMN[:, 0:4], h4(PS[:, 0, 0:SEQ]), AX_X))
                order.after(dve.tensor_scalar(RMN[:, 0:4], RMN[:, 0:4], 1.0 / HD, None, ALU.mult))
                order.after(dve.tensor_tensor(h4(Y_C), h4(PS[:, 0, 0:SEQ]), wide(RMN[:, 0:4]), ALU.subtract))
                order.after(dve.tensor_tensor(YQ, Y_C, Y_C, ALU.mult))
                dve.reduce_sum(RVR[:, 0:4], h4(YQ), AX_X).then_inc(po_dve.semaphore, 1)
                dve.wait_ge(in_act.semaphore, in_act.at(j, "tokens"))
                v = V0[:, :, P * j:P * (j + 1)].rearrange("p c (h n) -> p c h n", h=2)
                bs = RBS[:, 0:4].rearrange("p (c h) -> p c h", c=2).unsqueeze(3).to_broadcast([P, 2, 2, HD])
                dve.tensor_tensor(BV.rearrange("p (c h n) -> p c h n", c=2, h=2), v, bs, ALU.mult)
                dve.wait_ge(po_act.semaphore, po_act.at(j, "std"))
                order.after(dve.reciprocal(RMN[:, 4:8], RVR[:, 4:8]))
                dve.tensor_tensor(h4(Y_C), h4(Y_C), wide(RMN[:, 4:8]), ALU.mult).then_inc(po_dve.semaphore, 1)
                dve.wait_ge(po_pe.semaphore, po_pe.at(j, "turned"))
                g, b = COL["l1_lnx_g"] + j, COL["l1_lnx_b"] + j
                order.after(dve.tensor_scalar(FO, PS[:, 2, 0:SEQ], VEC[:, g:g + 1], VEC[:, b:b + 1], ALU.mult, ALU.add))
                order.after(dve.tensor_tensor(FO, FO, PS[:, 2, SEQ:2 * SEQ], ALU.add))
                dve.tensor_tensor(FO, FO, PS[:, 3, 0:SEQ], ALU.mult).then_inc(po_dve.semaphore, 1)
                dve.wait_ge(po_act.semaphore, po_act.at(j, "hi"))
                dve.tensor_tensor(ML[:, j, :], FO, MH[:, j, :].bitcast(F32), ALU.subtract).then_inc(po_dve.semaphore, 1)

            for part in range(4):
                factors(0, part)
            for j in range(NJ):
                inverse(j)
                outputs(j)
            for i in range(4):
                turn_lo(dve, n0 + 12 + i)
            post_add(dve, order, s, post_col)

        def rwkv_pe(pe, s, n0, op):
            pre_mean(pe, s)

            def small(name, m):
                return SMALLW[:, SMALL[name][0]:SMALL[name][0] + KT * m].rearrange("p (k n) -> p k n", k=KT)

            def lora(i, name, m, x, bank):
                w = small(name, m)
                for k in range(KT):
                    pe.wait_ge(rk_x, KT * i + k + 1)
                    last = pe.matmul(PS[0:m, bank, 0:SEQ], w[:, k, :], x[:, k, :], start=k == 0, stop=k == KT - 1)
                last.then_inc(rk_mid, 1)

            for i in range(12):
                if i == 8:
                    lora(2, "dec1", 64, XI[0], 6)
                    lora(3, "a1", 64, XI[1], 7)
                if i >= 2:
                    pe.wait_ge(rk_taken, i - 1)
                if i < 8:
                    column_products(pe, n0 + i, BANK[i % 2], op=op + i // 4 if i % 4 == 0 else None, x=((XH, XL), (MH, ML))[i // 4])
                else:
                    pe.wait_ge(xl_ready, KT * (op + 3))
                    pe.wait_ge(lo_ready, n0 + i + 1)
                    out = [BANK[i % 2][:, SEQ * t:SEQ * (t + 1)] for t in range(TT)]
                    token_products(pe, n0 + i, out, (0, COLS)).then_inc(products_done, 1)
            pe.wait_ge(rk_mid_taken, 1)
            lora(5, "g1", 128, XI[0], 6)
            pe.wait_ge(rk_mid_taken, 2)
            pe.wait_ge(rk_ksq, 1)
            for c in range(2):
                for j in range(NJ):
                    last = pe.matmul(PS[:, 7, 16 * c + 2 * j:16 * c + 2 * j + 2], XI[1][:, j, P * c:P * (c + 1)], HSEL[:],
                                     start=True, stop=True)
            last.then_inc(rk_n2, 1)
            pe.wait_ge(rk_mid_taken, 3)
            pe.wait_ge(rk_taken, 12)
            pe.wait_ge(x_ready, KT * (s + 1))
            pe.wait_ge(rk_n2done, 1)

            def factors(j):
                if j:
                    pe.wait_ge(ew_act.semaphore, ew_act.at(j - 1, "sigmoid"))
                    pe.wait_ge(ew_dve.semaphore, ew_dve.at(j - 1, "kk"))
                c = slice(P * j, P * (j + 1))
                a2, w2 = (SMALLW[0:64, SMALL[x][0]:SMALL[x][0] + D][:, c] for x in ("a2", "dec2"))
                pe.matmul(PS[:, 6, 0:SEQ], a2, AM, start=True, stop=True)
                pe.matmul(PS[:, 6, SEQ:2 * SEQ], w2, WM, start=True, stop=True).then_inc(ew_pe.semaphore, 1)
                for c in range(2):
                    for hh in range(2):
                        rn = RN[:, 16 * c + 2 * j + hh:16 * c + 2 * j + hh + 1].to_broadcast([P, HD])
                        last = pe.matmul(PS[HD * hh:HD * hh + HD, 7, P * c:P * (c + 1)], rn, IDENT[:], start=True, stop=True)
                last.then_inc(ew_pe.semaphore, 1)

            def inverse(j):
                kr, beta, kh, rk = KR[j % 2], BETA[j % 2], KH[j % 2], RK[j % 2]
                pe.wait_ge(ew_dve.semaphore, ew_dve.at(j, "factors"))
                if j:
                    pe.wait_ge(po_dve.semaphore, po_dve.at(j - 1, "output"))
                    pe.wait_ge(in_act.semaphore, in_act.at(j - 1, "nt%d%d" % levels[-1]))
                for q in range(4):
                    a, c = slice(HD * (q % 2), HD * (q % 2) + HD), q // 2
                    t = slice(P * c, P * (c + 1))
                    both = kr[a, c, :, :].rearrange("p w t -> p (w t)")
                    pe.matmul(PS[:, q, 0:2 * P], beta[a, t], both, start=True, stop=True)
                    pe.matmul(PS[:, q, 2 * P:4 * P], kh[a, t], both, start=True, stop=True)
                    pe.matmul(PS[:, 4 + q % 2, t], kr[a, c, 0, :], beta[a, t], start=True, stop=True)
                pe.transpose(PS[:, 4, 2 * P:3 * P], beta[:, 0:P], IDENT[:])
                pe.transpose(PS[:, 4, 3 * P:4 * P], kh[:, 0:P], IDENT[:])
                for c in range(2):
                    last = pe.matmul(PS[:, 5, SEQ + 2 * c:SEQ + 2 * c + 2], rk[:, P * c:P * (c + 1)], HSEL[:], start=True, stop=True)
                last.then_inc(in_pe.semaphore, 1)
                if j + 1 < NJ:
                    factors(j + 1)
                for l in range(1, TOPS):
                    for c in range(2):
                        if l == 1:
                            pe.wait_ge(in_dve.semaphore, in_dve.at(j, "first"))
                            pe.wait_ge(in_act.semaphore, in_act.at(j, "tokens"))
                        else:
                            pe.wait_ge(in_dve.semaphore, in_dve.at(j, "t%d%d" % (l - 1, c)))
                        for hh in range(2):
                            q = 2 * c + hh
                            last = pe.matmul(PS[:, 4 + c, P * hh:P * (hh + 1)], G4[:, q, 0:P], TI[:, q, 0:P], start=True, stop=True)
                        last.then_inc(in_pe.semaphore, 1)
                    for c in range(2):
                        pe.wait_ge(in_act.semaphore, in_act.at(j, "nt%d%d" % (l, c)))
                        for hh in range(2):
                            q, nt = 2 * c + hh, NTS[:, c, P * hh:P * (hh + 1)]
                            pe.matmul(PS[:, c, 2 * P * hh:2 * P * hh + P], TI[:, q, P:2 * P], nt, start=True, stop=True)
                            last = pe.matmul(PS[:, c, 2 * P * hh + P:2 * P * (hh + 1)], nt, TI[:, q, P:2 * P], start=True, stop=True)
                        last.then_inc(in_pe.semaphore, 1)

            def outputs(j):
                kr = KR[j % 2]
                pe.wait_ge(in_dve.semaphore, in_dve.at(j, "t%d1" % (TOPS - 1)))
                for c in range(2):
                    if c:
                        pe.wait_ge(po_dve.semaphore, po_dve.at(j, "state"))
                        pe.matmul(PS[:, 2, 0:P], kr[:, c, 0, :], ST, start=True, stop=False, skip_group_check=True)
                    for hh in range(2):
                        q, a = 2 * c + hh, slice(HD * hh, HD * hh + HD)
                        v = V0[:, c, P * j + HD * hh:P * j + HD * hh + HD]
                        last = pe.matmul(PS[:, 2, a], G4[:, q, 2 * P:3 * P], v, start=not c, stop=True, skip_group_check=True)
                    last.then_inc(po_pe.semaphore, 1)
                    pe.wait_ge(po_act.semaphore, po_act.at(j, "r%d" % c))
                    for hh in range(2):
                        q, a = 2 * c + hh, slice(HD * hh, HD * hh + HD)
                        last = pe.matmul(PS[:, 3, a], TI[:, q, P:2 * P], RS[:, a], start=True, stop=True)
                    last.then_inc(po_pe.semaphore, 1)
                    pe.wait_ge(po_act.semaphore, po_act.at(j, "u%d" % c))
                    if c:
                        pe.matmul(PS[:, 0, P:2 * P], kr[:, c, 1, :], ST, start=True, stop=False, skip_group_check=True)
                    for hh in range(2):
                        q, a = 2 * c + hh, slice(HD * hh, HD * hh + HD)
                        v = V0[:, c, P * j + HD * hh:P * j + HD * hh + HD]
                        out = PS[:, 0, P * c + HD * hh:P * c + HD * hh + HD]
                        pe.matmul(out, G4[:, q, P:2 * P], U_S[:, a], start=not c, stop=False, skip_group_check=True)
                        last = pe.matmul(out, G4[:, q, 3 * P:4 * P], v, start=False, stop=True, skip_group_check=True)
                    last.then_inc(po_pe.semaphore, 1)
                    if c == 0:
                        for hh in range(2):
                            a = slice(HD * hh, HD * hh + HD)
                            v = V0[:, 0, P * j + HD * hh:P * j + HD * hh + HD]
                            pe.matmul(PS[a, 1, 0:64], TOK[:, a], U_S[:, a], start=True, stop=False)
                            last = pe.matmul(PS[a, 1, 0:64], TOK[:, P + HD * hh:P + HD * hh + HD], v, start=False, stop=True)
                        last.then_inc(po_pe.semaphore, 1)
                pe.wait_ge(po_dve.semaphore, po_dve.at(j, "normed"))
                for c in range(2):
                    pe.transpose(PS[:, 2, P * c:P * (c + 1)], Y_C[:, P * c:P * (c + 1)], IDENT[:])
                    pe.transpose(PS[:, 2, SEQ + P * c:SEQ + P * (c + 1)], BV[:, P * c:P * (c + 1)], IDENT[:])
                g2 = SMALLW[:, SMALL["g2"][0]:SMALL["g2"][0] + D][:, P * j:P * (j + 1)]
                pe.matmul(PS[:, 3, 0:SEQ], g2, GM, start=True, stop=True).then_inc(po_pe.semaphore, 1)

            factors(0)
            for j in range(NJ):
                inverse(j)
                outputs(j)
            pe.wait_ge(po_dve.semaphore, po_dve.at(NJ - 1, "output"))
            open_outputs(pe, s)
            for i in range(4):
                pe.wait_ge(po_dve.semaphore, po_dve.at(2 * i + 1, "lo"))
                row_products(pe, n0 + 12 + i, MH[:, 2 * i:2 * i + 2, :], ML[:, 2 * i:2 * i + 2, :], end=s if i == 3 else None)

        F_UNITS = [(j, qt, hh) for j in range(8) for qt in range(TT) for hh in range(2)]
        FQ = SCR[:, 2048:4096].rearrange("p (j t) -> p j t", j=8)
        FK = SCR[:, 4096:6144].rearrange("p (j t) -> p j t", j=8)
        FV = SCR[:, 6144:8192].rearrange("p (t c) -> p t c", t=2)
        FS = SCR[:, 8192:8704].rearrange("p (b s) -> p b s", b=2)
        FP = SCR[:, 8704:9216].rearrange("p (b s) -> p b s", b=2)
        FPT = SCR[:, 9216:9728].rearrange("p (b s) -> p b s", b=2)
        FST = SCR[:, 9728:9736].rearrange("p (b s) -> p b s", b=2)
        F_Z, F_L, F_ONES, F_NEGC = (SCR[0:16, 9736 + SEQ * i:9736 + SEQ * (i + 1)] for i in range(4))
        CAUSAL = sb("causal_mask", [P, 2 * P], BF16)
        fox_taken = sem("fox_bank_taken")
        forget_ready, forget_abs, forget_ln, forget_done = (sem("fox_forget_" + x) for x in ("ready", "abs", "ln", "done"))
        fs_ready, fs_taken, fm_ready, fe_ready, fp_ready = (sem("fox_" + x) for x in ("scores", "scores_taken", "max", "exp", "probs"))
        fpt_ready, fpt_taken, fo_ready, foh_ready, fol_ready = (sem("fox_" + x) for x in ("pt", "pt_taken", "out", "out_hi", "out_lo"))

        def fox_pool(pool):
            pool.memset(CAUSAL[:], 0.0).then_inc(pool_order, 1)
            pool.wait_ge(pool_order, 11)
            pool.affine_select(out=CAUSAL[:, P:2 * P], in_=CAUSAL[:, P:2 * P], compare_op=ALU.is_ge, fill=-1e30, base=0,
                               pattern=[[-1, P]], channel_multiplier=1).then_inc(consts_made, 1)

        def fox_act(act, order, s, n0, op, col):
            pre_squares(act, s)
            pre_std(act, s)
            mixer_operand_act(act, 2, op)
            act.wait_ge(forget_abs, 1)
            order.after(act.activation(F_L, F_L, ACT.Exp, scale=-1.0))
            act.activation(F_L, F_L, ACT.Ln, bias=F_ONES[:, 0:1]).then_inc(forget_ln, 1)
            for i in range(12):
                turn_hi(act, n0 + i)
                act.wait_ge(products_done, n0 + i + 1)
                bank = two(BANK[i % 2])
                if i < 4:
                    last = act.activation(FQ[:, 2 * i:2 * i + 2, :], bank, ACT.Copy, scale=HD ** -0.5)
                elif i < 8:
                    last = act.activation(FK[:, 2 * i - 8:2 * i - 6, :], bank, ACT.Copy)
                else:
                    last = act.activation(FV[:, :, 256 * (i - 8):256 * (i - 7)], bank, ACT.Copy)
                last.then_inc(fox_taken, 1)

            def exps(u):
                nk = P * (F_UNITS[u][1] + 1)
                act.wait_ge(fm_ready, u + 1)
                if u >= 2:
                    act.wait_ge(fpt_ready, u - 1)
                act.activation(FP[:, u % 2, 0:nk], FS[:, u % 2, 0:nk], ACT.Exp, bias=FST[:, u % 2, 1:2],
                               accum_out=FST[:, u % 2, 2:3]).then_inc(fe_ready, 1)

            def take_pt(u):
                nk = P * (F_UNITS[u][1] + 1)
                act.wait_ge(fpt_ready, u + 1)
                if u >= 2:
                    act.wait_ge(fo_ready, u - 1)
                act.activation(FPT[:, u % 2, 0:nk], PS[:, 2 + u % 2, 0:nk], ACT.Copy).then_inc(fpt_taken, 1)

            def out_hi(j):
                act.wait_ge(fo_ready, 4 * j + 4)
                act.activation(MH[:, j, :], PS[:, 6 + j % 2, 0:SEQ], ACT.Copy).then_inc(foh_ready, 1)

            for u in range(32):
                exps(u)
                if u:
                    take_pt(u - 1)
                if u % 4 == 1 and u > 4:
                    out_hi(u // 4 - 1)
            take_pt(31)
            out_hi(7)
            for i in range(4):
                turn_hi(act, n0 + 12 + i)
            post_squares(act, s, n0 + 16)
            post_std(act, s)

        def fox_dve(dve, order, s, n0, op, col, post_col):
            pre_rstd(dve, s)
            mixer_norm_dve(dve, s, 2, col, op)
            order.after(dve.memset(F_ONES, 1.0))
            dve.wait_ge(forget_ready, 1)
            order.after(dve.tensor_scalar(F_Z, PS[0:16, 7, 0:SEQ], SMALLW[0:16, SMALL["b_f"][0]:SMALL["b_f"][0] + 1], None, ALU.add))
            dve.scalar_tensor_tensor(F_L, F_Z, -1.0, F_Z, ALU.mult, ALU.max).then_inc(forget_abs, 1)
            dve.wait_ge(forget_ln, 1)
            order.after(dve.scalar_tensor_tensor(F_Z, F_Z, 0.0, F_L, ALU.min, ALU.subtract))
            order.after(dve.tensor_tensor_scan(F_NEGC, F_ONES, F_Z, 0.0, ALU.mult, ALU.add))
            dve.tensor_scalar(F_NEGC, F_NEGC, -1.0, None, ALU.mult).then_inc(forget_done, 1)
            for i in range(12):
                turn_lo(dve, n0 + i)

            def mask(u):
                nk = P * (F_UNITS[u][1] + 1)
                dve.wait_ge(fs_ready, u + 1)
                if u >= 2:
                    dve.wait_ge(fe_ready, u - 1)
                dve.tensor_tensor_reduce(out=FS[:, u % 2, 0:nk], in0=PS[:, u % 2, 0:nk], in1=CAUSAL[:, 2 * P - nk:2 * P],
                                         scale=1.0, scalar=-3e38, op0=ALU.add, op1=ALU.max,
                                         accum_out=FST[:, u % 2, 0:1]).then_inc(fs_taken, 1)
                dve.wait_ge(fs_taken, u + 1)
                dve.tensor_scalar(FST[:, u % 2, 1:2], FST[:, u % 2, 0:1], -1.0, None, ALU.mult).then_inc(fm_ready, 1)

            def normalize(u):
                nk = P * (F_UNITS[u][1] + 1)
                dve.wait_ge(fe_ready, u + 1)
                order.after(dve.reciprocal(FST[:, u % 2, 3:4], FST[:, u % 2, 2:3]))
                dve.tensor_scalar(FP[:, u % 2, 0:nk], FP[:, u % 2, 0:nk], FST[:, u % 2, 3:4], None, ALU.mult).then_inc(fp_ready, 1)

            def out_lo(j):
                dve.wait_ge(foh_ready, j + 1)
                dve.tensor_tensor(ML[:, j, :], PS[:, 6 + j % 2, 0:SEQ], MH[:, j, :].bitcast(F32), ALU.subtract).then_inc(fol_ready, 1)

            mask(0)
            mask(1)
            for u in range(32):
                normalize(u)
                if u + 2 < 32:
                    mask(u + 2)
                if u % 4 == 1 and u > 4:
                    out_lo(u // 4 - 1)
            out_lo(7)
            for i in range(4):
                turn_lo(dve, n0 + 12 + i)
            post_add(dve, order, s, post_col)

        def fox_pe(pe, s, n0, op):
            pre_mean(pe, s)
            f_cols = SMALLW[:, SMALL["f"][0]:SMALL["f"][0] + KT * 16].rearrange("p (k n) -> p k n", k=KT)
            for k in range(KT):
                pe.wait_ge(hn_ready, KT * 2 + k + 1)
                last = pe.matmul(PS[0:16, 7, 0:SEQ], f_cols[:, k, :], HN[:, k, :], start=k == 0, stop=k == KT - 1)
            last.then_inc(forget_ready, 1)
            opening_products(pe, n0, op)
            for i in range(2, 12):
                if i >= 2:
                    pe.wait_ge(fox_taken, i - 1)
                if i < 8:
                    column_products(pe, n0 + i, BANK[i % 2])
                else:
                    pe.wait_ge(lo_ready, n0 + i + 1)
                    out = [BANK[i % 2][:, SEQ * t:SEQ * (t + 1)] for t in range(TT)]
                    token_products(pe, n0 + i, out, (0, COLS)).then_inc(products_done, 1)
            pe.wait_ge(fox_taken, 12)
            pe.wait_ge(forget_done, 1)
            pe.wait_ge(x_ready, KT * (s + 1))

            def scores(u):
                j, qt, hh = F_UNITS[u]
                nk, a, h = P * (qt + 1), HD * hh, 2 * j + hh
                if u >= 2:
                    pe.wait_ge(fs_taken, u - 1)
                out = PS[:, u % 2, 0:nk]
                pe.matmul(out, FQ[a:a + HD, j, qt * P:(qt + 1) * P], FK[a:a + HD, j, 0:nk], start=True, stop=False)
                pe.matmul(out, IDENT[0:16, h:h + 1].to_broadcast([16, P]), F_NEGC[:, 0:nk], start=False, stop=True).then_inc(fs_ready, 1)

            def transposes(u):
                qt = F_UNITS[u][1]
                pe.wait_ge(fp_ready, u + 1)
                if u >= 2:
                    pe.wait_ge(fpt_taken, u - 1)
                for b in range(qt + 1):
                    last = pe.transpose(PS[:, 2 + u % 2, b * P:(b + 1) * P], FP[:, u % 2, b * P:(b + 1) * P], IDENT[:])
                last.then_inc(fpt_ready, 1)

            def values(u):
                j, qt, hh = F_UNITS[u]
                h = 2 * j + hh
                pe.wait_ge(fpt_taken, u + 1)
                if u % 4 == 0 and j >= 2:
                    pe.wait_ge(fol_ready, j - 1)
                out = PS[HD * hh:HD * hh + HD, 6 + j % 2, qt * P:(qt + 1) * P]
                for b in range(qt + 1):
                    last = pe.matmul(out, FV[:, b, HD * h:HD * h + HD], FPT[:, u % 2, P * b:P * (b + 1)], start=b == 0, stop=b == qt)
                last.then_inc(fo_ready, 1)

            scores(0)
            scores(1)
            for u in range(32):
                if u + 2 < 32:
                    scores(u + 2)
                transposes(u)
                if u:
                    values(u - 1)
            values(31)
            pe.wait_ge(fs_taken, 32)
            pe.wait_ge(fpt_taken, 32)
            open_outputs(pe, s)
            for i in range(4):
                pe.wait_ge(fol_ready, 2 * i + 2)
                row_products(pe, n0 + 12 + i, MH[:, 2 * i:2 * i + 2, :], ML[:, 2 * i:2 * i + 2, :], end=s if i == 3 else None)

        LEVELS = [0] + [1 << i for i in range(8)]
        GH = D // P
        WB = [SCR[:, 2048 * i:2048 * (i + 1)] for i in range(2)]
        GQ, GK, GB, GV = (SCR[:, 4096 + 2048 * i:6144 + 2048 * i] for i in range(4))
        FREE = SMALL["dec1"][0]
        GA = SMALLW[:, FREE:FREE + 2048]
        GX = SMALLW[:, FREE + 2048:FREE + 3072]
        GR = SMALLW[:, FREE + 4224:FREE + 4240]
        LB = SMALLW[:, FREE + 4240:FREE + 4304].rearrange("p (a k) -> p a k", a=8)
        G_SILU = SQ[:].rearrange("p k t -> p (k t)")
        gh = lambda ap: ap.rearrange("p (h t) -> p h t", h=GH)
        hgrn_taken = sem("hgrn_bank_taken")
        lb_sub, lb_exp, keys_ready, ln_ready = (sem("hgrn_" + x) for x in ("bound_sub", "bound_exp", "keys", "ln"))
        we_ready, wx_ready, w_ready, ws_ready, ws_taken = (sem("hgrn_" + x) for x in ("exponents", "exp", "w", "level", "level_taken"))
        gx_taken, go_ready, gsq_ready, gms_ready, gstd_ready = (sem("hgrn_" + x) for x in ("cross_taken", "out", "squares", "mean", "std"))
        grs_ready, grb_ready, grb_taken, gn_ready, gnh_ready, gnl_ready = (
            sem("hgrn_" + x) for x in ("rstd", "rstd_wide", "rstd_taken", "normed", "normed_hi", "normed_lo"))

        def hgrn_act(act, order, s, n0, op, col):
            pre_squares(act, s)
            pre_std(act, s)
            mixer_operand_act(act, 3, op)
            act.wait_ge(lb_sub, 1)
            act.activation(LB[:, 0:3, :], LB[:, 0:3, :], ACT.Exp).then_inc(lb_exp, 1)

            def take(i):
                turn_hi(act, n0 + i)
                act.wait_ge(products_done, n0 + i + 1)
                bank, c = BANK[i % 2], 512 * (i % 4)
                if i < 4:
                    last = act.activation(GK[:, c:c + 512], bank, ACT.Sigmoid)
                elif i < 8:
                    last = act.activation(GQ[:, c:c + 512], bank, ACT.Copy)
                elif i < 12:
                    last = act.activation(GV.rearrange("p (t c) -> p t c", t=2)[:, :, 256 * (i - 8):256 * (i - 7)], two(bank), ACT.Copy)
                else:
                    last = act.activation(G_SILU[:, c:c + 512], bank, ACT.Silu)
                last.then_inc(hgrn_taken, 1)

            for i in range(8):
                take(i)
                if i == 4:
                    act.wait_ge(keys_ready, 4)
                    act.activation(WB[1], GB, ACT.Ln).then_inc(ln_ready, 1)
            for l in range(1, 9):
                act.wait_ge(we_ready, l)
                if l < 8:
                    act.activation(WB[l % 2], WB[l % 2], ACT.Exp).then_inc(wx_ready, 1)
                else:
                    w = gh(WB[0])
                    act.activation(w[:, :, 0:P], w[:, :, 0:P], ACT.Exp)
                    act.activation(w[:, :, P:2 * P], gh(GB)[:, :, P:2 * P], ACT.Exp).then_inc(wx_ready, 1)
                take(7 + l)
            act.wait_ge(ws_ready, 9)
            act.activation(GX, PS[:, 0:2, :].rearrange("p b t -> p (b t)"), ACT.Copy).then_inc(gx_taken, 1)
            for b in range(4):
                act.wait_ge(go_ready, b + 1)
                act.activation(WB[0][:, 512 * b:512 * (b + 1)], PS[:, 4 + b, :], ACT.Square).then_inc(gsq_ready, 1)
            act.wait_ge(gms_ready, 1)
            act.activation(GR, PS[:, 0, 0:16], ACT.Sqrt, bias=EPSILON[:, 0:1], scale=float(D // P)).then_inc(gstd_ready, 1)
            for b in range(4):
                act.wait_ge(grb_ready, b + 1)
                act.activation(WB[1][:, 512 * b:512 * (b + 1)], PS[:, b, :], ACT.Copy).then_inc(grb_taken, 1)
            for b in range(4):
                act.wait_ge(gn_ready, b + 1)
                act.activation(MH[:, 2 * b:2 * b + 2, :], two(WB[0][:, 512 * b:512 * (b + 1)]), ACT.Copy).then_inc(gnh_ready, 1)
            for i in range(4):
                turn_hi(act, n0 + 16 + i)
            post_squares(act, s, n0 + 20)
            post_std(act, s)

        def hgrn_dve(dve, order, s, n0, op, col, post_col):
            pre_rstd(dve, s)
            mixer_norm_dve(dve, s, 3, col, op)
            dve.wait_ge(x_ready, KT * (s + 1))
            c = COL["lb0"]
            order.after(dve.tensor_tensor(LB[:, 3, :], VEC[:, c:c + KT], VEC[:, c + KT:c + 2 * KT], ALU.max))
            order.after(dve.tensor_tensor(LB[:, 3, :], LB[:, 3, :], VEC[:, c + 2 * KT:c + 3 * KT], ALU.max))
            for i in range(3):
                last = dve.tensor_tensor(LB[:, i, :], VEC[:, c + i * KT:c + (i + 1) * KT], LB[:, 3, :], ALU.subtract)
            last.then_inc(lb_sub, 1)
            dve.wait_ge(lb_exp, 1)
            order.after(dve.tensor_tensor(LB[:, 4, :], LB[:, 0, :], LB[:, 1, :], ALU.add))
            order.after(dve.tensor_tensor(LB[:, 5, :], LB[:, 4, :], LB[:, 2, :], ALU.add))
            order.after(dve.reciprocal(LB[:, 5, :], LB[:, 5, :]))
            order.after(dve.tensor_tensor(LB[:, 6, :], LB[:, 4, :], LB[:, 5, :], ALU.mult))
            order.after(dve.tensor_scalar(LB[:, 7, :], LB[:, 6, :], -1.0, 1.0, ALU.mult, ALU.add))
            for i in range(4):
                turn_lo(dve, n0 + i)
                dve.wait_ge(hgrn_taken, i + 1)
                for h in (2 * i, 2 * i + 1):
                    a = slice(SEQ * h, SEQ * (h + 1))
                    order.after(dve.tensor_scalar(GB[:, a], GK[:, a], LB[:, 7, h:h + 1], LB[:, 6, h:h + 1], ALU.mult, ALU.add))
                    last = dve.tensor_scalar(GK[:, a], GB[:, a], -1.0, 1.0, ALU.mult, ALU.add)
                last.then_inc(keys_ready, 1)
            turn_lo(dve, n0 + 4)
            dve.wait_ge(ln_ready, 1)
            dve.wait_ge(masks_made, MASKS_MADE)
            for h in range(GH):
                a = slice(SEQ * h, SEQ * (h + 1))
                last = dve.tensor_tensor_scan(GB[:, a], CARRY[:], WB[1][:, a], 0.0, ALU.mult, ALU.add)
            order.after(last)

            def exponents(l):
                m = LEVELS[l]
                if l >= 3:
                    dve.wait_ge(ws_ready, l - 1)
                w = WB[l % 2].rearrange("p (b h x) -> p b h x", h=2, x=m)
                b = GB.rearrange("p (b h x) -> p b h x", h=2, x=m)
                edge = b[:, :, 0, m - 1:m].to_broadcast([P, SEQ * GH // (2 * m), m])
                if l < 8:
                    dve.tensor_tensor(w[:, :, 1, :], b[:, :, 1, :], edge, ALU.subtract)
                dve.tensor_tensor(w[:, :, 0, :], edge, b[:, :, 0, :], ALU.subtract).then_inc(we_ready, 1)

            def factors(l):
                m = LEVELS[l]
                dve.wait_ge(wx_ready, l)
                w, q, k = (x.rearrange("p (b h x) -> p b h x", h=2, x=m) for x in (WB[l % 2], GQ, GK))
                dve.tensor_tensor(w[:, :, 1, :], w[:, :, 1, :], q[:, :, 1, :], ALU.mult)
                dve.tensor_tensor(w[:, :, 0, :], w[:, :, 0, :], k[:, :, 0, :], ALU.mult).then_inc(w_ready, 1)

            def pick(l):
                dve.wait_ge(ws_ready, l + 1)
                for b in range(4):
                    a = GA[:, 512 * b:512 * (b + 1)].rearrange("p (u t) -> p u t", u=4)
                    p = PS[:, b, :].rearrange("p (u t) -> p u t", u=4)
                    if l == 0:
                        last = dve.tensor_tensor(a, p, IDENT[:, None, :].to_broadcast([P, 4, P]), ALU.mult)
                    else:
                        mask = LMASK[:, l - 1, 1:2, :].bitcast(mybir.dt.uint16).to_broadcast([P, 4, P])
                        last = dve.copy_predicated(a, mask, p)
                last.then_inc(ws_taken, 1)
                dve.wait_ge(ws_taken, l + 1)

            exponents(1)
            for i in range(5, 8):
                turn_lo(dve, n0 + i)
            for l in range(1, 9):
                if l < 8:
                    exponents(l + 1)
                if l == 1:
                    dve.wait_ge(hgrn_taken, 8)
                factors(l)
                turn_lo(dve, n0 + 7 + l)
                pick(l - 1)
            for b in range(4):
                dve.wait_ge(gx_taken, 1)
            dve.wait_ge(gstd_ready, 1)
            dve.reciprocal(GR, GR).then_inc(grs_ready, 1)
            for b in range(4):
                dve.wait_ge(grb_taken, b + 1)
                a = slice(512 * b, 512 * (b + 1))
                order.after(dve.scalar_tensor_tensor(WB[0][:, a], PS[:, 4 + b, :], VEC[:, GNORM_COL:GNORM_COL + 1], WB[1][:, a],
                                                     ALU.mult, ALU.mult))
                dve.tensor_tensor(WB[0][:, a], WB[0][:, a], G_SILU[:, a], ALU.mult).then_inc(gn_ready, 1)
                dve.wait_ge(gnh_ready, b + 1)
                dve.tensor_tensor(ML[:, 2 * b:2 * b + 2, :], two(WB[0][:, a]), MH[:, 2 * b:2 * b + 2, :].bitcast(F32),
                                  ALU.subtract).then_inc(gnl_ready, 1)
            for i in range(4):
                turn_lo(dve, n0 + 16 + i)
            post_add(dve, order, s, post_col)

        def hgrn_pe(pe, s, n0, op):
            pre_mean(pe, s)

            def project(i):
                if i >= 2:
                    pe.wait_ge(hgrn_taken, i - 1)
                if i < 8 or i >= 12:
                    column_products(pe, n0 + i, BANK[i % 2])
                else:
                    pe.wait_ge(lo_ready, n0 + i + 1)
                    out = [BANK[i % 2][:, SEQ * t:SEQ * (t + 1)] for t in range(TT)]
                    token_products(pe, n0 + i, out, (0, COLS)).then_inc(products_done, 1)

            def level(l):
                if l:
                    pe.wait_ge(w_ready, l)
                    pe.wait_ge(ws_taken, l)
                keys, queries = (gh(GK), gh(GQ)) if l == 0 else (gh(WB[l % 2]),) * 2
                if l == 8:
                    for h in range(GH):
                        last = pe.matmul(PS[:, h // 4, P * (h % 4):P * (h % 4 + 1)], keys[:, h, 0:P], queries[:, h, P:2 * P],
                                         start=True, stop=True)
                else:
                    for u in range(2 * GH):
                        h, t = u // 2, slice(P * (u % 2), P * (u % 2 + 1))
                        last = pe.matmul(PS[:, u // 4, P * (u % 4):P * (u % 4 + 1)], keys[:, h, t], queries[:, h, t],
                                         start=True, stop=True)
                last.then_inc(ws_ready, 1)

            opening_products(pe, n0, op)
            for i in range(2, 8):
                project(i)
            pe.wait_ge(hgrn_taken, 8)
            pe.wait_ge(keys_ready, 4)
            pe.wait_ge(x_ready, KT * (s + 1))
            level(0)
            for l in range(1, 9):
                project(7 + l)
                level(l)
            pe.wait_ge(hgrn_taken, 16)
            pe.wait_ge(gx_taken, 1)
            v = GV.rearrange("p (t h c) -> p t h c", t=2, h=GH)
            for h in range(GH):
                out = PS[:, 4 + h // 2, SEQ * (h % 2):SEQ * (h % 2 + 1)]
                pe.matmul(out[:, 0:P], v[:, 0, h, :], GA[:, SEQ * h:SEQ * h + P], start=True, stop=True)
                pe.matmul(out[:, P:2 * P], v[:, 1, h, :], GA[:, SEQ * h + P:SEQ * (h + 1)], start=True, stop=False)
                last = pe.matmul(out[:, P:2 * P], v[:, 0, h, :], GX[:, P * h:P * (h + 1)], start=False, stop=True)
                if h % 2:
                    last.then_inc(go_ready, 1)
            sq = gh(WB[0])
            for u in range(2 * GH):
                h, t = u // 2, slice(P * (u % 2), P * (u % 2 + 1))
                if u % 4 == 0:
                    pe.wait_ge(gsq_ready, u // 4 + 1)
                last = pe.matmul(PS[:, 0, u:u + 1], sq[:, h, t], MEAN[:, 0:1], start=True, stop=True)
            last.then_inc(gms_ready, 1)
            pe.wait_ge(grs_ready, 1)
            for u in range(2 * GH):
                last = pe.matmul(PS[:, u // 4, P * (u % 4):P * (u % 4 + 1)], GR[:, u:u + 1].to_broadcast([P, P]), IDENT[:],
                                 start=True, stop=True)
                if u % 4 == 3:
                    last.then_inc(grb_ready, 1)
            pe.wait_ge(grb_taken, 4)
            open_outputs(pe, s)
            for i in range(4):
                pe.wait_ge(gnl_ready, i + 1)
                row_products(pe, n0 + 16 + i, MH[:, 2 * i:2 * i + 2, :], ML[:, 2 * i:2 * i + 2, :], end=s if i == 3 else None)

        plan, n, op = [], 0, 0
        for s, (kind, slabs, operands) in enumerate(SUBLAYERS[:STOP]):
            plan.append((kind, s, n, op))
            n, op = n + slabs, op + operands
        ffns = ["l0_ffn1", "l0_ffn2", "l1_ffn1", "l1_ffn2", "gain02", "gain12"]
        ffn_cols = [(COL[f + "_pre_g"], COL[f + "_post_g"]) if "ffn" in f else (COL[f], COL[f] + KT) for f in ffns]
        f_of = {s: f for f, s in enumerate([0, 2, 3, 5, 7, 9])}

        ffn_operand = {s: (op, ffn_cols[f_of[s]][0]) for kind, s, n, op in plan if kind == "ffn"}
        sublayer_of = {op: s for kind, s, n, op in plan}

        block = ctx.enter_context(nc.Block())

        @block.sync
        def _(sp):
            for n in range(RING):
                sp.dma_start(RAW[:, n, :], slabs_dram[n, :, :]).then_inc(raw_loaded[n], 16)
            with sp.Fori(0, n_slabs // RING - 1) as i:
                for u in range(RING):
                    sp.wait_ge(lo_ready, i * RING + u + 1)
                    sp.dma_start(RAW[:, u, :], slabs_dram[bass.ds(i * RING + RING + u, 1), :, :]
                                 .rearrange("n p c -> p (n c)")).then_inc(raw_loaded[u], 16)
            for n in range(n_slabs - n_slabs % RING, n_slabs):
                sp.wait_ge(lo_ready, n - RING + 1)
                sp.dma_start(RAW[:, n % RING, :], slabs_dram[n, :, :]).then_inc(raw_loaded[n % RING], 16)
            sp.wait_ge(x_ready, KT * (len(plan) + 1))
            sp.dma_start(yT_dram.rearrange("(k p) t -> p k t", p=P), X[:]).then_inc(stored, 16)
            sp.wait_ge(stored, 16)

        @block.gpsimd
        def _(pool):
            pool.memset(MEAN[:], 1.0 / D)
            pool.memset(ZERO[:], 0.0)
            pool.memset(IDENT[:], 0.0).then_inc(pool_order, 1)
            pool.wait_ge(pool_order, 1)
            pool.affine_select(out=IDENT[:], in_=IDENT[:], compare_op=ALU.not_equal, fill=1.0, base=0,
                               pattern=[[-1, P]], channel_multiplier=1).then_inc(consts_made, 1)
            pool.memset(LMASK[:], 1.0)
            pool.memset(CARRY[:], 1.0).then_inc(masks_made, 1)
            pool.wait_ge(masks_made, 1)
            pool.memset(CARRY[:, 0:129:128], 0.0)
            for step in range(3):
                for l in range(7):
                    for side in range(2):
                        m, row, last = 1 << l, m_off(l, side), P // (2 << l)
                        view = LMASK[:, l, side, :].rearrange("p (b h x) -> p b h x", h=2, x=m)
                        base, pattern, mult = [
                            (-row, [[-2 * m, last], [0, 2], [0, m]], 1),
                            (row + m - 1, [[2 * m, last], [0, 2], [0, m]], -1),
                            ((0, -1)[side], [[0, last], [(-1, 1)[side], 2], [0, m]], 0)][step]
                        pool.affine_select(out=view, in_=view, compare_op=ALU.is_ge, fill=0.0, base=base, pattern=pattern,
                                           channel_multiplier=mult).then_inc(masks_made, 1)
                pool.wait_ge(masks_made, 1 + 14 * (step + 1))
            nsa_pool(pool)
            fox_pool(pool)
            rwkv_pool(pool)

        @block.scalar
        def _(act):
            act.dma_start(X[:], xT_dram.rearrange("(k p) t -> p k t", p=P)).then_inc(consts_loaded, 16)
            act.dma_start(VEC[:], vec_dram).then_inc(consts_loaded, 16)
            for n in range(AHEAD):
                split_hi(act, n)
            act.dma_start(SMALLW[:], small_dram).then_inc(small_loaded, 16)
            order = Order(act, act_order)
            for kind, s, n, op in plan:
                if kind == "ffn":
                    f = f_of[s]
                    ffn_act(act, s, f, n, op, ffn_cols[f][0])
                if kind == "nsa":
                    nsa_act(act, order, s, n, op, COL["l0_mix_pre_g"])
                if kind == "rwkv":
                    rwkv_act(act, order, s, n, op, COL["l1_mix_pre_g"])
                if kind == "fox":
                    fox_act(act, order, s, n, op, COL["gain00"])
                if kind == "hgrn":
                    hgrn_act(act, order, s, n, op, COL["gain10"])

        @block.vector
        def _(dve):
            order = Order(dve, dve_order)
            dve.memset(EPSILON[:, 0:1], EPS)
            dve.memset(EPSILON[:, 1:2], LNX_EPS)
            order.after(dve.memset(HSEL[:], 0.0))
            dve.memset(HSEL[0:64, 0:1], 1.0)
            dve.memset(HSEL[64:P, 1:2], 1.0)
            dve.wait_ge(consts_loaded, 32)
            dve.memset(RSTD[:, 0:1], 0.0).then_inc(x_ready, KT)
            for n in range(AHEAD):
                split_lo(dve, n)
            for f in range(4):
                c = ffn_cols[f][1]
                order.after(dve.tensor_scalar(VEC[:, c:c + KT], VEC[:, c:c + KT], 0.5, None, ALU.mult))
            for kind, s, n, op in plan:
                if kind == "ffn":
                    f = f_of[s]
                    ffn_dve(dve, order, s, f, n, op, *ffn_cols[f])
                if kind == "nsa":
                    nsa_dve(dve, order, s, n, op, COL["l0_mix_pre_g"], COL["l0_mix_post_g"])
                if kind == "rwkv":
                    rwkv_dve(dve, order, s, n, op, COL["l1_mix_pre_g"], COL["l1_mix_post_g"])
                if kind == "fox":
                    fox_dve(dve, order, s, n, op, COL["gain00"], COL["gain01"])
                if kind == "hgrn":
                    hgrn_dve(dve, order, s, n, op, COL["gain10"], COL["gain11"])

        @block.tensor
        def _(pe):
            pe.wait_ge(consts_made, 1)
            for kind, s, n, op in plan:
                if kind == "ffn":
                    ffn_pe(pe, s, f_of[s], n, op)
                if kind == "nsa":
                    nsa_pe(pe, s, n, op)
                if kind == "rwkv":
                    rwkv_pe(pe, s, n, op)
                if kind == "fox":
                    fox_pe(pe, s, n, op)
                if kind == "hgrn":
                    hgrn_pe(pe, s, n, op)


def kernel(**inputs):
    import numpy as np
    import concourse.bacc as bacc
    from concourse.bass_utils import run_bass_kernel_spmd

    a = {name: np.asarray(value) for name, value in inputs.items()}
    slabs = []

    def columns(w):
        for c in range(0, w.shape[1], COLS):
            slabs.append(w[:, c:c + COLS].reshape(KT, P, COLS).transpose(1, 0, 2).reshape(P, SLAB))

    def row_blocks(w):
        for r in range(0, w.shape[0], 2 * P):
            slabs.append(w[r:r + 2 * P].reshape(2, P, D).transpose(1, 0, 2).reshape(P, SLAB))

    def ffn(gate, up, down):
        for j in range(STEPS + 1):
            if j < STEPS:
                columns(gate[:, COLS * j:COLS * (j + 1)])
                columns(up[:, COLS * j:COLS * (j + 1)])
            if j:
                row_blocks(down[COLS * (j - 1):COLS * j])

    def named_ffn(name):
        ffn(a[name + "_w_gate"], a[name + "_w_up"], a[name + "_w_down"])

    named_ffn("l0_ffn1")
    w = a["l0_w_in"]
    columns(w[:, 0:512])
    columns(w[:, 536:792])
    columns(w[:, 792:1048])
    columns(w[:, 1048:1304])
    for kv in "kv":
        slabs.append(a["l0_cmp_w1_" + kv].reshape(16, P, P).transpose(1, 0, 2).reshape(P, SLAB))
    for c in range(0, 512, COLS):
        for part in (1816, 2328, 1304):
            columns(w[:, part + c:part + c + COLS])
    row_blocks(a["l0_w_out"])
    named_ffn("l0_ffn2")
    named_ffn("l1_ffn1")
    for name in "rkv":
        columns(a["l1_w_" + name])
    row_blocks(a["l1_w_o"])
    named_ffn("l1_ffn2")
    w = a["fox_w_in_2"][0]
    columns(w[:, 0:3 * D])
    row_blocks(a["fox_w_out_2"][0])
    w_in, w_out = a["ffn_w_in_2"], a["ffn_w_out_2"]
    ffn(w_in[0][:, :D_FF], w_in[0][:, D_FF:], w_out[0])
    w = a["hgrn_w_in_2"][0]
    columns(w[:, D:2 * D])
    columns(w[:, 0:D])
    columns(w[:, 2 * D:4 * D])
    row_blocks(a["hgrn_w_out_2"][0])
    ffn(w_in[1][:, :D_FF], w_in[1][:, D_FF:], w_out[1])
    n_slabs = sum(x[1] for x in SUBLAYERS[:STOP])
    slabs = np.stack(slabs[:n_slabs])

    def vector(name):
        if name.startswith("gain"):
            return a["norm_gains_2"][int(name[4]), int(name[5])]
        if name.startswith("mu"):
            return a["l1_mu"][int(name[2])]
        if name.startswith("lb"):
            return a["hgrn_lb_table_2"][int(name[2])]
        return a[name]

    cols = [vector(name).reshape(KT, P).T for name in COL]
    cols.append(a["l0_conv_w"].reshape(12, P).T)
    cols.append(a["l0_conv_b"].reshape(4, P).T)
    for kv in "kv":
        cols.append(np.repeat(a["l0_cmp_pe_" + kv].reshape(16, P).T, 2, axis=1))
    cols.append(a["hgrn_gnorm_2"].reshape(P, 1))
    vec = np.ascontiguousarray(np.concatenate(cols, axis=1))

    small = np.zeros((P, SMALL_COLS), np.float32)

    def put(name, w):
        c, n = SMALL[name]
        small[:w.shape[0], c:c + n] = w

    def tiled(w):
        return w.reshape(KT, P, -1).transpose(1, 0, 2).reshape(P, -1)

    put("g", tiled(a["l0_w_in"][:, 512:536]))
    put("f", tiled(a["fox_w_in_2"][0][:, 3 * D:]))
    put("w2_k", a["l0_cmp_w2_k"])
    put("w2_v", a["l0_cmp_w2_v"])
    put("dec1", tiled(a["l1_w_dec1"]))
    put("a1", tiled(a["l1_w_a1"]))
    put("g1", tiled(a["l1_w_g1"]))
    put("dec2", a["l1_w_dec2"])
    put("a2", a["l1_w_a2"])
    put("g2", a["l1_w_g2"])
    put("b_f", a["fox_b_f_2"].reshape(16, 1))

    nc = bacc.Bacc("TRN2", target_bir_lowering=False, num_devices=1)
    arrays = {"xT": np.ascontiguousarray(a["x"][0].T), "slabs": slabs, "vectors": vec, "small": small}
    args = [nc.dram_tensor("in_" + name, v.shape, F32, kind="ExternalInput").ap() for name, v in arrays.items()]
    args.append(nc.dram_tensor("out_yT", (D, SEQ), F32, kind="ExternalOutput").ap())
    build(nc, *args, n_slabs)
    result = run_bass_kernel_spmd(nc, [{"in_" + name: v for name, v in arrays.items()}], core_ids=[0])
    return np.ascontiguousarray(result.results[0]["out_yT"].T)[None]
```

```python
from contextlib import ExitStack

import concourse.bass as bass
from concourse import mybir

F32 = mybir.dt.float32
F32R = mybir.dt.float32r
BF16 = mybir.dt.bfloat16
ALU = mybir.AluOpType
ACT = mybir.ActivationFunctionType
AX_X = mybir.AxisListType.X

P = 128
SEQ = 256
D = 1024
KT = D // P
TT = SEQ // P
D_FF = 2816
SLAB = 2048
COLS = SLAB // KT
RING = 3
AHEAD = RING - 1
STEPS = D_FF // COLS
EPS = 1e-6
LNX_EPS = 64e-5
BIG = 1e32
N_CONSTS = 5
MASKS_MADE = 43
SUBLAYERS = [("ffn", 3 * STEPS, 1), ("nsa", 17, 3), ("ffn", 3 * STEPS, 1), ("ffn", 3 * STEPS, 1), ("rwkv", 16, 3),
             ("ffn", 3 * STEPS, 1), ("fox", 16, 1), ("ffn", 3 * STEPS, 1), ("hgrn", 20, 1), ("ffn", 3 * STEPS, 1)]


def vector_names():
    names = []
    for ffn in ("l0_ffn1", "l0_ffn2", "l1_ffn1", "l1_ffn2"):
        names += [ffn + "_pre_g", ffn + "_post_g"]
    for layer in ("l0", "l1"):
        names += [layer + "_mix_pre_g", layer + "_mix_post_g"]
    names += ["mu%d" % i for i in range(6)]
    names += ["l1_w0", "l1_a0", "l1_k_k", "l1_k_a", "l1_r_k", "l1_lnx_g", "l1_lnx_b"]
    names += ["gain%d%d" % (layer, i) for layer in range(2) for i in range(4)]
    names += ["lb%d" % i for i in range(3)]
    return names


COL = {name: KT * i for i, name in enumerate(vector_names())}
N_VEC = KT * len(COL)
CONV_COL = N_VEC
PE_COL = CONV_COL + 16
GNORM_COL = PE_COL + 64
VEC_COLS = GNORM_COL + 1

SMALL, SMALL_COLS = {}, 0
for _name, _cols in (("f", KT * 16), ("b_f", 1), ("g", KT * 24), ("w2_k", 64), ("w2_v", 64), ("dec1", KT * 64),
                     ("a1", KT * 64), ("g1", KT * 128), ("dec2", D), ("a2", D), ("g2", D)):
    SMALL[_name] = (SMALL_COLS, _cols)
    SMALL_COLS += _cols


def build(nc, xT_dram, slabs_dram, vec_dram, small_dram, yT_dram, n_slabs):
    ctx = ExitStack()
    with ctx:
        def sb(name, shape, dt=F32):
            return ctx.enter_context(nc.sbuf_tensor(name, shape, dt))

        def sem(name):
            return ctx.enter_context(nc.semaphore(name))

        X = sb("residual", [P, KT, SEQ])
        RAW = sb("slab_raw", [P, RING, SLAB])
        HI = sb("slab_hi", [P, RING, SLAB], F32R)
        LO = sb("slab_lo", [P, RING, SLAB], F32R)
        XH = sb("operand_hi", [P, KT, SEQ], F32R)
        XL = sb("operand_lo", [P, KT, SEQ], F32R)
        MH = sb("mixed_hi", [P, KT, SEQ], F32R)
        ML = sb("mixed_lo", [P, KT, SEQ], F32R)
        SQ = sb("squares", [P, KT, SEQ])
        NS = sb("norm_scratch", [P, 5 * SEQ])
        RSTD, RSTD_POST, STD = (NS[:, SEQ * i:SEQ * (i + 1)] for i in range(3))
        EPSILON = sb("epsilons", [P, 2])
        TABLE = sb("table_preloads", [P, 40])
        VEC = sb("vectors", [P, VEC_COLS])
        SMALLW = sb("small_weights", [P, SMALL_COLS])
        MEAN = sb("mean_matrix", [P, P])
        ZERO = sb("zeros", [P, 512], BF16)
        IDENT = sb("identity", [P, P])
        LMASK = sb("level_masks", [P, 7, 2, P], BF16)
        CARRY = sb("carry", [P, SEQ])
        SCR = sb("stage_scratch", [P, 13100])
        PS = ctx.enter_context(nc.psum_tensor("psum", [P, 8, 512], F32))
        ACC = PS[:, 0:4, :].rearrange("p b (h t) -> p (b h) t", h=2)
        NORMED = SCR[:, 0:1024].rearrange("p (k t) -> p k t", k=4)
        GATE, UP = PS[:, 4, :], PS[:, 5, :]
        MS_PRE, MS_POST = PS[:, 6, 0:SEQ], PS[:, 7, 0:SEQ]

        raw_loaded = [sem("raw_loaded%d" % i) for i in range(RING)]
        hi_ready = sem("hi_ready")
        lo_ready = sem("lo_ready")
        products_done = sem("products_done")
        consts_loaded = sem("consts_loaded")
        consts_made = sem("consts_made")
        x_ready = sem("x_ready")
        outputs_done = sem("outputs_done")
        small_loaded = sem("small_loaded")
        sq_ready = sem("squares_pre_ready")
        ms_ready = sem("mean_pre_ready")
        rstd_ready = sem("rstd_pre_ready")
        xh_ready = sem("operand_hi_ready")
        xl_ready = sem("operand_lo_ready")
        ysq_ready = sem("squares_post_ready")
        yms_ready = sem("mean_post_ready")
        std_ready, ystd_ready = sem("std_pre_ready"), sem("std_post_ready")
        dve_order = sem("vector_order")
        act_order = sem("scalar_order")
        gate_taken, up_taken = sem("gate_taken"), sem("up_taken")
        silu_ready = sem("silu_ready")
        hidden_ready = sem("hidden_ready")
        hh_ready, hl_ready = sem("hidden_hi_ready"), sem("hidden_lo_ready")
        stored = sem("stored")
        pool_order = sem("gpsimd_order")
        masks_made = sem("masks_made")

        def m_off(l, side):
            return (1 << l) if side == 0 else 0

        def slab(ring, n):
            return ring[:, n % RING, :].rearrange("p (k n) -> p k n", k=KT)

        def rows(ring, n):
            return ring[:, n % RING, :].rearrange("p (k n) -> p k n", k=2)

        class Order:
            def __init__(self, engine, semaphore):
                self.engine, self.semaphore, self.n = engine, semaphore, 0

            def after(self, instruction):
                self.n += 1
                instruction.then_inc(self.semaphore, 1)
                self.engine.wait_ge(self.semaphore, self.n)

        def split_hi(act, n, i=0):
            act.wait_ge(raw_loaded[n % RING], (i + n // RING) * 16 + 16)
            if n >= RING:
                act.wait_ge(products_done, i * RING + n - RING + 1)
            act.activation(HI[:, n % RING, :], RAW[:, n % RING, :], ACT.Copy).then_inc(hi_ready, 1)

        def split_lo(dve, n, i=0):
            dve.wait_ge(hi_ready, i * RING + n + 1)
            dve.tensor_tensor(LO[:, n % RING, :], RAW[:, n % RING, :], HI[:, n % RING, :].bitcast(F32),
                              ALU.subtract).then_inc(lo_ready, 1)

        def turn_hi(act, n, i=0):
            if n + AHEAD < n_slabs:
                split_hi(act, n + AHEAD, i)

        def turn_lo(dve, n, i=0):
            if n + AHEAD < n_slabs:
                split_lo(dve, n + AHEAD, i)

        def product(pe, out, w, x, start, stop):
            pe.matmul(out, w[0], x[0], start=start, stop=False, skip_group_check=True)
            pe.matmul(out, w[0], x[1], start=False, stop=False, skip_group_check=True)
            return pe.matmul(out, w[1], x[0], start=False, stop=stop, skip_group_check=True)

        def pre_squares(act, s):
            for b in range(4):
                act.wait_ge(x_ready, KT * s + 2 * b + 2)
                act.activation(SQ[:, 2 * b:2 * b + 2, :], X[:, 2 * b:2 * b + 2, :], ACT.Square).then_inc(sq_ready, 1)

        def pre_mean(pe, s, mixer=False):
            for k in range(KT):
                if k % 2 == 0:
                    pe.wait_ge(sq_ready, 4 * s + k // 2 + 1)
                last = pe.matmul(MS_PRE, MEAN[:], SQ[:, k, :], start=k == 0, stop=k == KT - 1)
                if mixer and k in (1, 3, 5):
                    keep_warm(pe, 3)
            last.then_inc(ms_ready, 1)
            if mixer:
                keep_warm(pe, 16)

        def pre_std(act, s):
            act.wait_ge(ms_ready, s + 1)
            act.activation(STD, MS_PRE, ACT.Sqrt, bias=EPSILON[:, 0:1]).then_inc(std_ready, 1)

        def pre_rstd(dve, s):
            dve.wait_ge(std_ready, s + 1)
            dve.reciprocal(RSTD, STD).then_inc(rstd_ready, 1)

        def preload(act, function):
            preloads[0] += 1
            act.activation(TABLE[:, preloads[0] - 1:preloads[0]], EPSILON[:, 0:1], function)

        preloads = [0]

        def post_squares(act, s, n_end):
            preload(act, ACT.Sqrt)
            for b in range(4):
                if b < 3:
                    act.wait_ge(outputs_done, 3 * s + b + 1)
                else:
                    act.wait_ge(products_done, n_end)
                act.activation(SQ[:, 2 * b:2 * b + 2, :], ACC[:, 2 * b:2 * b + 2, :], ACT.Square).then_inc(ysq_ready, 1)

        def post_mean(pe, s, b):
            pe.wait_ge(ysq_ready, 4 * s + b + 1)
            for k in (2 * b, 2 * b + 1):
                last = pe.matmul(MS_POST, MEAN[:], SQ[:, k, :], start=k == 0, stop=k == KT - 1)
            if b == 3:
                last.then_inc(yms_ready, 1)

        def post_std(act, s):
            act.wait_ge(yms_ready, s + 1)
            act.activation(STD, MS_POST, ACT.Sqrt, bias=EPSILON[:, 0:1]).then_inc(ystd_ready, 1)

        def post_add(dve, order, s, col):
            dve.wait_ge(ystd_ready, s + 1)
            order.after(dve.reciprocal(RSTD_POST, STD))
            first = order.n
            for k in range(KT + 3):
                if k < KT:
                    if k >= 4:
                        dve.wait_ge(x_ready, KT * (s + 1) + k - 3)
                    dve.scalar_tensor_tensor(NORMED[:, k % 4, :], ACC[:, k, :], VEC[:, col + k:col + k + 1],
                                             RSTD_POST, ALU.mult, ALU.mult).then_inc(dve_order, 1)
                    order.n += 1
                if 1 <= k <= KT:
                    dve.wait_ge(dve_order, first + k)
                    dve.tensor_tensor(X[:, k - 1, :], X[:, k - 1, :], NORMED[:, (k - 1) % 4, :], ALU.add).then_inc(x_ready, 1)
                if k >= 3 and s + 1 in ffn_operand:
                    ffn_lo(dve, *ffn_operand[s + 1], k - 3)

        def ffn_lo(dve, op, col, k):
            dve.wait_ge(xh_ready, KT * op + k + 1)
            dve.wait_ge(x_ready, KT * sublayer_of[op] + k + 1)
            dve.scalar_tensor_tensor(XL[:, k, :], X[:, k, :], VEC[:, col + k:col + k + 1], XH[:, k, :].bitcast(F32),
                                     ALU.mult, ALU.subtract).then_inc(xl_ready, 1)

        HH, HL = MH[:, 0:2, :], ML[:, 0:2, :]
        GS, US, SILU, HID = (SCR[:, 512 * i:512 * (i + 1)] for i in range(4))
        RSTD2 = RSTD.unsqueeze(1).to_broadcast([P, 2, SEQ])

        def two(ap):
            return ap.rearrange("p (h t) -> p h t", h=2)

        def ffn_act(act, s, f, n0, op, col):
            for k in range(KT):
                act.wait_ge(x_ready, KT * s + k + 1)
                act.activation(XH[:, k, :], X[:, k, :], ACT.Copy, scale=VEC[:, col + k:col + k + 1]).then_inc(xh_ready, 1)
            if s == 0:
                split_hi(act, 1)
            pre_squares(act, s)
            turn_hi(act, n0)
            pre_std(act, s)
            preload(act, ACT.Silu)

            def gate_turn(n, j, i=0):
                act.wait_ge(gate_taken, j + STEPS * f + 1)
                act.activation(SILU, GS, ACT.Silu).then_inc(silu_ready, 1)

            def hidden_hi(j):
                act.wait_ge(hidden_ready, j + STEPS * f + 1)
                act.activation(HH, two(HID), ACT.Copy).then_inc(hh_ready, 1)

            gate_turn(n0, 0)
            turn_hi(act, n0 + 1)
            hidden_hi(0)

            def step(n, j, i=0):
                turn_hi(act, n, i)
                gate_turn(n, j, i)
                turn_hi(act, n + 1, i)
                turn_hi(act, n + 2, i)
                act.wait_ge(products_done, i * RING + n + 3)
                hidden_hi(j)

            with act.Fori(0, STEPS - 2) as i:
                step(n0 + 2, i + 1, i)
            step(n0 + 3 * STEPS - 4, STEPS - 1)
            turn_hi(act, n0 + 3 * STEPS - 1)
            post_squares(act, s, n0 + 3 * STEPS)
            post_std(act, s)

        def ffn_dve(dve, order, s, f, n0, op, col, post_col):
            if s == 0:
                for k in range(KT):
                    ffn_lo(dve, op, col, k)
                split_lo(dve, 1)
                for g in range(4):
                    c = ffn_cols[g][1]
                    order.after(dve.tensor_scalar(VEC[:, c:c + KT], VEC[:, c:c + KT], 0.5, None, ALU.mult))
            turn_lo(dve, n0)
            pre_rstd(dve, s)

            def gate_turn(n, j, i=0):
                dve.wait_ge(products_done, i * RING + n + 1)
                dve.wait_ge(rstd_ready, s + 1)
                dve.tensor_tensor(two(GS), two(GATE), RSTD2, ALU.mult).then_inc(gate_taken, 1)

            def up_turn(n, j, i=0):
                turn_lo(dve, n, i)
                dve.wait_ge(products_done, i * RING + n + 1)
                dve.tensor_tensor(two(US), two(UP), RSTD2, ALU.mult).then_inc(up_taken, 1)
                dve.wait_ge(up_taken, j + STEPS * f + 1)
                dve.wait_ge(silu_ready, j + STEPS * f + 1)
                dve.tensor_tensor(HID, US, SILU, ALU.mult).then_inc(hidden_ready, 1)

            def hidden_lo(j):
                dve.wait_ge(hh_ready, j + STEPS * f + 1)
                dve.tensor_tensor(HL, two(HID), HH.bitcast(F32), ALU.subtract).then_inc(hl_ready, 1)

            gate_turn(n0, 0)
            up_turn(n0 + 1, 0)
            hidden_lo(0)

            def step(n, j, i=0):
                turn_lo(dve, n, i)
                gate_turn(n, j, i)
                up_turn(n + 1, j, i)
                turn_lo(dve, n + 2, i)
                hidden_lo(j)

            with dve.Fori(0, STEPS - 2) as i:
                step(n0 + 2, i + 1, i)
            step(n0 + 3 * STEPS - 4, STEPS - 1)
            turn_lo(dve, n0 + 3 * STEPS - 1)
            post_add(dve, order, s, post_col)

        def open_outputs(pe, s):
            for b in range(4):
                if b == 0 and s:
                    pe.wait_ge(x_ready, KT * (s + 1))
                pe.matmul(PS[:, b, :], ZERO[:, 0:P], ZERO[:], start=True, stop=False, skip_group_check=True)

        def keep_warm(pe, n):
            for _ in range(n):
                pe.matmul(GATE, ZERO[:, 0:P], ZERO[:], start=True, stop=True, skip_group_check=True)

        def row_products(pe, n, xh, xl, i=0, end=None, tiles=range(KT)):
            pe.wait_ge(lo_ready, i * RING + n + 1)
            for m in tiles:
                for k in range(2):
                    w = [rows(r, n)[:, k, m * P:(m + 1) * P] for r in (HI, LO)]
                    last = product(pe, ACC[:, m, :], w, (xh[:, k, :], xl[:, k, :]), False, end is not None and k == 1)
                if m == KT - 1:
                    last.then_inc(products_done, 1)
                elif end is not None and m % 2:
                    last.then_inc(outputs_done, 1)
                if end is not None and m in (3, 5, 7):
                    post_mean(pe, end, (m - 3) // 2)
            if end is not None:
                post_mean(pe, end, 3)
                if end + 1 < len(plan):
                    keep_warm(pe, 24 if end + 1 in ffn_operand else 20)

        def opening_products(pe, n, op, mean_of=None):
            pe.wait_ge(lo_ready, n + 2)
            for k in range(KT):
                if k == KT - 1 and mean_of is not None:
                    pre_mean(pe, mean_of)
                pe.wait_ge(xl_ready, KT * op + k + 1)
                for u, bank in enumerate((GATE, UP)):
                    for m in range(2):
                        w = [slab(r, n + u)[:, k, m * P:(m + 1) * P] for r in (HI, LO)]
                        last = product(pe, bank[:, m * SEQ:(m + 1) * SEQ], w, (XH[:, k, :], XL[:, k, :]),
                                       k == 0 and m == 0, k == KT - 1)
                    if k == KT - 1:
                        last.then_inc(products_done, 1)

        def column_products(pe, n, bank, i=0, op=None, x=(XH, XL), tiles=(0, 1)):
            pe.wait_ge(lo_ready, i * RING + n + 1)
            for m in tiles:
                for k in range(KT):
                    if op is not None and m == 0:
                        pe.wait_ge(xl_ready, KT * op + k + 1)
                    w = [slab(r, n)[:, k, m * P:(m + 1) * P] for r in (HI, LO)]
                    last = product(pe, bank[:, m * SEQ:(m + 1) * SEQ], w, (x[0][:, k, :], x[1][:, k, :]), k == 0, k == KT - 1)
            if 1 in tiles:
                last.then_inc(products_done, 1)

        def ffn_pe(pe, s, f, n0, op):
            if s:
                opening_products(pe, n0, op, s)
            else:
                column_products(pe, n0, GATE, op=op)
                pre_mean(pe, s)
                column_products(pe, n0 + 1, UP)
            open_outputs(pe, s)
            with pe.Fori(0, STEPS - 1) as i:
                pe.wait_ge(gate_taken, i + STEPS * f + 1)
                column_products(pe, n0 + 2, GATE, i)
                pe.wait_ge(up_taken, i + STEPS * f + 1)
                column_products(pe, n0 + 3, UP, i)
                pe.wait_ge(hl_ready, i + STEPS * f + 1)
                row_products(pe, n0 + 4, HH, HL, i)
            pe.wait_ge(hl_ready, STEPS * (f + 1))
            row_products(pe, n0 + 3 * STEPS - 1, HH, HL, end=s)

        N_H, N_G, HD, N_CMP = 8, 2, 64, 16
        UNITS = [(j, qt, hh) for j in range(4) for qt in range(TT) for hh in range(2)]
        HN = SCR[:, 0:2048].rearrange("p (k t) -> p k t", k=KT)
        QT = SCR[:, 2048:3072].rearrange("p (j t) -> p j t", j=4)
        KTB = SCR[:, 3072:4096].rearrange("p (b g t) -> p b g t", b=2, g=2)
        VB = SCR[:, 4096:4608].rearrange("p (b t c) -> p b t c", b=2, t=2)
        KV2 = SCR[:, 4608:5696].rearrange("p (v g t) -> p v g t", v=2, g=2)
        KV3H, KV3L = (m[:].rearrange("p k t -> p (k t)")[:, 0:1632].rearrange("p (v g t) -> p v g t", v=2, g=3) for m in (MH, ML))
        POSITION = VEC[:, PE_COL:PE_COL + 64].rearrange("p (v n) -> p v n", v=2)
        GELU = SCR[:, 5696:5760].rearrange("p (v n) -> p v n", v=2)
        HB = SCR[:, 5760:5764]
        KC2 = SCR[:, 5764:5796]
        VC = SCR[:, 5796:5924]
        GATES = SCR[:, 5924:5972]
        DIST = SCR[:, 5972:6516].rearrange("p (q s) -> p q s", q=2)
        SB = SCR[:, 6516:7572].rearrange("p (b s) -> p b s", b=2)
        PB = SCR[:, 7572:8628].rearrange("p (b s) -> p b s", b=2)
        MX = SCR[:, 8628:8636].rearrange("p (b s) -> p b s", b=2)
        NM = SCR[:, 8636:8644].rearrange("p (b s) -> p b s", b=2)
        SM = SCR[:, 8644:8652].rearrange("p (b s) -> p b s", b=2)
        RC = SCR[:, 8652:8660].rearrange("p (b s) -> p b s", b=2)
        PTS = SCR[:, 8660:9940].rearrange("p (b s) -> p b s", b=2)
        CC, CU, CB = (SCR[:, 9940 + 512 * i:9940 + 512 * (i + 1)] for i in range(3))
        Z = SCR[:, 11476:11992].rearrange("p (m t) -> p m t", m=2)
        YC = SCR[:, 11992:12504].rearrange("p (m t) -> p m t", m=2)
        DISTI = SCR[:, 12504:13048].bitcast(mybir.dt.int32)
        OUT = PS[:, 6, :].rearrange("p (j t) -> p j t", j=2)
        BANK = [PS[:, 4, :], PS[:, 5, :]]
        nsa_taken = sem("nsa_bank_taken")
        hn_ready = sem("normed_ready")
        gates_ready, gates_taken = sem("nsa_gates_ready"), sem("nsa_gates_taken")
        cmp_ready, cmp_taken = sem("nsa_compressed_ready"), sem("nsa_compressed_taken")
        scores_ready, biased = sem("nsa_scores_ready"), sem("nsa_scores_biased")
        nm_ready, exp_ready, prob_ready = sem("nsa_max_ready"), sem("nsa_exp_ready"), sem("nsa_probs_ready")
        pt_ready, pt_taken_a, pt_taken_d = sem("nsa_pt_ready"), sem("nsa_pt_taken_a"), sem("nsa_pt_taken_d")
        o_ready, oh_ready, ol_ready = sem("nsa_out_ready"), sem("nsa_out_hi_ready"), sem("nsa_out_lo_ready")
        conv_in, conv_out, convh_ready, convl_ready = (sem("conv_" + x) for x in ("in", "out", "hi", "lo"))

        def mixer_operand_act(act, mixer, op):
            for k in range(KT):
                act.wait_ge(hn_ready, KT * mixer + k + 1)
                act.activation(XH[:, k, :], HN[:, k, :], ACT.Copy).then_inc(xh_ready, 1)

        def mixer_norm_dve(dve, s, mixer, col, op=None):
            dve.wait_ge(rstd_ready, s + 1)
            for k in range(KT + 2):
                if k < KT:
                    dve.scalar_tensor_tensor(HN[:, k, :], X[:, k, :], VEC[:, col + k:col + k + 1], RSTD,
                                             ALU.mult, ALU.mult).then_inc(hn_ready, 1)
                if k >= 2 and op is not None:
                    dve.wait_ge(xh_ready, KT * op + k - 1)
                    dve.tensor_tensor(XL[:, k - 2, :], HN[:, k - 2, :], XH[:, k - 2, :].bitcast(F32),
                                      ALU.subtract).then_inc(xl_ready, 1)

        def token_products(pe, n, out, cols, x=(XH, XL)):
            for t in range(TT):
                for k in range(KT):
                    w = [slab(r, n)[:, k, cols[0]:cols[1]] for r in (HI, LO)]
                    xt = [y[:, k, t * P:(t + 1) * P] for y in x]
                    last = product(pe, out[t], xt, w, k == 0, k == KT - 1)
            return last

        def nsa_pool(pool):
            for qt in range(TT):
                for part, (a, b, base, step) in enumerate([(0, 16, qt * P - 31, -16), (16, 272, qt * P, -1)]):
                    pool.iota(DISTI[:, qt * 272 + a:qt * 272 + b], pattern=[[step, b - a]], base=base,
                              channel_multiplier=1).then_inc(pool_order, 1)
            pool.wait_ge(pool_order, 5)
            pool.tensor_copy(DIST.rearrange("p q s -> p (q s)"), DISTI).then_inc(pool_order, 1)
            pool.wait_ge(pool_order, 6)
            for qt in range(TT):
                for part, (a, b, base, step) in enumerate([(0, 16, qt * P - 31, -16), (16, 272, qt * P, -1)]):
                    d = DIST[:, qt, a:b]
                    pool.affine_select(out=d, in_=d, compare_op=ALU.is_ge, fill=BIG, base=base,
                                       pattern=[[step, b - a]], channel_multiplier=1).then_inc(pool_order, 1)
            pool.wait_ge(pool_order, 10)
            for qt in range(TT):
                pool.memset(DIST[:, qt, 15:16], BIG)
            pool.memset(KV2[:, :, :, 255:272], 0.0)
            pool.memset(Z[:, :, 0:2], 0.0).then_inc(consts_made, 1)

        def nsa_act(act, order, s, n0, op, col):
            pre_squares(act, s)
            pre_std(act, s)
            mixer_operand_act(act, 0, op)
            for m in (KV3H, KV3L):
                act.activation(m[:, :, 2, 32:272], ZERO[:, 0:480].rearrange("p (v n) -> p v n", v=2), ACT.Copy)
            act.activation(KV3H[:, :, 2, 0:32], POSITION, ACT.Copy).then_inc(xh_ready, KT)
            for i in range(2):
                turn_hi(act, n0 + i)
                act.wait_ge(products_done, n0 + i + 1)
                act.activation(QT[:, 2 * i:2 * i + 2, :], two(BANK[i % 2]), ACT.Copy, scale=HD ** -0.5).then_inc(nsa_taken, 1)
            act.wait_ge(gates_ready, 1)
            act.activation(GATES, PS[:, 7, 0:48], ACT.Sigmoid).then_inc(gates_taken, 1)
            turn_hi(act, n0 + 2)
            act.wait_ge(consts_made, N_CONSTS)
            act.wait_ge(products_done, n0 + 3)
            for v in range(2):
                for g in range(N_G):
                    src = BANK[0][HD * g:HD * g + HD, v * SEQ:(v + 1) * SEQ]
                    act.activation(KV2[0:HD, v, g, 0:SEQ], src, ACT.Copy)
                    last = act.activation(KV2[HD:P, v, g, 0:SEQ - 1], src[:, 1:SEQ], ACT.Copy)
            last.then_inc(nsa_taken, 1)
            act.wait_ge(nsa_taken, 3)
            act.activation(KV3H[:, :, 0:2, :], KV2, ACT.Copy).then_inc(xh_ready, KT)
            for b in range(2):
                turn_hi(act, n0 + 3 + b)
                act.wait_ge(products_done, n0 + 4 + b)
                bank = BANK[(3 + b) % 2]
                for g in range(N_G):
                    for half in range(2):
                        act.activation(KTB[HD * half:HD * half + HD, b, g, :], bank[HD * g:HD * g + HD, 0:SEQ], ACT.Copy)
                act.activation(VB[:, b, :, :], bank[:, SEQ:2 * SEQ].rearrange("p (t c) -> p t c", t=2), ACT.Copy).then_inc(nsa_taken, 1)
            for v in range(2):
                turn_hi(act, n0 + 5 + v)
                act.wait_ge(products_done, n0 + 6 + v)
                bank = BANK[(5 + v) % 2]
                order.after(act.activation(HB[:, 2 * v:2 * v + 2], bank[:, 32:34], ACT.Copy))
                act.activation(GELU[:, v, :], bank[:, 0:32], ACT.Gelu_apprx_tanh, bias=HB[:, 2 * v:2 * v + 1]).then_inc(nsa_taken, 1)
            act.wait_ge(cmp_ready, 1)
            act.activation(KC2, PS[:, 7, 0:32], ACT.Copy)
            act.activation(VC[0:N_CMP, :], PS[0:N_CMP, 7, 64:192], ACT.Copy).then_inc(cmp_taken, 1)

            def conv_take(i):
                act.wait_ge(products_done, n0 + 8 + i)
                if i == 3:
                    act.wait_ge(conv_out, 1)
                act.activation((CC, CU, CB)[i % 3], PS[:, 7, :], ACT.Copy).then_inc(nsa_taken, 1)

            def conv_hi(c):
                act.wait_ge(conv_out, c + 1)
                act.activation(MH[:, 4 + 2 * c:6 + 2 * c, :], two(CB), ACT.Copy).then_inc(convh_ready, 1)

            def exps(u):
                j, qt, hh = UNITS[u]
                nk = P * (qt + 1)
                act.wait_ge(nm_ready, u + 1)
                if u >= 2:
                    act.wait_ge(pt_ready, u - 1)
                for i, (a, b) in enumerate([(0, 16), (16, 16 + nk), (16 + nk, 16 + 2 * nk)]):
                    last = act.activation(PB[:, u % 2, a:b], SB[:, u % 2, a:b], ACT.Exp, bias=NM[:, u % 2, i:i + 1],
                                          accum_out=SM[:, u % 2, i:i + 1])
                last.then_inc(exp_ready, 1)

            def take_pt(u):
                j, qt, hh = UNITS[u]
                nk = P * (qt + 1)
                act.wait_ge(pt_ready, u + 1)
                if u >= 2:
                    act.wait_ge(o_ready, u - 1)
                act.activation(PTS[:, u % 2, 0:nk], PS[:, 4, 0:nk], ACT.Copy)
                act.activation(PTS[0:N_CMP, u % 2, 512:640], PS[0:N_CMP, 4, 256:384], ACT.Copy).then_inc(pt_taken_a, 1)

            def out_hi(j):
                act.wait_ge(o_ready, 4 * j + 4)
                act.activation(MH[:, j, :], OUT[:, j % 2, :], ACT.Copy).then_inc(oh_ready, 1)

            exps(0)
            for u in range(16):
                if u:
                    take_pt(u - 1)
                if u + 1 < 16:
                    exps(u + 1)
                if u % 2 == 0 and 2 <= u <= 12:
                    conv_take(u // 2 - 1)
                if u % 4 == 0 and u:
                    out_hi(u // 4 - 1)
                if u in (7, 13):
                    conv_hi(u // 8)
                if u % 2 and u <= 11:
                    turn_hi(act, n0 + 7 + u // 2)
            take_pt(15)
            out_hi(3)
            for i in range(4):
                turn_hi(act, n0 + 13 + i)
            post_squares(act, s, n0 + 17)
            post_std(act, s)

        def nsa_dve(dve, order, s, n0, op, col, post_col):
            pre_rstd(dve, s)
            mixer_norm_dve(dve, s, 0, col, op)
            for i in range(3):
                turn_lo(dve, n0 + i)
            dve.wait_ge(xh_ready, KT * (op + 2))
            dve.tensor_tensor(KV3L[:, :, 2, 0:32], POSITION, KV3H[:, :, 2, 0:32].bitcast(F32), ALU.subtract).then_inc(xl_ready, KT)
            dve.wait_ge(xh_ready, KT * (op + 3))
            dve.tensor_tensor(KV3L[:, :, 0:2, :], KV2, KV3H[:, :, 0:2, :].bitcast(F32), ALU.subtract).then_inc(xl_ready, KT)
            for i in range(3, 7):
                turn_lo(dve, n0 + i)

            def conv(c):
                dve.wait_ge(nsa_taken, 9 + 3 * c)
                if c:
                    dve.wait_ge(convh_ready, 1)
                order.after(dve.tensor_tensor(Z[:, :, 2:258], two(CC), two(CU), ALU.mult))
                for m in range(2):
                    w = [VEC[:, CONV_COL + 4 * tap + 2 * c + m:CONV_COL + 4 * tap + 2 * c + m + 1] for tap in range(4)]
                    order.after(dve.tensor_scalar(YC[:, m, :], Z[:, m, 0:256], w[0], w[3], ALU.mult, ALU.add))
                    order.after(dve.scalar_tensor_tensor(YC[:, m, :], Z[:, m, 1:257], w[1], YC[:, m, :], ALU.mult, ALU.add))
                    order.after(dve.scalar_tensor_tensor(YC[:, m, :], Z[:, m, 2:258], w[2], YC[:, m, :], ALU.mult, ALU.add))

            def conv_gate(c):
                dve.wait_ge(nsa_taken, 10 + 3 * c)
                dve.tensor_tensor(two(CB), two(CB), YC, ALU.mult).then_inc(conv_out, 1)

            def conv_lo(c):
                dve.wait_ge(convh_ready, c + 1)
                dve.tensor_tensor(ML[:, 4 + 2 * c:6 + 2 * c, :], two(CB), MH[:, 4 + 2 * c:6 + 2 * c, :].bitcast(F32),
                                  ALU.subtract).then_inc(convl_ready, 1)

            def bias(u):
                j, qt, hh = UNITS[u]
                nk = P * (qt + 1)
                slope = -2.0 ** -(2 * j + hh + 1)
                dve.wait_ge(scores_ready, u + 1)
                if u >= 2:
                    dve.wait_ge(exp_ready, u - 1)
                bank = 2 * (u % 2)
                dve.scalar_tensor_tensor(SB[:, u % 2, 0:16 + nk], DIST[:, qt, 0:16 + nk], slope, PS[:, bank, 0:16 + nk],
                                         ALU.mult, ALU.add)
                dve.scalar_tensor_tensor(SB[:, u % 2, 16 + nk:16 + 2 * nk], DIST[:, qt, 16:16 + nk], slope,
                                         PS[:, bank + 1, 0:nk], ALU.mult, ALU.add).then_inc(biased, 1)
                dve.wait_ge(biased, u + 1)
                dve.reduce_max(MX[:, u % 2, 0:1], SB[:, u % 2, 0:16], AX_X)
                order.after(dve.reduce_max(MX[:, u % 2, 1:3], SB[:, u % 2, 16:16 + 2 * nk].rearrange("p (b s) -> p b s", b=2), AX_X))
                dve.tensor_scalar(NM[:, u % 2, 0:3], MX[:, u % 2, 0:3], -1e20, -1.0, ALU.max, ALU.mult).then_inc(nm_ready, 1)

            def normalize(u):
                j, qt, hh = UNITS[u]
                nk, h = P * (qt + 1), 2 * j + hh
                dve.wait_ge(exp_ready, u + 1)
                r = RC[:, u % 2, 0:3]
                order.after(dve.tensor_scalar(r, SM[:, u % 2, 0:3], 1e-30, None, ALU.max))
                order.after(dve.reciprocal(r, r))
                order.after(dve.tensor_tensor(r, r, GATES[:, qt * 24 + 3 * h:qt * 24 + 3 * h + 3], ALU.mult))
                for i, (a, b) in enumerate([(0, 16), (16, 16 + nk), (16 + nk, 16 + 2 * nk)]):
                    last = dve.tensor_scalar(PB[:, u % 2, a:b], PB[:, u % 2, a:b], RC[:, u % 2, i:i + 1], None, ALU.mult)
                last.then_inc(prob_ready, 1)

            def take_pt(u):
                j, qt, hh = UNITS[u]
                nk = P * (qt + 1)
                dve.wait_ge(pt_ready, u + 1)
                if u >= 2:
                    dve.wait_ge(o_ready, u - 1)
                dve.tensor_copy(PTS[:, u % 2, 256:256 + nk], PS[:, 5, 0:nk]).then_inc(pt_taken_d, 1)

            def out_lo(j):
                dve.wait_ge(oh_ready, j + 1)
                dve.tensor_tensor(ML[:, j, :], OUT[:, j % 2, :], MH[:, j, :].bitcast(F32), ALU.subtract).then_inc(ol_ready, 1)

            dve.wait_ge(gates_taken, 1)
            bias(0)
            bias(1)
            for u in range(16):
                if u:
                    take_pt(u - 1)
                normalize(u)
                if u + 2 < 16:
                    bias(u + 2)
                if u % 4 == 0 and u:
                    out_lo(u // 4 - 1)
                if u in (6, 12):
                    conv(u // 8)
                if u in (7, 13):
                    conv_gate(u // 8)
                if u in (8, 14):
                    conv_lo(u // 14)
                if u % 2 and u <= 11:
                    turn_lo(dve, n0 + 7 + u // 2)
            take_pt(15)
            out_lo(3)
            for i in range(4):
                turn_lo(dve, n0 + 13 + i)
            post_add(dve, order, s, post_col)

        def nsa_pe(pe, s, n0, op):
            pre_mean(pe, s, mixer=True)
            pe.wait_ge(small_loaded, 16)
            pe.wait_ge(consts_made, N_CONSTS)
            opening_products(pe, n0, op)
            g_cols = SMALLW[:, SMALL["g"][0]:SMALL["g"][0] + KT * 24].rearrange("p (k n) -> p k n", k=KT)
            if s:
                pe.wait_ge(x_ready, KT * (s + 1))
            for t in range(TT):
                for k in range(KT):
                    pe.wait_ge(hn_ready, k + 1)
                    last = pe.matmul(PS[:, 7, 24 * t:24 * t + 24], HN[:, k, t * P:(t + 1) * P], g_cols[:, k, :],
                                     start=k == 0, stop=k == KT - 1)
            last.then_inc(gates_ready, 1)
            pe.wait_ge(nsa_taken, 1)
            column_products(pe, n0 + 2, BANK[0])
            for b in range(2):
                n, bank = n0 + 3 + b, BANK[(3 + b) % 2]
                pe.wait_ge(nsa_taken, 2 + b)
                pe.wait_ge(lo_ready, n + 1)
                for k in range(KT):
                    product(pe, bank[:, 0:SEQ], [slab(r, n)[:, k, 0:P] for r in (HI, LO)], (XH[:, k, :], XL[:, k, :]),
                            k == 0, k == KT - 1)
                last = token_products(pe, n, [bank[:, SEQ + P * t:SEQ + P * (t + 1)] for t in range(TT)], (P, 2 * P))
                last.then_inc(products_done, 1)
            pe.wait_ge(xl_ready, KT * (op + 3))
            pe.wait_ge(gates_taken, 1)
            for v, name in enumerate(("w2_k", "w2_v")):
                n, bank = n0 + 5 + v, BANK[(5 + v) % 2]
                pe.wait_ge(nsa_taken, 4 + v)
                pe.wait_ge(lo_ready, n + 1)
                w1 = [r[:, n % RING, :].rearrange("p (l n) -> p l n", l=16) for r in (HI, LO)]
                for l in range(16):
                    x = [y[:, v, :, 2 * l:2 * l + 241:16] for y in (KV3H, KV3L)]
                    last = product(pe, bank[:, 0:48].rearrange("p (g n) -> p g n", g=3), [w[:, l, :] for w in w1], x, l == 0, l == 15)
                last.then_inc(products_done, 1)
            for v, name in enumerate(("w2_k", "w2_v")):
                w2 = SMALLW[:, SMALL[name][0]:SMALL[name][0] + 64]
                pe.wait_ge(nsa_taken, 6 + v)
                for g in range(N_G):
                    if v == 0:
                        for half in range(2):
                            pe.matmul(PS[HD * half:HD * half + HD, 7, 16 * g:16 * g + 16], w2, GELU[:, 0, 16 * g:16 * g + 16],
                                      start=True, stop=True)
                    else:
                        last = pe.matmul(PS[0:N_CMP, 7, 64 + 64 * g:128 + 64 * g], GELU[:, 1, 16 * g:16 * g + 16], w2,
                                         start=True, stop=True)
            last.then_inc(cmp_ready, 1)
            pe.wait_ge(nsa_taken, 7)
            pe.wait_ge(cmp_taken, 1)

            def scores(u):
                j, qt, hh = UNITS[u]
                nk, g, a = P * (qt + 1), j // 2, HD * hh
                if u >= 2:
                    pe.wait_ge(biased, u - 1)
                bank = 2 * (u % 2)
                q = QT[a:a + HD, j, qt * P:(qt + 1) * P]
                pe.matmul(PS[:, bank, 0:16], q, KC2[a:a + HD, 16 * g:16 * g + 16], start=True, stop=True)
                pe.matmul(PS[:, bank, 16:16 + nk], q, KTB[a:a + HD, 0, g, 0:nk], start=True, stop=True)
                pe.matmul(PS[:, bank + 1, 0:nk], q, KTB[a:a + HD, 1, g, 0:nk], start=True, stop=True).then_inc(scores_ready, 1)

            def transposes(u):
                j, qt, hh = UNITS[u]
                nk = P * (qt + 1)
                pe.wait_ge(prob_ready, u + 1)
                if u:
                    pe.wait_ge(pt_taken_a, u)
                    pe.wait_ge(pt_taken_d, u)
                for b in range(qt + 1):
                    pe.transpose(PS[:, 4, b * P:(b + 1) * P], PB[:, u % 2, 16 + b * P:16 + (b + 1) * P], IDENT[:])
                    pe.transpose(PS[:, 5, b * P:(b + 1) * P], PB[:, u % 2, 16 + nk + b * P:16 + nk + (b + 1) * P], IDENT[:])
                pe.transpose(PS[0:N_CMP, 4, 256:384], PB[:, u % 2, 0:16], IDENT[:]).then_inc(pt_ready, 1)

            def values(u):
                j, qt, hh = UNITS[u]
                g = j // 2
                pe.wait_ge(pt_taken_a, u + 1)
                pe.wait_ge(pt_taken_d, u + 1)
                if u % 4 == 0 and j:
                    pe.wait_ge(ol_ready, j)
                out = OUT[HD * hh:HD * hh + HD, j % 2, qt * P:(qt + 1) * P]
                pe.matmul(out, VC[0:N_CMP, HD * g:HD * g + HD], PTS[0:N_CMP, u % 2, 512:640], start=True, stop=False)
                for b in range(2):
                    for kb in range(qt + 1):
                        last = pe.matmul(out, VB[:, b, kb, HD * g:HD * g + HD], PTS[:, u % 2, 256 * b + P * kb:256 * b + P * (kb + 1)],
                                         start=False, stop=b == 1 and kb == qt)
                last.then_inc(o_ready, 1)

            scores(0)
            scores(1)
            for u in range(16):
                if u + 2 < 16:
                    scores(u + 2)
                transposes(u)
                if u < 12:
                    if u % 2 == 0 and u:
                        pe.wait_ge(nsa_taken, 7 + u // 2)
                    column_products(pe, n0 + 7 + u // 2, PS[:, 7, :], tiles=(u % 2,))
                if u:
                    values(u - 1)
            values(15)
            pe.wait_ge(biased, 16)
            open_outputs(pe, s)
            pe.wait_ge(convl_ready, 2)
            for i in range(4):
                if i < 2:
                    pe.wait_ge(ol_ready, 2 * i + 2)
                row_products(pe, n0 + 13 + i, MH[:, 2 * i:2 * i + 2, :], ML[:, 2 * i:2 * i + 2, :], end=s if i == 3 else None)

        DECAY = 2.718281828459045 ** -0.5
        NJ, TOPS = KT, 7
        V0 = SCR[:, 0:2048].rearrange("p (c n) -> p c n", c=2)
        XX = SCR[:, 2048:4096].rearrange("p (k t) -> p k t", k=KT)
        XI = [SCR[:, 4096 + 2048 * i:6144 + 2048 * i].rearrange("p (k t) -> p k t", k=KT) for i in range(2)]
        XI.append(SQ)
        RT = SCR[:, 8192:10240].rearrange("p (k t) -> p k t", k=KT)
        KF = SCR[:, 10240:12288].rearrange("p (k t) -> p k t", k=KT)
        WM, AM, GM = SCR[0:64, 12288:12544], SCR[0:64, 12544:12800], SCR[:, 12800:13056]
        RN = SCR[:, 13056:13088]
        OMK = SCR[:, 13088:13096]
        NT4 = SCR[:, 2048:2560].rearrange("p (q n) -> p q n", q=4)
        ODD = [SCR[:, 7424 + 256 * i:7680 + 256 * i] for i in range(3)] + [SQ[:, 6, :], SQ[:, 7, :]]
        ODD.append(SMALLW[:, SMALL["g"][0]:SMALL["g"][0] + 256])
        G3 = [[x.rearrange("p (h n) -> p h n", h=2) for x in xs] for xs in
              ([SCR[:, 2560 + 256 * i:2816 + 256 * i] for i in range(6)], ODD)]
        TIS = [x.rearrange("p (q n) -> p q n", q=4) for x in (SCR[:, 4096:5120], NS[:, 0:1024])]
        NTS = SCR[:, 5120:5632].rearrange("p (c n) -> p c n", c=2)
        KR = [SCR[:, 5632 + 512 * i:6144 + 512 * i].rearrange("p (c w t) -> p c w t", c=2, w=2) for i in range(2)]
        BETA, KH, RK = (SCR[:, 6656 + 256 * i:6912 + 256 * i] for i in range(3))
        S_T, A_T, C_T, D_T, EX, KKN = (SQ[:, i, :] for i in range(6))
        EN, EP = S_T, C_T
        RFREE = SMALLW[:, SMALL["dec1"][0]:SMALL["dec1"][0] + 2048]
        TOK0, RS, U_S, Y_C, YQ, BV, FO = (RFREE[:, 256 * i:256 * (i + 1)] for i in range(7))
        TOKS = [TOK0, NS[:, 1024:1280]]
        ST = RFREE[:, 1792:1920]
        RMN, RVR, RBS, SF = (RFREE[:, 1920 + 8 * i:1928 + 8 * i] for i in range(4))
        HSEL = sb("head_columns", [P, 2])
        MASK2 = sb("strict_inclusive", [P, 2 * P], BF16)
        rk_taken, rk_x, rk_mid, rk_mid_taken = (sem("rwkv_" + x) for x in ("bank_taken", "operand", "lora_mid", "lora_mid_taken"))
        rk_ksq, rk_n2, rk_n2max, rk_n2root, rk_n2done = (sem("rwkv_kk_" + x) for x in ("squares", "sums", "bounded", "root", "norm"))

        class Steps:
            def __init__(self, name, steps):
                self.semaphore, self.steps = sem(name), steps

            def at(self, j, step):
                return len(self.steps) * j + self.steps.index(step) + 1

        levels = [(l, c) for l in range(1, TOPS) for c in range(2)]
        pe_inv = [x + "%d%d" % lc for l in range(1, TOPS) for x, lc in
                  (("nt", (l, 0)), ("nt", (l, 1)), ("tnt", (l, 0)), ("tnt", (l, 1)))]
        ew_pe, ew_act, ew_dve = (Steps("rwkv_factors_" + e, x) for e, x in (
            ("tensor", ["lora", "norm"]), ("scalar", ["sigmoid", "exp"]), ("vector", ["kk", "exponents", "factors"])))
        in_pe = Steps("rwkv_inverse_tensor", ["matrices", "turns"] + pe_inv)
        in_act = Steps("rwkv_inverse_scalar", ["identity", "tokens"] + ["nt%d%d" % lc for lc in levels])
        in_dve = Steps("rwkv_inverse_vector", ["first", "masked1", "masked0"] + ["t%d%d" % lc for lc in levels])
        po_pe = Steps("rwkv_output_tensor", ["r0", "u0", "y0", "state", "r1", "u1", "y1", "turned"])
        po_act = Steps("rwkv_output_scalar", ["r0", "u0", "r1", "u1", "std", "hi"])
        po_dve = Steps("rwkv_output_vector", ["state", "variance", "normed", "output", "lo"])

        def out_banks(j):
            return (PS[:, 2, :], PS[:, 3, :]) if j + 1 < NJ else (PS[:, 4, :], PS[:, 5, :])

        def rwkv_pool(pool):
            pool.memset(MASK2[:], 1.0).then_inc(pool_order, 1)
            pool.wait_ge(pool_order, 12)
            for w in range(2):
                v = MASK2[:, P * w:P * (w + 1)]
                pool.affine_select(out=v, in_=v, compare_op=ALU.is_ge, fill=0.0, base=w - 1, pattern=[[1, P]],
                                   channel_multiplier=-1).then_inc(consts_made, 1)

        def rwkv_act(act, order, s, n0, op, col):
            pre_squares(act, s)
            pre_std(act, s)

            def operand(i, hi):
                for k in range(KT):
                    act.wait_ge(rk_x, KT * i + k + 1)
                    act.activation(hi[:, k, :], XI[(0, 1, None, None, 2)[i]][:, k, :], ACT.Copy).then_inc(xh_ready, 1)

            def take(i):
                if i >= 2:
                    turn_hi(act, n0 + i)
                act.wait_ge(products_done, n0 + i + 1)
                bank = two(BANK[i % 2])
                if i < 8:
                    last = act.activation((RT, KF)[i // 4][:, 2 * (i % 4):2 * (i % 4) + 2, :], bank, ACT.Copy)
                else:
                    last = act.activation(V0[:, :, 256 * (i - 8):256 * (i - 7)], bank, ACT.Copy)
                last.then_inc(rk_taken, 1)

            operand(0, XH)
            turn_hi(act, n0)
            take(0)
            turn_hi(act, n0 + 1)
            operand(1, MH)
            for i in range(1, 4):
                take(i)
            take(4)
            operand(4, XH)
            for i in range(5, 8):
                take(i)
            act.wait_ge(rk_mid, 1)
            act.activation(WM, PS[0:64, 6, 0:SEQ], ACT.Tanh).then_inc(rk_mid_taken, 1)
            act.wait_ge(rk_mid, 2)
            act.activation(AM, PS[0:64, 7, 0:SEQ], ACT.Copy).then_inc(rk_mid_taken, 1)
            act.wait_ge(rk_taken, 8)
            for k in range(KT):
                c = COL["l1_k_k"] + k
                last = act.activation(XI[1][:, k, :], KF[:, k, :], ACT.Square, scale=VEC[:, c:c + 1])
            last.then_inc(rk_ksq, 1)
            act.wait_ge(rk_x, KT * 6)
            for i in range(8, 12):
                take(i)
                if i == 9:
                    act.wait_ge(rk_n2max, 1)
                    act.activation(RN, RN, ACT.Sqrt).then_inc(rk_n2root, 1)
            act.wait_ge(rk_mid, 3)
            act.activation(GM, PS[:, 6, 0:SEQ], ACT.Sigmoid).then_inc(rk_mid_taken, 1)

            def factors(j, part):
                if part == 0:
                    act.wait_ge(ew_pe.semaphore, ew_pe.at(j, "lora"))
                    a0, w0 = COL["l1_a0"] + j, COL["l1_w0"] + j
                    act.activation(A_T, PS[:, 6, 0:SEQ], ACT.Sigmoid, bias=VEC[:, a0:a0 + 1])
                    act.activation(S_T, PS[:, 6, SEQ:2 * SEQ], ACT.Sigmoid, bias=VEC[:, w0:w0 + 1]).then_inc(ew_act.semaphore, 1)
                if part == 1:
                    act.wait_ge(ew_dve.semaphore, ew_dve.at(j, "exponents"))
                    act.activation(EP, D_T, ACT.Exp, scale=-DECAY)
                    act.activation(EN, D_T, ACT.Exp, scale=DECAY)
                    act.activation(SF[:, j % 2:j % 2 + 1], SF[:, 2 + j % 2:3 + j % 2], ACT.Exp, scale=-DECAY)
                    act.activation(EX, EX, ACT.Exp, scale=-DECAY).then_inc(ew_act.semaphore, 1)

            def output(j, step):
                bank = out_banks(j)[0]
                if step in ("r0", "r1"):
                    act.wait_ge(po_pe.semaphore, po_pe.at(j, step))
                    act.activation(RS[:, 0:P], bank[:, 0:P], ACT.Copy).then_inc(po_act.semaphore, 1)
                if step in ("u0", "u1"):
                    act.wait_ge(po_pe.semaphore, po_pe.at(j, step))
                    act.activation(U_S[:, 0:P], bank[:, P:2 * P], ACT.Copy).then_inc(po_act.semaphore, 1)
                if step == "std":
                    act.wait_ge(po_dve.semaphore, po_dve.at(j, "variance"))
                    act.activation(RVR[:, 4:8], RVR[:, 0:4], ACT.Sqrt, scale=1.0 / HD, bias=EPSILON[:, 1:2]).then_inc(po_act.semaphore, 1)
                if step == "hi":
                    act.wait_ge(po_dve.semaphore, po_dve.at(j, "output"))
                    act.activation(MH[:, j, :], FO, ACT.Copy).then_inc(po_act.semaphore, 1)

            def inverse(j):
                if j >= 2:
                    act.wait_ge(po_pe.semaphore, po_pe.at(j - 2, "y1"))
                act.activation(TIS[j % 2].rearrange("p q (w n) -> p (q w) n", w=2), IDENT[:, None, :].to_broadcast([P, 8, P]),
                               ACT.Copy).then_inc(in_act.semaphore, 1)
                if j >= 2:
                    output(j - 2, "hi")
                act.wait_ge(in_pe.semaphore, in_pe.at(j, "turns"))
                act.activation(TOKS[j % 2], PS[:, 4, SEQ:2 * SEQ], ACT.Copy)
                act.activation(RBS[:, 4 * (j % 2):4 * (j % 2) + 4], PS[:, 5, SEQ:SEQ + 4], ACT.Copy).then_inc(in_act.semaphore, 1)
                for l, c in levels:
                    act.wait_ge(in_pe.semaphore, in_pe.at(j, "nt%d%d" % (l, c)))
                    act.activation(NTS[:, c, :], PS[:, 4 + c, 0:SEQ], ACT.Copy).then_inc(in_act.semaphore, 1)
                    if j and c:
                        for step in {1: ("r0", "u0"), 2: ("r1", "u1"), 5: ("std",)}.get(l, ()):
                            output(j - 1, step)
                    if c and l in (1, 3) and j + 1 < NJ:
                        factors(j + 1, l // 2)

            factors(0, 0)
            factors(0, 1)
            for j in range(NJ):
                inverse(j)
            output(NJ - 2, "hi")
            turn_hi(act, n0 + 12)
            for step in po_act.steps:
                output(NJ - 1, step)
                if step == "std":
                    turn_hi(act, n0 + 13)
            for i in (2, 3):
                turn_hi(act, n0 + 12 + i)
            post_squares(act, s, n0 + 16)
            post_std(act, s)

        def rwkv_dve(dve, order, s, n0, op, col, post_col):
            pre_rstd(dve, s)

            def mix(i, mu, out, tiles=range(KT)):
                for k in tiles:
                    c = COL["mu%d" % mu] + k
                    dve.scalar_tensor_tensor(out[:, k, :], XX[:, k, :], VEC[:, c:c + 1], HN[:, k, :], ALU.mult,
                                             ALU.add).then_inc(rk_x, 1)

            def lo(i, x, hi, out, tiles=range(KT)):
                for k in tiles:
                    dve.wait_ge(xh_ready, KT * (op + i) + k + 1)
                    dve.tensor_tensor(out[:, k, :], x[:, k, :], hi[:, k, :].bitcast(F32), ALU.subtract).then_inc(xl_ready, 1)

            dve.wait_ge(rstd_ready, s + 1)
            for k in range(KT + 2):
                if k < KT:
                    dve.scalar_tensor_tensor(HN[:, k, :], X[:, k, :], VEC[:, col + k:col + k + 1], RSTD,
                                             ALU.mult, ALU.mult).then_inc(hn_ready, 1)
                    dve.wait_ge(hn_ready, KT + k + 1)
                    dve.tensor_scalar(XX[:, k, 0:1], HN[:, k, 0:1], -1.0, None, ALU.mult)
                    order.after(dve.tensor_tensor(XX[:, k, 1:SEQ], HN[:, k, 0:SEQ - 1], HN[:, k, 1:SEQ], ALU.subtract))
                    mix(0, 0, XI[0], (k,))
                if k >= 2:
                    lo(0, XI[0], XH, XL, (k - 2,))
            turn_lo(dve, n0)
            mix(1, 2, XI[1])
            turn_lo(dve, n0 + 1)
            lo(1, XI[1], MH, ML)
            dve.wait_ge(xl_ready, KT * (op + 1))
            mix(2, 1, XI[0])
            dve.wait_ge(xl_ready, KT * (op + 2))
            mix(3, 4, XI[1])
            turn_lo(dve, n0 + 2)
            mix(4, 3, SQ)
            for i in range(3, 5):
                turn_lo(dve, n0 + i)
            lo(2, SQ, XH, XL)
            for i in range(5, 8):
                turn_lo(dve, n0 + i)
            dve.wait_ge(rk_mid, 1)
            mix(5, 5, XI[0])
            for i in range(8, 12):
                turn_lo(dve, n0 + i)
                if i == 9:
                    dve.wait_ge(rk_n2, 1)
                    dve.tensor_scalar(RN, PS[:, 7, 0:32], 1e-12, None, ALU.max).then_inc(rk_n2max, 1)
            c = COL["l1_k_a"]
            order.after(dve.tensor_scalar(OMK, VEC[:, c:c + KT], -1.0, 1.0, ALU.mult, ALU.add))
            dve.wait_ge(rk_mid_taken, 3)
            order.after(dve.memset(ST, 0.0))
            dve.wait_ge(rk_n2root, 1)
            dve.reciprocal(RN, RN).then_inc(rk_n2done, 1)
            dve.wait_ge(masks_made, MASKS_MADE)

            def factors(j, part):
                if part == 0:
                    dve.wait_ge(ew_act.semaphore, ew_act.at(j, "sigmoid"))
                    order.after(dve.tensor_tensor_scan(C_T, CARRY[:], S_T, 0.0, ALU.mult, ALU.add))
                    c3 = C_T.rearrange("p (c t) -> p c t", c=2)
                    d3 = D_T.rearrange("p (c t) -> p c t", c=2)
                    order.after(dve.tensor_tensor(d3, c3, c3[:, :, 63:64].to_broadcast([P, 2, P]), ALU.subtract))
                    dve.tensor_tensor(SF[:, 2 + j % 2:3 + j % 2], D_T[:, P - 1:P], C_T[:, P + 63:P + 64], ALU.add)
                    dve.tensor_tensor(EX, D_T, S_T, ALU.subtract).then_inc(ew_dve.semaphore, 1)
                if part == 1:
                    dve.wait_ge(ew_pe.semaphore, ew_pe.at(j, "norm"))
                    c = COL["l1_k_k"] + j
                    dve.scalar_tensor_tensor(KKN, KF[:, j, :], VEC[:, c:c + 1], PS[:, 7, 0:SEQ], ALU.mult, ALU.mult).then_inc(ew_dve.semaphore, 1)
                if part == 2:
                    c = COL["l1_k_a"] + j
                    dve.wait_ge(ew_dve.semaphore, ew_dve.at(j, "kk"))
                    dve.wait_ge(ew_act.semaphore, ew_act.at(j, "sigmoid"))
                    order.after(dve.tensor_tensor(BETA, KKN, A_T, ALU.mult))
                    order.after(dve.tensor_scalar(A_T, A_T, VEC[:, c:c + 1], OMK[:, j:j + 1], ALU.mult, ALU.add))
                    order.after(dve.tensor_tensor(KF[:, j, :], KF[:, j, :], A_T, ALU.mult))
                if part == 3:
                    kr, t3 = KR[j % 2], lambda x: x.rearrange("p (c t) -> p c t", c=2)
                    c = COL["l1_r_k"] + j
                    dve.wait_ge(ew_act.semaphore, ew_act.at(j, "exp"))
                    dve.scalar_tensor_tensor(kr[:, :, 0, :], t3(KKN), -1.0, t3(EX), ALU.mult, ALU.mult)
                    dve.tensor_tensor(kr[:, :, 1, :], t3(RT[:, j, :]), t3(EP), ALU.mult)
                    dve.tensor_tensor(BETA, BETA, EN, ALU.mult)
                    dve.tensor_tensor(KH, KF[:, j, :], EN, ALU.mult)
                    dve.scalar_tensor_tensor(RK, RT[:, j, :], VEC[:, c:c + 1], KF[:, j, :], ALU.mult, ALU.mult).then_inc(ew_dve.semaphore, 1)

            h4 = lambda x: x.rearrange("p (h n) -> p h n", h=4)
            wide = lambda x: x.unsqueeze(2).to_broadcast([P, 4, HD])

            def output(j, step):
                bank_a, bank_b = out_banks(j)
                if step == "state":
                    dve.wait_ge(po_pe.semaphore, po_pe.at(j, "state"))
                    for hh in range(2):
                        a = slice(HD * hh, HD * hh + HD)
                        last = dve.tensor_scalar(ST[a, a], bank_b[a, SEQ:SEQ + HD], SF[a, j % 2:j % 2 + 1], None, ALU.mult)
                    last.then_inc(po_dve.semaphore, 1)
                if step == "mean":
                    dve.wait_ge(po_pe.semaphore, po_pe.at(j, "y1"))
                    order.after(dve.reduce_sum(RMN[:, 0:4], h4(bank_b[:, 0:SEQ]), AX_X))
                    order.after(dve.tensor_scalar(RMN[:, 0:4], RMN[:, 0:4], 1.0 / HD, None, ALU.mult))
                    order.after(dve.tensor_tensor(h4(Y_C), h4(bank_b[:, 0:SEQ]), wide(RMN[:, 0:4]), ALU.subtract))
                if step == "variance":
                    order.after(dve.tensor_tensor(YQ, Y_C, Y_C, ALU.mult))
                    dve.reduce_sum(RVR[:, 0:4], h4(YQ), AX_X).then_inc(po_dve.semaphore, 1)
                    dve.wait_ge(in_act.semaphore, in_act.at(j, "tokens"))
                    v = V0[:, :, P * j:P * (j + 1)].rearrange("p c (h n) -> p c h n", h=2)
                    bs = RBS[:, 4 * (j % 2):4 * (j % 2) + 4].rearrange("p (c h) -> p c h", c=2).unsqueeze(3).to_broadcast([P, 2, 2, HD])
                    dve.tensor_tensor(BV.rearrange("p (c h n) -> p c h n", c=2, h=2), v, bs, ALU.mult)
                if step == "normed":
                    dve.wait_ge(po_act.semaphore, po_act.at(j, "std"))
                    order.after(dve.reciprocal(RMN[:, 4:8], RVR[:, 4:8]))
                    dve.tensor_tensor(h4(Y_C), h4(Y_C), wide(RMN[:, 4:8]), ALU.mult).then_inc(po_dve.semaphore, 1)
                if step == "output":
                    dve.wait_ge(po_pe.semaphore, po_pe.at(j, "turned"))
                    g, b = COL["l1_lnx_g"] + j, COL["l1_lnx_b"] + j
                    order.after(dve.tensor_scalar(FO, bank_a[:, 0:SEQ], VEC[:, g:g + 1], VEC[:, b:b + 1], ALU.mult, ALU.add))
                    order.after(dve.tensor_tensor(FO, FO, bank_a[:, SEQ:2 * SEQ], ALU.add))
                    dve.tensor_tensor(FO, FO, bank_b[:, 0:SEQ], ALU.mult).then_inc(po_dve.semaphore, 1)
                if step == "lo":
                    dve.wait_ge(po_act.semaphore, po_act.at(j, "hi"))
                    dve.tensor_tensor(ML[:, j, :], FO, MH[:, j, :].bitcast(F32), ALU.subtract).then_inc(po_dve.semaphore, 1)

            def inverse(j):
                ti = TIS[j % 2]

                def masked(c, w):
                    out = NT4[:, 2 * c:2 * c + 2, :] if w == 0 else G3[j % 2][2 * (w - 1) + c]
                    mask = MASK2[:, P * (w % 2):P * (w % 2) + P]
                    return dve.tensor_tensor(out, PS[:, 2 * c:2 * c + 2, P * w:P * (w + 1)], mask[:, None, :].to_broadcast([P, 2, P]), ALU.mult)

                if j >= 2:
                    output(j - 2, "output")
                dve.wait_ge(in_pe.semaphore, in_pe.at(j, "matrices"))
                masked(0, 0)
                masked(1, 0)
                dve.wait_ge(in_act.semaphore, in_act.at(j, "identity"))
                mask = LMASK[:, 0, 1:2, :].bitcast(mybir.dt.uint16).to_broadcast([P, 4, P])
                dve.copy_predicated(ti[:, :, P:2 * P], mask, PS[:, 0:4, 0:P])
                dve.wait_ge(in_act.semaphore, in_act.at(j, "tokens"))
                for hh in range(2):
                    mask = LMASK[:, 0, 0:1, :].bitcast(mybir.dt.uint16).to_broadcast([P, 2, P])
                    last = dve.copy_predicated(ti.rearrange("p (c h) n -> p h c n", h=2)[:, hh, :, 0:P], mask,
                                               PS[:, 4 + hh, 0:SEQ].rearrange("p (c n) -> p c n", c=2))
                last.then_inc(in_dve.semaphore, 1)
                for c in (1, 0):
                    for w in (1, 2, 3):
                        last = masked(c, w)
                    last.then_inc(in_dve.semaphore, 1)
                if j >= 2:
                    output(j - 2, "lo")
                for l, c in levels:
                    dve.wait_ge(in_pe.semaphore, in_pe.at(j, "tnt%d%d" % (l, c)))
                    w = 0 if l < TOPS - 1 else P
                    mask = LMASK[:, l:l + 1, :, :].rearrange("p l w n -> p l (w n)")[:, :, w:2 * P].bitcast(mybir.dt.uint16)
                    dve.copy_predicated(ti[:, 2 * c:2 * c + 2, w:2 * P], mask.to_broadcast([P, 2, 2 * P - w]),
                                        PS[:, c, :].rearrange("p (h n) -> p h n", h=2)[:, :, w:2 * P]).then_inc(in_dve.semaphore, 1)
                    if j and c and l in (1, 3, 4, 5):
                        output(j - 1, {1: "state", 3: "mean", 4: "variance", 5: "normed"}[l])
                    if c and j + 1 < NJ:
                        for part in {1: (1, 2), 2: (0,), 5: (3,)}.get(l, ()):
                            factors(j + 1, part)

            for part in (1, 0, 2, 3):
                factors(0, part)
            for j in range(NJ):
                inverse(j)
            output(NJ - 2, "output")
            output(NJ - 2, "lo")
            turn_lo(dve, n0 + 12)
            for step in ("state", "mean", "variance", "normed", "output", "lo"):
                output(NJ - 1, step)
                if step == "normed":
                    turn_lo(dve, n0 + 13)
            for i in (2, 3):
                turn_lo(dve, n0 + 12 + i)
            post_add(dve, order, s, post_col)

        def rwkv_pe(pe, s, n0, op):
            pre_mean(pe, s, mixer=True)

            def small(name, m):
                return SMALLW[:, SMALL[name][0]:SMALL[name][0] + KT * m].rearrange("p (k n) -> p k n", k=KT)

            def lora(i, name, m, x, bank):
                w = small(name, m)
                for k in range(KT):
                    pe.wait_ge(rk_x, KT * i + k + 1)
                    last = pe.matmul(PS[0:m, bank, 0:SEQ], w[:, k, :], x[:, k, :], start=k == 0, stop=k == KT - 1)
                last.then_inc(rk_mid, 1)

            opening_products(pe, n0, op)
            for i in range(2, 12):
                if i == 8:
                    lora(2, "dec1", 64, XI[0], 6)
                    lora(3, "a1", 64, XI[1], 7)
                if i == 10:
                    pe.wait_ge(rk_mid_taken, 2)
                    pe.wait_ge(rk_ksq, 1)
                    for c in range(2):
                        for j in range(NJ):
                            last = pe.matmul(PS[:, 7, 16 * c + 2 * j:16 * c + 2 * j + 2], XI[1][:, j, P * c:P * (c + 1)], HSEL[:],
                                             start=True, stop=True)
                    last.then_inc(rk_n2, 1)
                if i >= 2:
                    pe.wait_ge(rk_taken, i - 1)
                if i < 8:
                    column_products(pe, n0 + i, BANK[i % 2], op=op + 1 if i == 4 else None, x=((XH, XL), (MH, ML))[i // 4])
                else:
                    pe.wait_ge(xl_ready, KT * (op + 3))
                    pe.wait_ge(lo_ready, n0 + i + 1)
                    out = [BANK[i % 2][:, SEQ * t:SEQ * (t + 1)] for t in range(TT)]
                    token_products(pe, n0 + i, out, (0, COLS)).then_inc(products_done, 1)
            pe.wait_ge(rk_mid_taken, 1)
            lora(5, "g1", 128, XI[0], 6)
            pe.wait_ge(rk_mid_taken, 3)
            pe.wait_ge(rk_taken, 12)
            pe.wait_ge(x_ready, KT * (s + 1))
            pe.wait_ge(rk_n2done, 1)

            def factors(j):
                if j:
                    pe.wait_ge(ew_act.semaphore, ew_act.at(j - 1, "sigmoid"))
                    pe.wait_ge(ew_dve.semaphore, ew_dve.at(j - 1, "kk"))
                c = slice(P * j, P * (j + 1))
                a2, w2 = (SMALLW[0:64, SMALL[x][0]:SMALL[x][0] + D][:, c] for x in ("a2", "dec2"))
                pe.matmul(PS[:, 6, 0:SEQ], a2, AM, start=True, stop=True)
                pe.matmul(PS[:, 6, SEQ:2 * SEQ], w2, WM, start=True, stop=True).then_inc(ew_pe.semaphore, 1)
                for c in range(2):
                    for hh in range(2):
                        rn = RN[:, 16 * c + 2 * j + hh:16 * c + 2 * j + hh + 1].to_broadcast([P, HD])
                        last = pe.matmul(PS[HD * hh:HD * hh + HD, 7, P * c:P * (c + 1)], rn, IDENT[:], start=True, stop=True)
                last.then_inc(ew_pe.semaphore, 1)

            def inverse(j):
                kr, ti = KR[j % 2], TIS[j % 2]
                pe.wait_ge(ew_dve.semaphore, ew_dve.at(j, "factors"))
                if j:
                    pe.wait_ge(in_act.semaphore, in_act.at(j - 1, "nt%d%d" % levels[-1]))
                    pe.wait_ge(in_dve.semaphore, in_dve.at(j - 1, "t%d%d" % levels[-1]))
                for q in range(4):
                    if q == 2 and j >= 2:
                        pe.wait_ge(po_dve.semaphore, po_dve.at(j - 2, "output"))
                    a, c = slice(HD * (q % 2), HD * (q % 2) + HD), q // 2
                    t = slice(P * c, P * (c + 1))
                    both = kr[a, c, :, :].rearrange("p w t -> p (w t)")
                    pe.matmul(PS[:, q, 0:2 * P], BETA[a, t], both, start=True, stop=True)
                    pe.matmul(PS[:, q, 2 * P:4 * P], KH[a, t], both, start=True, stop=True)
                    last = pe.matmul(PS[:, 4 + q % 2, t], kr[a, c, 0, :], BETA[a, t], start=True, stop=True)
                last.then_inc(in_pe.semaphore, 1)
                pe.transpose(PS[:, 4, 2 * P:3 * P], BETA[:, 0:P], IDENT[:])
                pe.transpose(PS[:, 4, 3 * P:4 * P], KH[:, 0:P], IDENT[:])
                for c in range(2):
                    last = pe.matmul(PS[:, 5, SEQ + 2 * c:SEQ + 2 * c + 2], RK[:, P * c:P * (c + 1)], HSEL[:], start=True, stop=True)
                last.then_inc(in_pe.semaphore, 1)
                if j + 1 < NJ:
                    factors(j + 1)
                for l in range(1, TOPS):
                    for c in range(2):
                        if l == 1:
                            pe.wait_ge(in_dve.semaphore, in_dve.at(j, "first"))
                            pe.wait_ge(in_act.semaphore, in_act.at(j, "tokens"))
                        else:
                            pe.wait_ge(in_dve.semaphore, in_dve.at(j, "t%d%d" % (l - 1, c)))
                        for hh in range(2):
                            q = 2 * c + hh
                            last = pe.matmul(PS[:, 4 + c, P * hh:P * (hh + 1)], NT4[:, q, :], ti[:, q, 0:P], start=True, stop=True)
                        last.then_inc(in_pe.semaphore, 1)
                        if j and (l, c) in ((1, 1), (2, 0)):
                            output(j - 1, l - 1, "r")
                    for c in range(2):
                        if l == 1 and c == 0:
                            pe.wait_ge(in_dve.semaphore, in_dve.at(j, "masked0"))
                        pe.wait_ge(in_act.semaphore, in_act.at(j, "nt%d%d" % (l, c)))
                        for hh in range(2):
                            q, nt = 2 * c + hh, NTS[:, c, P * hh:P * (hh + 1)]
                            if l < TOPS - 1:
                                pe.matmul(PS[:, c, 2 * P * hh:2 * P * hh + P], ti[:, q, P:2 * P], nt, start=True, stop=True)
                            last = pe.matmul(PS[:, c, 2 * P * hh + P:2 * P * (hh + 1)], nt, ti[:, q, P:2 * P], start=True, stop=True)
                        last.then_inc(in_pe.semaphore, 1)
                        if j and l <= 2:
                            output(j - 1, l - 1, "uy"[c])
                    if j and l == TOPS - 1:
                        turned(j - 1)

            def output(j, c, step):
                kr, tok, ti = KR[j % 2], TOKS[j % 2], TIS[j % 2]
                bank_a, bank_b = out_banks(j)
                rb, kk, rk = (G3[j % 2][2 * i + c] for i in range(3))
                heads = [(hh, slice(HD * hh, HD * hh + HD), V0[:, c, P * j + HD * hh:P * j + HD * hh + HD]) for hh in range(2)]
                if step == "r":
                    if c:
                        pe.wait_ge(po_dve.semaphore, po_dve.at(j, "state"))
                        pe.matmul(bank_a[:, 0:P], kr[:, c, 0, :], ST, start=True, stop=False, skip_group_check=True)
                    elif j + 1 < NJ:
                        pe.wait_ge(in_dve.semaphore, in_dve.at(j + 1, "masked1"))
                    else:
                        pe.wait_ge(in_dve.semaphore, in_dve.at(j, "t%d%d" % levels[-1]))
                        pe.wait_ge(in_act.semaphore, in_act.at(j, "nt%d%d" % levels[-1]))
                    for hh, a, v in heads:
                        last = pe.matmul(bank_a[:, a], kk[:, hh, :], v, start=not c, stop=True, skip_group_check=True)
                    last.then_inc(po_pe.semaphore, 1)
                if step == "u":
                    pe.wait_ge(po_act.semaphore, po_act.at(j, "r%d" % c))
                    for hh, a, v in heads:
                        last = pe.matmul(bank_a[:, P + HD * hh:P + HD * hh + HD], ti[:, 2 * c + hh, P:2 * P], RS[:, a], start=True, stop=True)
                    last.then_inc(po_pe.semaphore, 1)
                if step == "y":
                    pe.wait_ge(po_act.semaphore, po_act.at(j, "u%d" % c))
                    if c:
                        pe.matmul(bank_b[:, P:2 * P], kr[:, c, 1, :], ST, start=True, stop=False, skip_group_check=True)
                    for hh, a, v in heads:
                        out = bank_b[:, P * c + HD * hh:P * c + HD * hh + HD]
                        pe.matmul(out, rb[:, hh, :], U_S[:, a], start=not c, stop=False, skip_group_check=True)
                        last = pe.matmul(out, rk[:, hh, :], v, start=False, stop=True, skip_group_check=True)
                    last.then_inc(po_pe.semaphore, 1)
                    if c == 0:
                        for hh, a, v in heads:
                            pe.matmul(bank_b[a, SEQ:SEQ + HD], tok[:, a], U_S[:, a], start=True, stop=False)
                            last = pe.matmul(bank_b[a, SEQ:SEQ + HD], tok[:, P + HD * hh:P + HD * hh + HD], v, start=False, stop=True)
                        last.then_inc(po_pe.semaphore, 1)

            def turned(j):
                pe.wait_ge(po_dve.semaphore, po_dve.at(j, "normed"))
                bank_a, bank_b = out_banks(j)
                for c in range(2):
                    pe.transpose(bank_a[:, P * c:P * (c + 1)], Y_C[:, P * c:P * (c + 1)], IDENT[:])
                    pe.transpose(bank_a[:, SEQ + P * c:SEQ + P * (c + 1)], BV[:, P * c:P * (c + 1)], IDENT[:])
                g2 = SMALLW[:, SMALL["g2"][0]:SMALL["g2"][0] + D][:, P * j:P * (j + 1)]
                pe.matmul(bank_b[:, 0:SEQ], g2, GM, start=True, stop=True).then_inc(po_pe.semaphore, 1)

            factors(0)
            keep_warm(pe, 24)
            for j in range(NJ):
                inverse(j)

            def out_rows(i, tiles=range(KT), end=None):
                row_products(pe, n0 + 12 + i, MH[:, 2 * i:2 * i + 2, :], ML[:, 2 * i:2 * i + 2, :], end=end, tiles=tiles)

            pe.wait_ge(po_dve.semaphore, po_dve.at(NJ - 2, "output"))
            open_outputs(pe, s)
            for n, (c, step) in enumerate([(c, step) for c in range(2) for step in "ruy"]):
                output(NJ - 1, c, step)
                if n < 4:
                    out_rows(0, range(2 * n, 2 * n + 2))
                elif n == 4:
                    out_rows(1, range(2))
                else:
                    out_rows(1, range(2, KT))
            turned(NJ - 1)
            out_rows(2)
            pe.wait_ge(po_dve.semaphore, po_dve.at(NJ - 1, "lo"))
            out_rows(3, end=s)
        F_UNITS = [(j, qt, hh) for j in range(8) for qt in range(TT) for hh in range(2)]
        FQ = SCR[:, 2048:4096].rearrange("p (j t) -> p j t", j=8)
        FK = SCR[:, 4096:6144].rearrange("p (j t) -> p j t", j=8)
        FV = SCR[:, 6144:8192].rearrange("p (t c) -> p t c", t=2)
        FS = SCR[:, 8192:8704].rearrange("p (b s) -> p b s", b=2)
        FP = SCR[:, 8704:9216].rearrange("p (b s) -> p b s", b=2)
        FPT = SCR[:, 9216:9728].rearrange("p (b s) -> p b s", b=2)
        FST = SCR[:, 9728:9736].rearrange("p (b s) -> p b s", b=2)
        F_Z, F_L, F_ONES, F_NEGC = (SCR[0:16, 9736 + SEQ * i:9736 + SEQ * (i + 1)] for i in range(4))
        CAUSAL = sb("causal_mask", [P, 2 * P], BF16)
        fox_taken = sem("fox_bank_taken")
        forget_ready, forget_abs, forget_ln, forget_done = (sem("fox_forget_" + x) for x in ("ready", "abs", "ln", "done"))
        fs_ready, fs_taken, fm_ready, fe_ready, fp_ready = (sem("fox_" + x) for x in ("scores", "scores_taken", "max", "exp", "probs"))
        fpt_ready, fpt_taken, fo_ready, foh_ready, fol_ready = (sem("fox_" + x) for x in ("pt", "pt_taken", "out", "out_hi", "out_lo"))

        def fox_pool(pool):
            pool.memset(CAUSAL[:], 0.0).then_inc(pool_order, 1)
            pool.wait_ge(pool_order, 11)
            pool.affine_select(out=CAUSAL[:, P:2 * P], in_=CAUSAL[:, P:2 * P], compare_op=ALU.is_ge, fill=-1e30, base=0,
                               pattern=[[-1, P]], channel_multiplier=1).then_inc(consts_made, 1)

        def fox_act(act, order, s, n0, op, col):
            pre_squares(act, s)
            pre_std(act, s)
            mixer_operand_act(act, 2, op)
            act.wait_ge(forget_abs, 1)
            order.after(act.activation(F_L, F_L, ACT.Exp, scale=-1.0))
            act.activation(F_L, F_L, ACT.Ln, bias=F_ONES[:, 0:1]).then_inc(forget_ln, 1)
            for i in range(12):
                turn_hi(act, n0 + i)
                act.wait_ge(products_done, n0 + i + 1)
                bank = two(BANK[i % 2])
                if i < 4:
                    last = act.activation(FQ[:, 2 * i:2 * i + 2, :], bank, ACT.Copy, scale=HD ** -0.5)
                elif i < 8:
                    last = act.activation(FK[:, 2 * i - 8:2 * i - 6, :], bank, ACT.Copy)
                else:
                    last = act.activation(FV[:, :, 256 * (i - 8):256 * (i - 7)], bank, ACT.Copy)
                last.then_inc(fox_taken, 1)

            def exps(u):
                nk = P * (F_UNITS[u][1] + 1)
                act.wait_ge(fm_ready, u + 1)
                if u >= 2:
                    act.wait_ge(fpt_ready, u - 1)
                act.activation(FP[:, u % 2, 0:nk], FS[:, u % 2, 0:nk], ACT.Exp, bias=FST[:, u % 2, 1:2],
                               accum_out=FST[:, u % 2, 2:3]).then_inc(fe_ready, 1)

            def take_pt(u):
                nk = P * (F_UNITS[u][1] + 1)
                act.wait_ge(fpt_ready, u + 1)
                if u >= 2:
                    act.wait_ge(fo_ready, u - 1)
                act.activation(FPT[:, u % 2, 0:nk], PS[:, 2 + u % 2, 0:nk], ACT.Copy).then_inc(fpt_taken, 1)

            def out_hi(j):
                act.wait_ge(fo_ready, 4 * j + 4)
                act.activation(MH[:, j, :], PS[:, 6 + j % 2, 0:SEQ], ACT.Copy).then_inc(foh_ready, 1)

            exps(0)
            for u in range(32):
                if u:
                    take_pt(u - 1)
                if u + 1 < 32:
                    exps(u + 1)
                if u % 4 == 1 and u > 4:
                    out_hi(u // 4 - 1)
            take_pt(31)
            out_hi(7)
            for i in range(4):
                turn_hi(act, n0 + 12 + i)
            post_squares(act, s, n0 + 16)
            post_std(act, s)

        def fox_dve(dve, order, s, n0, op, col, post_col):
            pre_rstd(dve, s)
            mixer_norm_dve(dve, s, 2, col, op)
            order.after(dve.memset(F_ONES, 1.0))
            dve.wait_ge(forget_ready, 1)
            order.after(dve.tensor_scalar(F_Z, PS[0:16, 7, 0:SEQ], SMALLW[0:16, SMALL["b_f"][0]:SMALL["b_f"][0] + 1], None, ALU.add))
            dve.scalar_tensor_tensor(F_L, F_Z, -1.0, F_Z, ALU.mult, ALU.max).then_inc(forget_abs, 1)
            dve.wait_ge(forget_ln, 1)
            order.after(dve.scalar_tensor_tensor(F_Z, F_Z, 0.0, F_L, ALU.min, ALU.subtract))
            order.after(dve.tensor_tensor_scan(F_NEGC, F_ONES, F_Z, 0.0, ALU.mult, ALU.add))
            dve.tensor_scalar(F_NEGC, F_NEGC, -1.0, None, ALU.mult).then_inc(forget_done, 1)
            for i in range(12):
                turn_lo(dve, n0 + i)

            def mask(u):
                nk = P * (F_UNITS[u][1] + 1)
                dve.wait_ge(fs_ready, u + 1)
                if u >= 2:
                    dve.wait_ge(fe_ready, u - 1)
                dve.tensor_tensor_reduce(out=FS[:, u % 2, 0:nk], in0=PS[:, u % 2, 0:nk], in1=CAUSAL[:, 2 * P - nk:2 * P],
                                         scale=1.0, scalar=-3e38, op0=ALU.add, op1=ALU.max,
                                         accum_out=FST[:, u % 2, 0:1]).then_inc(fs_taken, 1)
                dve.wait_ge(fs_taken, u + 1)
                dve.tensor_scalar(FST[:, u % 2, 1:2], FST[:, u % 2, 0:1], -1.0, None, ALU.mult).then_inc(fm_ready, 1)

            def normalize(u):
                nk = P * (F_UNITS[u][1] + 1)
                dve.wait_ge(fe_ready, u + 1)
                order.after(dve.reciprocal(FST[:, u % 2, 3:4], FST[:, u % 2, 2:3]))
                dve.tensor_scalar(FP[:, u % 2, 0:nk], FP[:, u % 2, 0:nk], FST[:, u % 2, 3:4], None, ALU.mult).then_inc(fp_ready, 1)

            def out_lo(j):
                dve.wait_ge(foh_ready, j + 1)
                dve.tensor_tensor(ML[:, j, :], PS[:, 6 + j % 2, 0:SEQ], MH[:, j, :].bitcast(F32), ALU.subtract).then_inc(fol_ready, 1)

            mask(0)
            mask(1)
            for u in range(32):
                normalize(u)
                if u + 2 < 32:
                    mask(u + 2)
                if u % 4 == 1 and u > 4:
                    out_lo(u // 4 - 1)
            out_lo(7)
            for i in range(4):
                turn_lo(dve, n0 + 12 + i)
            post_add(dve, order, s, post_col)

        def fox_pe(pe, s, n0, op):
            pre_mean(pe, s, mixer=True)
            f_cols = SMALLW[:, SMALL["f"][0]:SMALL["f"][0] + KT * 16].rearrange("p (k n) -> p k n", k=KT)
            for k in range(KT):
                pe.wait_ge(hn_ready, KT * 2 + k + 1)
                last = pe.matmul(PS[0:16, 7, 0:SEQ], f_cols[:, k, :], HN[:, k, :], start=k == 0, stop=k == KT - 1)
            last.then_inc(forget_ready, 1)
            opening_products(pe, n0, op)
            for i in range(2, 12):
                if i >= 2:
                    pe.wait_ge(fox_taken, i - 1)
                if i < 8:
                    column_products(pe, n0 + i, BANK[i % 2])
                else:
                    pe.wait_ge(lo_ready, n0 + i + 1)
                    out = [BANK[i % 2][:, SEQ * t:SEQ * (t + 1)] for t in range(TT)]
                    token_products(pe, n0 + i, out, (0, COLS)).then_inc(products_done, 1)
            pe.wait_ge(fox_taken, 12)
            pe.wait_ge(forget_done, 1)
            pe.wait_ge(x_ready, KT * (s + 1))

            def scores(u):
                j, qt, hh = F_UNITS[u]
                nk, a, h = P * (qt + 1), HD * hh, 2 * j + hh
                if u >= 2:
                    pe.wait_ge(fs_taken, u - 1)
                out = PS[:, u % 2, 0:nk]
                pe.matmul(out, FQ[a:a + HD, j, qt * P:(qt + 1) * P], FK[a:a + HD, j, 0:nk], start=True, stop=False)
                pe.matmul(out, IDENT[0:16, h:h + 1].to_broadcast([16, P]), F_NEGC[:, 0:nk], start=False, stop=True).then_inc(fs_ready, 1)

            def transposes(u):
                qt = F_UNITS[u][1]
                pe.wait_ge(fp_ready, u + 1)
                if u >= 2:
                    pe.wait_ge(fpt_taken, u - 1)
                for b in range(qt + 1):
                    last = pe.transpose(PS[:, 2 + u % 2, b * P:(b + 1) * P], FP[:, u % 2, b * P:(b + 1) * P], IDENT[:])
                last.then_inc(fpt_ready, 1)

            def values(u):
                j, qt, hh = F_UNITS[u]
                h = 2 * j + hh
                pe.wait_ge(fpt_taken, u + 1)
                if u % 4 == 0 and j >= 2:
                    pe.wait_ge(fol_ready, j - 1)
                out = PS[HD * hh:HD * hh + HD, 6 + j % 2, qt * P:(qt + 1) * P]
                for b in range(qt + 1):
                    last = pe.matmul(out, FV[:, b, HD * h:HD * h + HD], FPT[:, u % 2, P * b:P * (b + 1)], start=b == 0, stop=b == qt)
                last.then_inc(fo_ready, 1)

            scores(0)
            scores(1)
            for u in range(32):
                if u + 2 < 32:
                    scores(u + 2)
                transposes(u)
                if u:
                    values(u - 1)
            values(31)
            pe.wait_ge(fs_taken, 32)
            pe.wait_ge(fpt_taken, 32)
            open_outputs(pe, s)
            for i in range(4):
                pe.wait_ge(fol_ready, 2 * i + 2)
                row_products(pe, n0 + 12 + i, MH[:, 2 * i:2 * i + 2, :], ML[:, 2 * i:2 * i + 2, :], end=s if i == 3 else None)

        LEVELS = [0] + [1 << i for i in range(8)]
        GH = D // P
        WB = [SCR[:, 2048 * i:2048 * (i + 1)] for i in range(2)]
        GQ, GK, GB, GV = (SCR[:, 4096 + 2048 * i:6144 + 2048 * i] for i in range(4))
        FREE = SMALL["dec1"][0]
        GA = SMALLW[:, FREE:FREE + 2048]
        GX = SMALLW[:, FREE + 2048:FREE + 3072]
        GR = SMALLW[:, FREE + 4224:FREE + 4240]
        LB = SMALLW[:, FREE + 4240:FREE + 4304].rearrange("p (a k) -> p a k", a=8)
        G_SILU = SQ[:].rearrange("p k t -> p (k t)")
        gh = lambda ap: ap.rearrange("p (h t) -> p h t", h=GH)
        hgrn_taken = sem("hgrn_bank_taken")
        lb_sub, lb_exp, keys_ready, ln_ready = (sem("hgrn_" + x) for x in ("bound_sub", "bound_exp", "keys", "ln"))
        we_ready, wx_ready, w_ready, ws_ready, ws_taken = (sem("hgrn_" + x) for x in ("exponents", "exp", "w", "level", "level_taken"))
        gx_taken, go_ready, gsq_ready, gms_ready, gstd_ready = (sem("hgrn_" + x) for x in ("cross_taken", "out", "squares", "mean", "std"))
        grs_ready, grb_ready, grb_taken, gn_ready, gnh_ready, gnl_ready = (
            sem("hgrn_" + x) for x in ("rstd", "rstd_wide", "rstd_taken", "normed", "normed_hi", "normed_lo"))

        def hgrn_act(act, order, s, n0, op, col):
            pre_squares(act, s)
            pre_std(act, s)
            mixer_operand_act(act, 3, op)
            act.wait_ge(lb_sub, 1)
            act.activation(LB[:, 0:3, :], LB[:, 0:3, :], ACT.Exp).then_inc(lb_exp, 1)

            def take(i):
                act.wait_ge(products_done, n0 + i + 1)
                bank, c = BANK[i % 2], 512 * (i % 4)
                if i < 4:
                    last = act.activation(GK[:, c:c + 512], bank, ACT.Sigmoid)
                elif i < 8:
                    last = act.activation(GQ[:, c:c + 512], bank, ACT.Copy)
                elif i < 12:
                    last = act.activation(GV.rearrange("p (t c) -> p t c", t=2)[:, :, 256 * (i - 8):256 * (i - 7)], two(bank), ACT.Copy)
                else:
                    last = act.activation(G_SILU[:, c:c + 512], bank, ACT.Silu)
                last.then_inc(hgrn_taken, 1)

            for i in range(8):
                turn_hi(act, n0 + i)
                take(i)
                if i == 4:
                    act.wait_ge(keys_ready, 4)
                    act.activation(WB[1], GB, ACT.Ln).then_inc(ln_ready, 1)

            def exps(l):
                act.wait_ge(we_ready, l)
                if l < 8:
                    act.activation(WB[l % 2], WB[l % 2], ACT.Exp).then_inc(wx_ready, 1)
                else:
                    w = gh(WB[0])
                    act.activation(w[:, :, 0:P], w[:, :, 0:P], ACT.Exp)
                    act.activation(w[:, :, P:2 * P], gh(GB)[:, :, P:2 * P], ACT.Exp).then_inc(wx_ready, 1)

            exps(1)
            for l in range(8):
                turn_hi(act, n0 + 8 + l)
                if l < 7:
                    exps(l + 2)
                take(8 + l)
            act.wait_ge(ws_ready, 9)
            act.activation(GX, PS[:, 0:2, :].rearrange("p b t -> p (b t)"), ACT.Copy).then_inc(gx_taken, 1)
            for b in range(4):
                act.wait_ge(go_ready, b + 1)
                act.activation(WB[0][:, 512 * b:512 * (b + 1)], PS[:, 4 + b, :], ACT.Square).then_inc(gsq_ready, 1)
            act.wait_ge(gms_ready, 1)
            act.activation(GR, PS[:, 0, 0:16], ACT.Sqrt, bias=EPSILON[:, 0:1], scale=float(D // P)).then_inc(gstd_ready, 1)
            for b in range(4):
                act.wait_ge(grb_ready, b + 1)
                act.activation(WB[1][:, 512 * b:512 * (b + 1)], PS[:, b, :], ACT.Copy).then_inc(grb_taken, 1)
            for b in range(4):
                act.wait_ge(gn_ready, b + 1)
                act.activation(MH[:, 2 * b:2 * b + 2, :], two(WB[0][:, 512 * b:512 * (b + 1)]), ACT.Copy).then_inc(gnh_ready, 1)
            for i in range(4):
                turn_hi(act, n0 + 16 + i)
            post_squares(act, s, n0 + 20)
            post_std(act, s)

        def hgrn_dve(dve, order, s, n0, op, col, post_col):
            pre_rstd(dve, s)
            mixer_norm_dve(dve, s, 3, col, op)
            dve.wait_ge(x_ready, KT * (s + 1))
            c = COL["lb0"]
            order.after(dve.tensor_tensor(LB[:, 3, :], VEC[:, c:c + KT], VEC[:, c + KT:c + 2 * KT], ALU.max))
            order.after(dve.tensor_tensor(LB[:, 3, :], LB[:, 3, :], VEC[:, c + 2 * KT:c + 3 * KT], ALU.max))
            for i in range(3):
                last = dve.tensor_tensor(LB[:, i, :], VEC[:, c + i * KT:c + (i + 1) * KT], LB[:, 3, :], ALU.subtract)
            last.then_inc(lb_sub, 1)
            dve.wait_ge(lb_exp, 1)
            order.after(dve.tensor_tensor(LB[:, 4, :], LB[:, 0, :], LB[:, 1, :], ALU.add))
            order.after(dve.tensor_tensor(LB[:, 5, :], LB[:, 4, :], LB[:, 2, :], ALU.add))
            order.after(dve.reciprocal(LB[:, 5, :], LB[:, 5, :]))
            order.after(dve.tensor_tensor(LB[:, 6, :], LB[:, 4, :], LB[:, 5, :], ALU.mult))
            order.after(dve.tensor_scalar(LB[:, 7, :], LB[:, 6, :], -1.0, 1.0, ALU.mult, ALU.add))
            for i in range(4):
                turn_lo(dve, n0 + i)
                dve.wait_ge(hgrn_taken, i + 1)
                for h in (2 * i, 2 * i + 1):
                    a = slice(SEQ * h, SEQ * (h + 1))
                    order.after(dve.tensor_scalar(GB[:, a], GK[:, a], LB[:, 7, h:h + 1], LB[:, 6, h:h + 1], ALU.mult, ALU.add))
                    last = dve.tensor_scalar(GK[:, a], GB[:, a], -1.0, 1.0, ALU.mult, ALU.add)
                last.then_inc(keys_ready, 1)
            turn_lo(dve, n0 + 4)
            dve.wait_ge(ln_ready, 1)
            dve.wait_ge(masks_made, MASKS_MADE)
            for h in range(GH):
                a = slice(SEQ * h, SEQ * (h + 1))
                last = dve.tensor_tensor_scan(GB[:, a], CARRY[:], WB[1][:, a], 0.0, ALU.mult, ALU.add)
            order.after(last)

            def exponents(l):
                m = LEVELS[l]
                if l >= 3:
                    dve.wait_ge(ws_ready, l - 1)
                w = WB[l % 2].rearrange("p (b h x) -> p b h x", h=2, x=m)
                b = GB.rearrange("p (b h x) -> p b h x", h=2, x=m)
                edge = b[:, :, 0, m - 1:m].to_broadcast([P, SEQ * GH // (2 * m), m])
                if l < 8:
                    dve.tensor_tensor(w[:, :, 1, :], b[:, :, 1, :], edge, ALU.subtract)
                dve.tensor_tensor(w[:, :, 0, :], edge, b[:, :, 0, :], ALU.subtract).then_inc(we_ready, 1)

            def factors(l):
                m = LEVELS[l]
                dve.wait_ge(wx_ready, l)
                w, q, k = (x.rearrange("p (b h x) -> p b h x", h=2, x=m) for x in (WB[l % 2], GQ, GK))
                dve.tensor_tensor(w[:, :, 1, :], w[:, :, 1, :], q[:, :, 1, :], ALU.mult)
                dve.tensor_tensor(w[:, :, 0, :], w[:, :, 0, :], k[:, :, 0, :], ALU.mult).then_inc(w_ready, 1)

            def pick(l):
                dve.wait_ge(ws_ready, l + 1)
                for b in range(4):
                    a = GA[:, 512 * b:512 * (b + 1)].rearrange("p (u t) -> p u t", u=4)
                    p = PS[:, b, :].rearrange("p (u t) -> p u t", u=4)
                    if l == 0:
                        last = dve.tensor_tensor(a, p, IDENT[:, None, :].to_broadcast([P, 4, P]), ALU.mult)
                    else:
                        mask = LMASK[:, l - 1, 1:2, :].bitcast(mybir.dt.uint16).to_broadcast([P, 4, P])
                        last = dve.copy_predicated(a, mask, p)
                last.then_inc(ws_taken, 1)
                dve.wait_ge(ws_taken, l + 1)

            exponents(1)
            for i in range(5, 8):
                turn_lo(dve, n0 + i)
            dve.wait_ge(hgrn_taken, 8)
            factors(1)
            exponents(2)
            for l in range(8):
                pick(l)
                if 1 <= l < 7:
                    exponents(l + 2)
                turn_lo(dve, n0 + 8 + l)
                if l < 7:
                    factors(l + 2)
            dve.wait_ge(gx_taken, 1)
            dve.wait_ge(gstd_ready, 1)
            dve.reciprocal(GR, GR).then_inc(grs_ready, 1)
            for b in range(4):
                dve.wait_ge(grb_taken, b + 1)
                a = slice(512 * b, 512 * (b + 1))
                order.after(dve.scalar_tensor_tensor(WB[0][:, a], PS[:, 4 + b, :], VEC[:, GNORM_COL:GNORM_COL + 1], WB[1][:, a],
                                                     ALU.mult, ALU.mult))
                dve.tensor_tensor(WB[0][:, a], WB[0][:, a], G_SILU[:, a], ALU.mult).then_inc(gn_ready, 1)
                dve.wait_ge(gnh_ready, b + 1)
                dve.tensor_tensor(ML[:, 2 * b:2 * b + 2, :], two(WB[0][:, a]), MH[:, 2 * b:2 * b + 2, :].bitcast(F32),
                                  ALU.subtract).then_inc(gnl_ready, 1)
            for i in range(4):
                turn_lo(dve, n0 + 16 + i)
            post_add(dve, order, s, post_col)

        def hgrn_pe(pe, s, n0, op):
            pre_mean(pe, s, mixer=True)

            def project(i):
                if i >= 2:
                    pe.wait_ge(hgrn_taken, i - 1)
                if i < 8 or i >= 12:
                    column_products(pe, n0 + i, BANK[i % 2])
                else:
                    pe.wait_ge(lo_ready, n0 + i + 1)
                    out = [BANK[i % 2][:, SEQ * t:SEQ * (t + 1)] for t in range(TT)]
                    token_products(pe, n0 + i, out, (0, COLS)).then_inc(products_done, 1)

            def level(l):
                if l:
                    pe.wait_ge(w_ready, l)
                    pe.wait_ge(ws_taken, l)
                keys, queries = (gh(GK), gh(GQ)) if l == 0 else (gh(WB[l % 2]),) * 2
                if l == 8:
                    for h in range(GH):
                        last = pe.matmul(PS[:, h // 4, P * (h % 4):P * (h % 4 + 1)], keys[:, h, 0:P], queries[:, h, P:2 * P],
                                         start=True, stop=True)
                else:
                    for u in range(2 * GH):
                        h, t = u // 2, slice(P * (u % 2), P * (u % 2 + 1))
                        last = pe.matmul(PS[:, u // 4, P * (u % 4):P * (u % 4 + 1)], keys[:, h, t], queries[:, h, t],
                                         start=True, stop=True)
                last.then_inc(ws_ready, 1)

            opening_products(pe, n0, op)
            for i in range(2, 8):
                project(i)
            pe.wait_ge(hgrn_taken, 8)
            pe.wait_ge(keys_ready, 4)
            pe.wait_ge(x_ready, KT * (s + 1))
            level(0)
            for l in range(1, 9):
                project(7 + l)
                level(l)
            pe.wait_ge(hgrn_taken, 16)
            pe.wait_ge(gx_taken, 1)
            v = GV.rearrange("p (t h c) -> p t h c", t=2, h=GH)
            for h in range(GH):
                out = PS[:, 4 + h // 2, SEQ * (h % 2):SEQ * (h % 2 + 1)]
                pe.matmul(out[:, 0:P], v[:, 0, h, :], GA[:, SEQ * h:SEQ * h + P], start=True, stop=True)
                pe.matmul(out[:, P:2 * P], v[:, 1, h, :], GA[:, SEQ * h + P:SEQ * (h + 1)], start=True, stop=False)
                last = pe.matmul(out[:, P:2 * P], v[:, 0, h, :], GX[:, P * h:P * (h + 1)], start=False, stop=True)
                if h % 2:
                    last.then_inc(go_ready, 1)
            sq = gh(WB[0])
            for u in range(2 * GH):
                h, t = u // 2, slice(P * (u % 2), P * (u % 2 + 1))
                if u % 4 == 0:
                    pe.wait_ge(gsq_ready, u // 4 + 1)
                last = pe.matmul(PS[:, 0, u:u + 1], sq[:, h, t], MEAN[:, 0:1], start=True, stop=True)
            last.then_inc(gms_ready, 1)
            pe.wait_ge(grs_ready, 1)
            for u in range(2 * GH):
                last = pe.matmul(PS[:, u // 4, P * (u % 4):P * (u % 4 + 1)], GR[:, u:u + 1].to_broadcast([P, P]), IDENT[:],
                                 start=True, stop=True)
                if u % 4 == 3:
                    last.then_inc(grb_ready, 1)
            pe.wait_ge(grb_taken, 4)
            open_outputs(pe, s)
            for i in range(4):
                pe.wait_ge(gnl_ready, i + 1)
                row_products(pe, n0 + 16 + i, MH[:, 2 * i:2 * i + 2, :], ML[:, 2 * i:2 * i + 2, :], end=s if i == 3 else None)

        plan, n, op = [], 0, 0
        for s, (kind, slabs, operands) in enumerate(SUBLAYERS):
            plan.append((kind, s, n, op))
            n, op = n + slabs, op + operands
        ffns = ["l0_ffn1", "l0_ffn2", "l1_ffn1", "l1_ffn2", "gain02", "gain12"]
        ffn_cols = [(COL[f + "_pre_g"], COL[f + "_post_g"]) if "ffn" in f else (COL[f], COL[f] + KT) for f in ffns]
        f_of = {s: f for f, s in enumerate([0, 2, 3, 5, 7, 9])}

        ffn_operand = {s: (op, ffn_cols[f_of[s]][0]) for kind, s, n, op in plan if kind == "ffn"}
        sublayer_of = {op: s for kind, s, n, op in plan}

        x_dram, y_dram = (d.rearrange("(k p) t -> p k t", p=P) for d in (xT_dram, yT_dram))

        block = ctx.enter_context(nc.Block())

        @block.sync
        def _(sp):
            sp.dma_start(X[:, 0:4, :], x_dram[:, 0:4, :]).then_inc(consts_loaded, 16)
            for n in range(RING):
                sp.dma_start(RAW[:, n, :], slabs_dram[n, :, :]).then_inc(raw_loaded[n], 16)
            with sp.Fori(0, n_slabs // RING - 1) as i:
                for u in range(RING):
                    sp.wait_ge(lo_ready, i * RING + u + 1)
                    sp.dma_start(RAW[:, u, :], slabs_dram[bass.ds(i * RING + RING + u, 1), :, :]
                                 .rearrange("n p c -> p (n c)")).then_inc(raw_loaded[u], 16)
            for n in range(n_slabs - n_slabs % RING, n_slabs):
                sp.wait_ge(lo_ready, n - RING + 1)
                sp.dma_start(RAW[:, n % RING, :], slabs_dram[n, :, :]).then_inc(raw_loaded[n % RING], 16)
            for k in range(0, KT, 2):
                sp.wait_ge(x_ready, KT * len(plan) + k + 2)
                sp.dma_start(y_dram[:, k:k + 2, :], X[:, k:k + 2, :]).then_inc(stored, 16)
            sp.wait_ge(stored, 16 * KT // 2)

        @block.gpsimd
        def _(pool):
            pool.memset(MEAN[:], 1.0 / D)
            pool.memset(ZERO[:], 0.0)
            pool.memset(IDENT[:], 0.0).then_inc(pool_order, 1)
            pool.wait_ge(pool_order, 1)
            pool.affine_select(out=IDENT[:], in_=IDENT[:], compare_op=ALU.not_equal, fill=1.0, base=0,
                               pattern=[[-1, P]], channel_multiplier=1).then_inc(consts_made, 1)
            pool.memset(LMASK[:], 1.0)
            pool.memset(CARRY[:], 1.0).then_inc(masks_made, 1)
            pool.wait_ge(masks_made, 1)
            pool.memset(CARRY[:, 0:129:128], 0.0)
            for step in range(3):
                for l in range(7):
                    for side in range(2):
                        m, row, last = 1 << l, m_off(l, side), P // (2 << l)
                        view = LMASK[:, l, side, :].rearrange("p (b h x) -> p b h x", h=2, x=m)
                        base, pattern, mult = [
                            (-row, [[-2 * m, last], [0, 2], [0, m]], 1),
                            (row + m - 1, [[2 * m, last], [0, 2], [0, m]], -1),
                            ((0, -1)[side], [[0, last], [(-1, 1)[side], 2], [0, m]], 0)][step]
                        pool.affine_select(out=view, in_=view, compare_op=ALU.is_ge, fill=0.0, base=base, pattern=pattern,
                                           channel_multiplier=mult).then_inc(masks_made, 1)
                pool.wait_ge(masks_made, 1 + 14 * (step + 1))
            nsa_pool(pool)
            fox_pool(pool)
            rwkv_pool(pool)

        @block.scalar
        def _(act):
            act.dma_start(X[:, 4:8, :], x_dram[:, 4:8, :]).then_inc(consts_loaded, 16)
            act.dma_start(VEC[:], vec_dram).then_inc(consts_loaded, 16)
            split_hi(act, 0)
            act.dma_start(SMALLW[:], small_dram).then_inc(small_loaded, 16)
            order = Order(act, act_order)
            for kind, s, n, op in plan:
                if kind == "ffn":
                    f = f_of[s]
                    ffn_act(act, s, f, n, op, ffn_cols[f][0])
                if kind == "nsa":
                    nsa_act(act, order, s, n, op, COL["l0_mix_pre_g"])
                if kind == "rwkv":
                    rwkv_act(act, order, s, n, op, COL["l1_mix_pre_g"])
                if kind == "fox":
                    fox_act(act, order, s, n, op, COL["gain00"])
                if kind == "hgrn":
                    hgrn_act(act, order, s, n, op, COL["gain10"])

        @block.vector
        def _(dve):
            order = Order(dve, dve_order)
            dve.memset(EPSILON[:, 0:1], EPS)
            dve.memset(EPSILON[:, 1:2], LNX_EPS)
            order.after(dve.memset(HSEL[:], 0.0))
            dve.memset(HSEL[0:64, 0:1], 1.0)
            dve.memset(HSEL[64:P, 1:2], 1.0)
            dve.wait_ge(consts_loaded, 48)
            dve.memset(RSTD[:, 0:1], 0.0).then_inc(x_ready, KT)
            split_lo(dve, 0)
            for kind, s, n, op in plan:
                if kind == "ffn":
                    f = f_of[s]
                    ffn_dve(dve, order, s, f, n, op, *ffn_cols[f])
                if kind == "nsa":
                    nsa_dve(dve, order, s, n, op, COL["l0_mix_pre_g"], COL["l0_mix_post_g"])
                if kind == "rwkv":
                    rwkv_dve(dve, order, s, n, op, COL["l1_mix_pre_g"], COL["l1_mix_post_g"])
                if kind == "fox":
                    fox_dve(dve, order, s, n, op, COL["gain00"], COL["gain01"])
                if kind == "hgrn":
                    hgrn_dve(dve, order, s, n, op, COL["gain10"], COL["gain11"])

        @block.tensor
        def _(pe):
            pe.wait_ge(consts_made, 1)
            for kind, s, n, op in plan:
                if kind == "ffn":
                    ffn_pe(pe, s, f_of[s], n, op)
                if kind == "nsa":
                    nsa_pe(pe, s, n, op)
                if kind == "rwkv":
                    rwkv_pe(pe, s, n, op)
                if kind == "fox":
                    fox_pe(pe, s, n, op)
                if kind == "hgrn":
                    hgrn_pe(pe, s, n, op)


def kernel(**inputs):
    import numpy as np
    import concourse.bacc as bacc
    from concourse.bass_utils import run_bass_kernel_spmd

    a = {name: np.asarray(value) for name, value in inputs.items()}
    slabs = []

    def columns(w):
        for c in range(0, w.shape[1], COLS):
            slabs.append(w[:, c:c + COLS].reshape(KT, P, COLS).transpose(1, 0, 2).reshape(P, SLAB))

    def row_blocks(w):
        for r in range(0, w.shape[0], 2 * P):
            slabs.append(w[r:r + 2 * P].reshape(2, P, D).transpose(1, 0, 2).reshape(P, SLAB))

    def ffn(gate, up, down):
        for j in range(STEPS + 1):
            if j < STEPS:
                columns(gate[:, COLS * j:COLS * (j + 1)])
                columns(up[:, COLS * j:COLS * (j + 1)])
            if j:
                row_blocks(down[COLS * (j - 1):COLS * j])

    def named_ffn(name):
        ffn(a[name + "_w_gate"], a[name + "_w_up"], a[name + "_w_down"])

    named_ffn("l0_ffn1")
    w = a["l0_w_in"]
    columns(w[:, 0:512])
    columns(w[:, 536:792])
    columns(w[:, 792:1048])
    columns(w[:, 1048:1304])
    for kv in "kv":
        slabs.append(a["l0_cmp_w1_" + kv].reshape(16, P, P).transpose(1, 0, 2).reshape(P, SLAB))
    for c in range(0, 512, COLS):
        for part in (1816, 2328, 1304):
            columns(w[:, part + c:part + c + COLS])
    row_blocks(a["l0_w_out"])
    named_ffn("l0_ffn2")
    named_ffn("l1_ffn1")
    for name in "rkv":
        columns(a["l1_w_" + name])
    row_blocks(a["l1_w_o"])
    named_ffn("l1_ffn2")
    w = a["fox_w_in_2"][0]
    columns(w[:, 0:3 * D])
    row_blocks(a["fox_w_out_2"][0])
    w_in, w_out = a["ffn_w_in_2"], a["ffn_w_out_2"]
    ffn(w_in[0][:, :D_FF], w_in[0][:, D_FF:], w_out[0])
    w = a["hgrn_w_in_2"][0]
    columns(w[:, D:2 * D])
    columns(w[:, 0:D])
    columns(w[:, 2 * D:4 * D])
    row_blocks(a["hgrn_w_out_2"][0])
    ffn(w_in[1][:, :D_FF], w_in[1][:, D_FF:], w_out[1])
    n_slabs = sum(x[1] for x in SUBLAYERS)
    slabs = np.stack(slabs[:n_slabs])

    def vector(name):
        if name.startswith("gain"):
            return a["norm_gains_2"][int(name[4]), int(name[5])]
        if name.startswith("mu"):
            return a["l1_mu"][int(name[2])]
        if name.startswith("lb"):
            return a["hgrn_lb_table_2"][int(name[2])]
        return a[name]

    cols = [vector(name).reshape(KT, P).T for name in COL]
    cols.append(a["l0_conv_w"].reshape(12, P).T)
    cols.append(a["l0_conv_b"].reshape(4, P).T)
    for kv in "kv":
        cols.append(np.repeat(a["l0_cmp_pe_" + kv].reshape(16, P).T, 2, axis=1))
    cols.append(a["hgrn_gnorm_2"].reshape(P, 1))
    vec = np.ascontiguousarray(np.concatenate(cols, axis=1))

    small = np.zeros((P, SMALL_COLS), np.float32)

    def put(name, w):
        c, n = SMALL[name]
        small[:w.shape[0], c:c + n] = w

    def tiled(w):
        return w.reshape(KT, P, -1).transpose(1, 0, 2).reshape(P, -1)

    put("g", tiled(a["l0_w_in"][:, 512:536]))
    put("f", tiled(a["fox_w_in_2"][0][:, 3 * D:]))
    put("w2_k", a["l0_cmp_w2_k"])
    put("w2_v", a["l0_cmp_w2_v"])
    put("dec1", tiled(a["l1_w_dec1"]))
    put("a1", tiled(a["l1_w_a1"]))
    put("g1", tiled(a["l1_w_g1"]))
    put("dec2", a["l1_w_dec2"])
    put("a2", a["l1_w_a2"])
    put("g2", a["l1_w_g2"])
    put("b_f", a["fox_b_f_2"].reshape(16, 1))

    nc = bacc.Bacc("TRN2", target_bir_lowering=False, num_devices=1)
    arrays = {"xT": np.ascontiguousarray(a["x"][0].T), "slabs": slabs, "vectors": vec, "small": small}
    args = [nc.dram_tensor("in_" + name, v.shape, F32, kind="ExternalInput").ap() for name, v in arrays.items()]
    args.append(nc.dram_tensor("out_yT", (D, SEQ), F32, kind="ExternalOutput").ap())
    build(nc, *args, n_slabs)
    result = run_bass_kernel_spmd(nc, [{"in_" + name: v for name, v in arrays.items()}], core_ids=[0])
    return np.ascontiguousarray(result.results[0]["out_yT"].T)[None]
```
